# Optimizing a Trainium2 kernel written in Bass

```python
import jax
import jax.numpy as jnp
from jax import lax
import numpy as np

D_MODEL = 1024
BATCH = 1
SEQ = 512
DEPTH = 2

D_FF = 2816
LN_EPS = 1e-5
RMS_EPS = 1e-6
DEEPNORM_ALPHA = (2 * DEPTH) ** 0.25
DEEPNORM_BETA = (8 * DEPTH) ** -0.25
HALF_STEP = 0.5
N_EVEN = (DEPTH + 1) // 2
N_ODD = DEPTH // 2
NEG = -1e30
BIG = 1e9
ALIBI_MAX_BIAS = 8.0

MLA_HEADS = 8
MLA_Q_RANK = 384
MLA_KV_RANK = 256
MLA_NOPE = 64
MLA_ROPE = 32
MLA_V = 64
ROPE_THETA = 10000.0
MLA_BLOCK = 128

NSA_HEADS = 8
NSA_KV_GROUPS = 2
NSA_HEADS_PER_GROUP = NSA_HEADS // NSA_KV_GROUPS
NSA_HEAD_DIM = 64
CMP_LEN = 32
CMP_STRIDE = 16
CMP_HIDDEN = 256
SEL_BLOCK = 64
SEL_TOPK = 16
WIN = 512
NSA_CHUNK = SEL_BLOCK

DIL_PATTERNS = ((128, 1), (512, 4), (2048, 16))
DIL_GROUPS = 3
DIL_HEADS_PER_GROUP = 4
DIL_HEAD_DIM = 128
DIL_CHUNK = 128
DIL_MAX_WIN = 2048

NSA_KV_WIDTH = NSA_KV_GROUPS * NSA_HEAD_DIM
EVEN_SPLITS = (MLA_Q_RANK, MLA_KV_RANK, MLA_ROPE, NSA_HEADS * NSA_HEAD_DIM) + (NSA_KV_WIDTH,) * 6 + (3 * NSA_HEADS,)
EVEN_IN = sum(EVEN_SPLITS)
EVEN_OUT = MLA_HEADS * MLA_V + NSA_HEADS * NSA_HEAD_DIM
ODD_IN = 3 * DIL_GROUPS * DIL_HEADS_PER_GROUP * DIL_HEAD_DIM
ODD_OUT = DIL_HEADS_PER_GROUP * DIL_HEAD_DIM

kernel_name = "hybrid_mla_nsa_dilated_macaron_deepnorm"

def layer_norm(x, g, b):
    x32 = x.astype(jnp.float32)
    mu = jnp.mean(x32, axis=-1, keepdims=True)
    var = jnp.mean(jnp.square(x32 - mu), axis=-1, keepdims=True)
    y = (x32 - mu) * lax.rsqrt(var + LN_EPS)
    return (y * g.astype(jnp.float32) + b.astype(jnp.float32)).astype(x.dtype)

def rms_norm(x, g):
    x32 = x.astype(jnp.float32)
    y = x32 * lax.rsqrt(jnp.mean(x32 * x32, axis=-1, keepdims=True) + RMS_EPS)
    return (y * g.astype(jnp.float32)).astype(x.dtype)

def swiglu(x, w_gate, w_up, w_down):
    return (jax.nn.silu(x @ w_gate) * (x @ w_up)) @ w_down

def alibi_slopes(n):
    return 2.0 ** (-ALIBI_MAX_BIAS * jnp.arange(1, n + 1, dtype=jnp.float32) / n)

def masked_softmax(s, mask):
    s = jnp.where(mask, s, NEG)
    m = jnp.max(s, axis=-1, keepdims=True)
    e = jnp.where(mask, jnp.exp(s - m), 0.0)
    den = jnp.sum(e, axis=-1, keepdims=True)
    return e / jnp.maximum(den, 1e-30)

def rope(x, pos):
    half = x.shape[-1] // 2
    inv = ROPE_THETA ** (-jnp.arange(half, dtype=jnp.float32) / half)
    ang = pos.astype(jnp.float32)[..., None] * inv
    ang = ang.reshape(ang.shape[:2] + (1,) * (x.ndim - 3) + (half,))
    cos, sin = jnp.cos(ang), jnp.sin(ang)
    x32 = x.astype(jnp.float32)
    x1, x2 = x32[..., :half], x32[..., half:]
    return jnp.concatenate([x1 * cos - x2 * sin, x2 * cos + x1 * sin], axis=-1).astype(x.dtype)

def mla_attention(c_q, c_kv, k_pe, pos, q_norm_g, kv_norm_g, w_uq, w_uk, w_uv):
    B, S, _ = c_kv.shape
    cq = rms_norm(c_q, q_norm_g)
    ckv = rms_norm(c_kv, kv_norm_g)
    q = (cq @ w_uq).reshape(B, S, MLA_HEADS, MLA_NOPE + MLA_ROPE)
    q_nope = q[..., :MLA_NOPE]
    q_pe = rope(q[..., MLA_NOPE:], pos)
    k_nope = (ckv @ w_uk).reshape(B, S, MLA_HEADS, MLA_NOPE)
    v = (ckv @ w_uv).reshape(B, S, MLA_HEADS, MLA_V)
    k_rot = rope(k_pe, pos)
    scale = (MLA_NOPE + MLA_ROPE) ** -0.5
    key_idx = jnp.arange(S)

    def block(i):
        start = i * MLA_BLOCK
        qn = lax.dynamic_slice_in_dim(q_nope, start, MLA_BLOCK, axis=1)
        qp = lax.dynamic_slice_in_dim(q_pe, start, MLA_BLOCK, axis=1)
        s = (jnp.einsum('bqhd,bkhd->bhqk', qn, k_nope)
             + jnp.einsum('bqhr,bkr->bhqk', qp, k_rot)).astype(jnp.float32) * scale
        q_idx = start + jnp.arange(MLA_BLOCK)
        p = masked_softmax(s, q_idx[:, None] >= key_idx[None, :])
        return jnp.einsum('bhqk,bkhd->bqhd', p.astype(v.dtype), v)

    out = lax.map(block, jnp.arange(S // MLA_BLOCK))
    return out.transpose(1, 0, 2, 3, 4).reshape(B, S, MLA_HEADS * MLA_V)

def nsa_attention(q, k_cmp, v_cmp, k_sel, v_sel, k_win, v_win, gate_logits, pos,
                  cmp_pos, cmp_k_w1, cmp_k_w2, cmp_v_w1, cmp_v_w2):
    B, S, _ = q.shape
    G, HPG, DH = NSA_KV_GROUPS, NSA_HEADS_PER_GROUP, NSA_HEAD_DIM
    NC = S // CMP_STRIDE - 1
    NS = S // SEL_BLOCK
    SEL_K = min(SEL_TOPK, NS)
    scale = DH ** -0.5
    q = q.reshape(B, S, G, HPG, DH)
    slopes = alibi_slopes(NSA_HEADS).reshape(G, HPG)[:, :, None, None]
    pos_f = pos.astype(jnp.float32)

    def compress(kv, w1, w2):
        halves = kv.reshape(B, S // CMP_STRIDE, CMP_STRIDE, G, DH)
        blocks = jnp.concatenate([halves[:, :-1], halves[:, 1:]], axis=2) + cmp_pos[:, None, :]
        flat = blocks.transpose(0, 1, 3, 2, 4).reshape(B, NC, G, CMP_LEN * DH)
        return jax.nn.gelu(flat @ w1) @ w2

    kc = compress(k_cmp, cmp_k_w1, cmp_k_w2)
    vc = compress(v_cmp, cmp_v_w1, cmp_v_w2)
    cend_idx = jnp.arange(NC) * CMP_STRIDE + (CMP_LEN - 1)
    pos_cend = pos_f[:, CMP_LEN - 1::CMP_STRIDE]
    cstart = jnp.arange(NC)[:, None] * CMP_STRIDE
    sstart = jnp.arange(NS)[None, :] * SEL_BLOCK
    overlap = ((cstart < sstart + SEL_BLOCK) & (cstart + CMP_LEN > sstart)).astype(jnp.float32)

    ks = k_sel.reshape(B, NS, SEL_BLOCK, G, DH).transpose(0, 3, 1, 2, 4)
    vs = v_sel.reshape(B, NS, SEL_BLOCK, G, DH).transpose(0, 3, 1, 2, 4)
    pos_sel = pos_f.reshape(B, NS, SEL_BLOCK)
    pad = ((0, 0), (WIN, 0), (0, 0), (0, 0))
    kw = jnp.pad(k_win.reshape(B, S, G, DH), pad)
    vw = jnp.pad(v_win.reshape(B, S, G, DH), pad)
    pos_win = jnp.pad(pos_f, ((0, 0), (WIN, 0)))
    gates = jax.nn.sigmoid(gate_logits.reshape(B, S, 3, G, HPG))
    b_ix = jnp.arange(B)[:, None, None, None]
    g_ix = jnp.arange(G)[None, :, None, None]
    blk = jnp.arange(NS)
    J = SEL_K * SEL_BLOCK
    L = WIN + NSA_CHUNK

    def chunk(c):
        start = c * NSA_CHUNK
        t = start + jnp.arange(NSA_CHUNK)
        qc = lax.dynamic_slice_in_dim(q, start, NSA_CHUNK, axis=1)
        pq = lax.dynamic_slice_in_dim(pos_f, start, NSA_CHUNK, axis=1)
        s = jnp.einsum('bqgnd,bkgd->bgnqk', qc, kc).astype(jnp.float32) * scale
        s = s - slopes * (pq[:, :, None] - pos_cend[:, None, :])[:, None, None]
        p_c = masked_softmax(s, cend_idx[None, :] <= t[:, None])
        o_c = jnp.einsum('bgnqk,bkgd->bqgnd', p_c.astype(vc.dtype), vc)
        imp = jnp.einsum('bgnqk,ks->bgqs', p_c, overlap)
        imp = jnp.where((blk == 0) | (blk == c), BIG, imp)
        imp = jnp.where(blk <= c, imp, NEG)
        _, idx = lax.top_k(imp, SEL_K)
        valid = idx <= c
        kg = ks[b_ix, g_ix, idx].reshape(B, G, NSA_CHUNK, J, DH)
        vg = vs[b_ix, g_ix, idx].reshape(B, G, NSA_CHUNK, J, DH)
        kpos = pos_sel[b_ix, idx].reshape(B, G, NSA_CHUNK, J)
        kidx = idx[..., None] * SEL_BLOCK + jnp.arange(SEL_BLOCK)
        mask_s = (valid[..., None] & (kidx <= t[:, None, None])).reshape(B, G, NSA_CHUNK, J)
        s = jnp.einsum('bqgnd,bgqjd->bgnqj', qc, kg).astype(jnp.float32) * scale
        s = s - slopes * (pq[:, None, :, None] - kpos)[:, :, None]
        p_s = masked_softmax(s, mask_s[:, :, None])
        o_s = jnp.einsum('bgnqj,bgqjd->bqgnd', p_s.astype(vg.dtype), vg)
        kwc = lax.dynamic_slice_in_dim(kw, start, L, axis=1)
        vwc = lax.dynamic_slice_in_dim(vw, start, L, axis=1)
        pwc = lax.dynamic_slice_in_dim(pos_win, start, L, axis=1)
        widx = start - WIN + jnp.arange(L)
        diff = t[:, None] - widx[None, :]
        mask_w = (widx[None, :] >= 0) & (diff >= 0) & (diff < WIN)
        s = jnp.einsum('bqgnd,bkgd->bgnqk', qc, kwc).astype(jnp.float32) * scale
        s = s - slopes * (pq[:, :, None] - pwc[:, None, :])[:, None, None]
        p_w = masked_softmax(s, mask_w)
        o_w = jnp.einsum('bgnqk,bkgd->bqgnd', p_w.astype(vwc.dtype), vwc)
        gc = lax.dynamic_slice_in_dim(gates, start, NSA_CHUNK, axis=1)
        return (gc[:, :, 0, :, :, None] * o_c + gc[:, :, 1, :, :, None] * o_s
                + gc[:, :, 2, :, :, None] * o_w)

    out = lax.map(chunk, jnp.arange(S // NSA_CHUNK))
    return out.transpose(1, 0, 2, 3, 4, 5).reshape(B, S, NSA_HEADS * DH)

def dilated_attention(qkv, pos):
    B, S, _ = qkv.shape
    GH, DH, Q = DIL_HEADS_PER_GROUP, DIL_HEAD_DIM, DIL_CHUNK
    scale = DH ** -0.5
    qkv = qkv.reshape(B, S, 3, DIL_GROUPS, GH, DH)
    pad = ((0, 0), (DIL_MAX_WIN, 0), (0, 0), (0, 0))
    pos_f = pos.astype(jnp.float32)
    pos_pad = jnp.pad(pos_f, ((0, 0), (DIL_MAX_WIN, 0)))
    slopes = alibi_slopes(DIL_GROUPS * GH).reshape(DIL_GROUPS, GH)
    qs = [qkv[:, :, 0, g] for g in range(DIL_GROUPS)]
    ks = [jnp.pad(qkv[:, :, 1, g], pad) for g in range(DIL_GROUPS)]
    vs = [jnp.pad(qkv[:, :, 2, g], pad) for g in range(DIL_GROUPS)]

    def chunk(c):
        start = c * Q
        pq = lax.dynamic_slice_in_dim(pos_f, start, Q, axis=1)
        outs, lses = [], []
        for g, (w, dil) in enumerate(DIL_PATTERNS):
            L = w + Q
            off = start + DIL_MAX_WIN - w
            qg = lax.dynamic_slice_in_dim(qs[g], start, Q, axis=1).reshape(B, Q // dil, dil, GH, DH)
            kg = lax.dynamic_slice_in_dim(ks[g], off, L, axis=1).reshape(B, L // dil, dil, GH, DH)
            vg = lax.dynamic_slice_in_dim(vs[g], off, L, axis=1).reshape(B, L // dil, dil, GH, DH)
            pk = lax.dynamic_slice_in_dim(pos_pad, off, L, axis=1).reshape(B, L // dil, dil)
            dist = (pq.reshape(B, Q // dil, dil).transpose(0, 2, 1)[:, :, :, None]
                    - pk.transpose(0, 2, 1)[:, :, None, :])
            s = jnp.einsum('bjrhd,birhd->bhrji', qg, kg).astype(jnp.float32) * scale
            s = s - slopes[g][:, None, None, None] * dist[:, None]
            jj = jnp.arange(Q // dil)[:, None]
            ii = jnp.arange(L // dil)[None, :]
            kidx = start - w + ii * dil + jnp.arange(dil)[:, None, None]
            mask = (ii >= jj) & (ii <= jj + w // dil) & (kidx >= 0)
            s = jnp.where(mask, s, NEG)
            m = jnp.max(s, axis=-1, keepdims=True)
            e = jnp.exp(s - m)
            den = jnp.sum(e, axis=-1, keepdims=True)
            o = jnp.einsum('bhrji,birhd->bjrhd', (e / den).astype(vg.dtype), vg)
            outs.append(o.reshape(B, Q, GH, DH))
            lses.append((m + jnp.log(den))[..., 0].transpose(0, 3, 2, 1).reshape(B, Q, GH))
        wts = jax.nn.softmax(jnp.stack(lses), axis=0)
        out = jnp.einsum('gbqh,gbqhd->bqhd', wts.astype(outs[0].dtype), jnp.stack(outs))
        return out.reshape(B, Q, GH * DH)

    out = lax.map(chunk, jnp.arange(S // Q))
    return out.transpose(1, 0, 2, 3).reshape(B, S, ODD_OUT)

def even_mixer(x, pos, w_in, q_norm_g, kv_norm_g, w_uq, w_uk, w_uv,
               cmp_pos, cmp_k_w1, cmp_k_w2, cmp_v_w1, cmp_v_w2, w_out):
    h = x @ w_in
    cuts = np.cumsum(EVEN_SPLITS)[:-1].tolist()
    c_q, c_kv, k_pe, q, k_c, v_c, k_s, v_s, k_w, v_w, gate_logits = jnp.split(h, cuts, axis=-1)
    o_mla = mla_attention(c_q, c_kv, k_pe, pos, q_norm_g, kv_norm_g, w_uq, w_uk, w_uv)
    o_nsa = nsa_attention(q, k_c, v_c, k_s, v_s, k_w, v_w, gate_logits, pos,
                          cmp_pos, cmp_k_w1, cmp_k_w2, cmp_v_w1, cmp_v_w2)
    return jnp.concatenate([o_mla, o_nsa], axis=-1) @ w_out

def odd_mixer(x, pos, w_in, w_out):
    return dilated_attention(x @ w_in, pos) @ w_out

def setup_inputs(seed: int = 0) -> dict:
    key = jax.random.key(seed)
    keys = iter(jax.random.split(key, 40))
    f32 = jnp.float32

    def nrm(shape, scale):
        return jax.random.normal(next(keys), shape, f32) * scale

    def gain(shape):
        return 1.0 + nrm(shape, 0.02)

    x = jax.random.normal(next(keys), (BATCH, SEQ, D_MODEL), f32)
    offset = jax.random.randint(next(keys), (BATCH, 1), 0, 4096, dtype=jnp.int32)
    positions = offset + jnp.arange(SEQ, dtype=jnp.int32)[None, :]
    return {
        "x": x,
        "positions": positions,
        "ln1_g": gain((DEPTH, D_MODEL)),
        "ln1_b": nrm((DEPTH, D_MODEL), 0.02),
        "ffn1_w_gate": nrm((DEPTH, D_MODEL, D_FF), D_MODEL ** -0.5),
        "ffn1_w_up": nrm((DEPTH, D_MODEL, D_FF), D_MODEL ** -0.5),
        "ffn1_w_down": nrm((DEPTH, D_FF, D_MODEL), DEEPNORM_BETA * D_FF ** -0.5),
        "mix_in_even": nrm((N_EVEN, D_MODEL, EVEN_IN), D_MODEL ** -0.5),
        "mla_q_norm": gain((N_EVEN, MLA_Q_RANK)),
        "mla_kv_norm": gain((N_EVEN, MLA_KV_RANK)),
        "mla_w_uq": nrm((N_EVEN, MLA_Q_RANK, MLA_HEADS * (MLA_NOPE + MLA_ROPE)), MLA_Q_RANK ** -0.5),
        "mla_w_uk": nrm((N_EVEN, MLA_KV_RANK, MLA_HEADS * MLA_NOPE), MLA_KV_RANK ** -0.5),
        "mla_w_uv": nrm((N_EVEN, MLA_KV_RANK, MLA_HEADS * MLA_V), MLA_KV_RANK ** -0.5),
        "nsa_cmp_pos": nrm((N_EVEN, CMP_LEN, NSA_HEAD_DIM), 0.5),
        "nsa_cmp_k_w1": nrm((N_EVEN, CMP_LEN * NSA_HEAD_DIM, CMP_HIDDEN), (CMP_LEN * NSA_HEAD_DIM) ** -0.5),
        "nsa_cmp_k_w2": nrm((N_EVEN, CMP_HIDDEN, NSA_HEAD_DIM), CMP_HIDDEN ** -0.5),
        "nsa_cmp_v_w1": nrm((N_EVEN, CMP_LEN * NSA_HEAD_DIM, CMP_HIDDEN), (CMP_LEN * NSA_HEAD_DIM) ** -0.5),
        "nsa_cmp_v_w2": nrm((N_EVEN, CMP_HIDDEN, NSA_HEAD_DIM), CMP_HIDDEN ** -0.5),
        "mix_out_even": nrm((N_EVEN, EVEN_OUT, D_MODEL), DEEPNORM_BETA * EVEN_OUT ** -0.5),
        "mix_in_odd": nrm((N_ODD, D_MODEL, ODD_IN), D_MODEL ** -0.5),
        "mix_out_odd": nrm((N_ODD, ODD_OUT, D_MODEL), DEEPNORM_BETA * ODD_OUT ** -0.5),
        "ln2_g": gain((DEPTH, D_MODEL)),
        "ln2_b": nrm((DEPTH, D_MODEL), 0.02),
        "ffn2_w_gate": nrm((DEPTH, D_MODEL, D_FF), D_MODEL ** -0.5),
        "ffn2_w_up": nrm((DEPTH, D_MODEL, D_FF), D_MODEL ** -0.5),
        "ffn2_w_down": nrm((DEPTH, D_FF, D_MODEL), DEEPNORM_BETA * D_FF ** -0.5),
        "ln3_g": gain((DEPTH, D_MODEL)),
        "ln3_b": nrm((DEPTH, D_MODEL), 0.02),
    }

def reference(x, positions, ln1_g, ln1_b, ffn1_w_gate, ffn1_w_up, ffn1_w_down,
              mix_in_even, mla_q_norm, mla_kv_norm, mla_w_uq, mla_w_uk, mla_w_uv,
              nsa_cmp_pos, nsa_cmp_k_w1, nsa_cmp_k_w2, nsa_cmp_v_w1, nsa_cmp_v_w2, mix_out_even,
              mix_in_odd, mix_out_odd, ln2_g, ln2_b,
              ffn2_w_gate, ffn2_w_up, ffn2_w_down, ln3_g, ln3_b):
    for i in range(DEPTH):
        j = i // 2
        x = layer_norm(DEEPNORM_ALPHA * x + HALF_STEP * swiglu(x, ffn1_w_gate[i], ffn1_w_up[i], ffn1_w_down[i]),
                       ln1_g[i], ln1_b[i])
        if i % 2 == 0:
            mix = even_mixer(x, positions, mix_in_even[j], mla_q_norm[j], mla_kv_norm[j],
                             mla_w_uq[j], mla_w_uk[j], mla_w_uv[j], nsa_cmp_pos[j],
                             nsa_cmp_k_w1[j], nsa_cmp_k_w2[j], nsa_cmp_v_w1[j], nsa_cmp_v_w2[j],
                             mix_out_even[j])
        else:
            mix = odd_mixer(x, positions, mix_in_odd[j], mix_out_odd[j])
        x = layer_norm(DEEPNORM_ALPHA * x + mix, ln2_g[i], ln2_b[i])
        x = layer_norm(DEEPNORM_ALPHA * x + HALF_STEP * swiglu(x, ffn2_w_gate[i], ffn2_w_up[i], ffn2_w_down[i]),
                       ln3_g[i], ln3_b[i])
    return x


_drawn_inputs = setup_inputs


def setup_inputs(seed=0):
    import zlib

    import numpy as np

    out = dict(_drawn_inputs(seed))
    spreads = {}
    factors = {'mla_q_norm': 8.0, 'mla_kv_norm': 8.0, 'nsa_cmp_k_w1': 4.433, 'nsa_cmp_k_w2': 4.644}
    for name, (base, spread) in spreads.items():
        noise = np.random.default_rng([zlib.crc32(name.encode()), seed]).standard_normal(out[name].shape)
        drawn = base * np.exp(spread * noise) if base else spread * noise
        out[name] = jnp.asarray(drawn.astype(out[name].dtype))
    for name, factor in factors.items():
        out[name] = (out[name] * factor).astype(out[name].dtype)
    return out
```

```python
from contextlib import ExitStack

import numpy as np

import concourse.bass as bass
from concourse import mybir

F32 = mybir.dt.float32
F32R = mybir.dt.float32r
I32 = mybir.dt.int32
ACT = mybir.ActivationFunctionType
ALU = mybir.AluOpType
AX = mybir.AxisListType

P = 128
D_MODEL, SEQ, DEPTH, D_FF = 1024, 512, 2, 2816
KD = D_MODEL // P
KF = D_FF // P
TT = SEQ // P
ALPHA = (2 * DEPTH) ** 0.25
LN_EPS, RMS_EPS = 1e-5, 1e-6
BIG = 1e30

H = 8
Q_RANK, KV_RANK, NOPE, ROPE = 384, 256, 64, 32
KQ, KV = Q_RANK // P, KV_RANK // P
MLA_SCALE = (NOPE + ROPE) ** -0.5
DH = 64
NSA_SCALE = DH ** -0.5
NC = SEQ // 16 - 1
CMP_K = 16
NB = 2 * NC
DIL = ((128, 1), (512, 4), (2048, 16))
DG, DHEADS = 3, 4
DIL_SCALE = P ** -0.5
NSA_SLOPES = [2.0 ** (-8.0 * (n + 1) / H) for n in range(H)]
DIL_SLOPES = [2.0 ** (-8.0 * (n + 1) / (DG * DHEADS)) for n in range(DG * DHEADS)]

C_INVD, C_RMS_EPS, C_FREQ, C_TURN, C_PHASE = range(5)
MAGIC = 1.5 * 2.0 ** 23
PI2_A = 6.28125
PI2_B = float(np.float32(2 * np.pi - PI2_A) // 2.0 ** -20 * 2.0 ** -20)
PI2_C = float(2 * np.pi - PI2_A - PI2_B)
PI_SAFE = float(np.nextafter(np.float32(np.pi), np.float32(0)))



class Store:
    pass


RAW, SPLIT = 4, 2
UNIT = KD * P
LEAD = SPLIT

EVEN_IN_UNITS, EVEN_CMP_UNITS, UQ_UNITS = 19, 8, 4
EVEN_UNITS = EVEN_IN_UNITS + EVEN_CMP_UNITS + 2 + UQ_UNITS + KD
ODD_IN_UNITS = 3 * DG * DHEADS
ODD_UNITS = ODD_IN_UNITS + KD // 2
DN_BLOCKS = (8, 7, 7)
DN_STARTS = (0, 8, 15)
FFN_W = [KD * P] * (2 * KF) + [b * P for b in DN_BLOCKS] * KD
EVEN_W = ([KD * P] * 18 + [KD * 24] + [KD * P] * EVEN_CMP_UNITS + [KV * 512] * 2
          + [2 * KQ * P] * UQ_UNITS + [KD * P] * KD)
ODD_W = [KD * P] * ODD_UNITS
WIDTH = FFN_W + EVEN_W + FFN_W + FFN_W + ODD_W + FFN_W
U_FFN = [0, len(FFN_W) + EVEN_UNITS, 2 * len(FFN_W) + EVEN_UNITS,
         3 * len(FFN_W) + EVEN_UNITS + ODD_UNITS]
U_EVEN = len(FFN_W)
U_ODD = 3 * len(FFN_W) + EVEN_UNITS
N_UNITS = len(WIDTH)
LN_OF_FFN = (0, 2, 3, 5)
GU_STEPS = KF // 2
DN_STEPS = 2
DN_UNITS = 12


def load_unit(sp, t, u, src, width, d=0):
    sp.wait_ge(t.units_split, d + (u + 1))
    sp.dma_start(t.raw[:, u % RAW, :width], src).then_inc(t.raw_landed[u % RAW], 16)


def split_hi(act, t, u, d=0):
    if u >= N_UNITS:
        return
    act.wait_ge(t.raw_landed[u % RAW], d * (16 // RAW) + 16 * (u // RAW + 1))
    act.wait_ge(t.units_used, d + (u + 1))
    act.activation(t.whi[:, u % SPLIT, :WIDTH[u]], t.raw[:, u % RAW, :WIDTH[u]],
                   ACT.Copy).then_inc(t.units_hi, 1)


def split_lo(dve, t, u, d=0):
    if u >= N_UNITS:
        return
    dve.wait_ge(t.units_hi, d + (u + 1))
    dve.tensor_tensor(t.wlo[:, u % SPLIT, :WIDTH[u]], t.raw[:, u % RAW, :WIDTH[u]],
                      t.whi[:, u % SPLIT, :WIDTH[u]].bitcast(F32), ALU.subtract
                      ).then_inc(t.units_split, 1)


def split_ready(pe, t, u, d=0):
    pe.wait_ge(t.units_split, d + (RAW + u + 1))


def used(eng, t, u, d=0):
    eng.wait_ge(t.units_used, d + (SPLIT + u + 1))


def product3(pe, out, wh, wl, xh, xl, start, stop):
    pe.matmul(out, wl, xh, start=start, stop=False)
    pe.matmul(out, wh, xl, start=False, stop=False)
    return pe.matmul(out, wh, xh, start=False, stop=stop)


def ffn_sync(sp, t, f):
    u0 = U_FFN[f]
    with sp.Fori(0, GU_STEPS) as i:
        for j in range(4):
            w = (t.w_gate, t.w_up)[j % 2][f]
            load_unit(sp, t, u0 + j, w[bass.ds(2 * i + j // 2, 1)].rearrange("a p n -> p (a n)"),
                      UNIT, 4 * i)
    with sp.Fori(0, DN_STEPS) as i:
        for j in range(DN_UNITS):
            m, part = divmod(j, 3)
            row = t.w_down[f][bass.ds(4 * i + m, 1)].rearrange("a p n -> p (a n)")
            at, w = DN_STARTS[part] * P, DN_BLOCKS[part] * P
            load_unit(sp, t, u0 + 2 * KF + j, row[:, at:at + w], w, DN_UNITS * i)


def ffn_tensor(pe, t, f, x_ready):
    u0, ln = U_FFN[f], LN_OF_FFN[f]
    pe.sem_inc(t.h_mul[f], 2)
    pe.sem_inc(t.z_done[ln], 2)
    with pe.Fori(0, GU_STEPS) as i:
        for j in range(4):
            split_ready(pe, t, u0 + j, 4 * i)
            if j % 2 == 0:
                pe.wait_ge(t.h_mul[f], 2 * i + (j // 2 + 1))
            for k in range(KD):
                if j == 0:
                    pe.wait_ge(x_ready, k + 1)
                b = slice(k * P, k * P + P)
                s = (u0 + j) % SPLIT
                last = product3(pe, t.bank[j][:, :], t.whi[:, s, b], t.wlo[:, s, b],
                                t.xh[:, k, :], t.xl[:, k, :], k == 0, k == KD - 1)
            last.then_inc(t.units_used, 1)
    u1 = u0 + 2 * KF
    with pe.Fori(0, DN_STEPS) as i:
        for j in range(DN_UNITS):
            m, part = divmod(j, 3)
            split_ready(pe, t, u1 + j, DN_UNITS * i)
            if part == 0:
                pe.wait_ge(t.z_done[ln], 4 * i + (m + 1))
            for kk in range(DN_BLOCKS[part]):
                k = DN_STARTS[part] + kk
                if m == 0:
                    pe.wait_ge(t.h_ready[f], k + 1)
                b = slice(kk * P, kk * P + P)
                s = (u1 + j) % SPLIT
                last = product3(pe, t.bank[4 + m % 2][:, :], t.whi[:, s, b], t.wlo[:, s, b],
                                t.hh[:, k, :], t.hl[:, k, :], k == 0, k == KF - 1)
            last.then_inc(t.units_used, 1)


def ffn_scalar(act, t, f):
    u0, u1 = U_FFN[f], U_FFN[f] + 2 * KF
    u2 = u1 + 3 * KD

    def silu(j, i):
        if j % 2 == 0:
            used(act, t, u0 + j, 4 * i)
            act.wait_ge(t.h_mul[f], 2 * i + (j // 2 + 1))
            act.activation(t.sg[:, j // 2, :], t.bank[j][:, :], ACT.Silu).then_inc(t.silu_done[f], 1)

    with act.Fori(0, GU_STEPS - 1) as i:
        for j in range(4):
            split_hi(act, t, u0 + j + LEAD, 4 * i)
            silu(j, i)
    for j in range(4):
        split_hi(act, t, u1 - 4 + j + LEAD)
        silu(j, GU_STEPS - 1)
    with act.Fori(0, DN_STEPS - 1) as i:
        for j in range(DN_UNITS):
            split_hi(act, t, u1 + j + LEAD, DN_UNITS * i)
    for j in range(DN_UNITS):
        split_hi(act, t, u2 - DN_UNITS + j + LEAD)


def ffn_vector(dve, t, f):
    u0, u1, ln = U_FFN[f], U_FFN[f] + 2 * KF, LN_OF_FFN[f]
    u2 = u1 + 3 * KD

    def hidden(j, i):
        if j % 2 == 0:
            return
        p = j // 2
        dve.wait_ge(t.silu_done[f], 2 * i + (p + 1))
        used(dve, t, u0 + j, 4 * i)
        dve.tensor_tensor(t.hf[:, p, :], t.sg[:, p, :], t.bank[j][:, :], ALU.mult).then_inc(t.h_mul[f], 1)
        dve.wait_ge(t.h_mul[f], 2 * i + (p + 3))
        dst = bass.ds(2 * i + p, 1)
        dve.tensor_copy(t.hh[:, dst, :], t.hf[:, p:p + 1, :]).then_inc(t.h_hi[f], 1)
        dve.wait_ge(t.h_hi[f], 2 * i + (p + 1))
        dve.tensor_tensor(t.hl[:, dst, :], t.hf[:, p:p + 1, :], t.hh[:, dst, :].bitcast(F32),
                          ALU.subtract).then_inc(t.h_ready[f], 1)

    def residual(j, i):
        m, part = divmod(j, 3)
        if part < 2:
            return
        used(dve, t, u1 + j, DN_UNITS * i)
        dst = bass.ds(4 * i + m, 1)
        dve.scalar_tensor_tensor(t.xt[:, dst, :], t.xt[:, dst, :], 2 * ALPHA,
                                 t.bank[4 + m % 2][:, :].rearrange("p (a n) -> p a n", a=1),
                                 ALU.mult, ALU.add).then_inc(t.z_done[ln], 1)

    with dve.Fori(0, GU_STEPS - 1) as i:
        for j in range(4):
            split_lo(dve, t, u0 + j + LEAD, 4 * i)
            hidden(j, i)
    for j in range(4):
        split_lo(dve, t, u1 - 4 + j + LEAD)
        hidden(j, GU_STEPS - 1)
    with dve.Fori(0, DN_STEPS - 1) as i:
        for j in range(DN_UNITS):
            split_lo(dve, t, u1 + j + LEAD, DN_UNITS * i)
            residual(j, i)
    for j in range(DN_UNITS):
        split_lo(dve, t, u2 - DN_UNITS + j + LEAD)
        residual(j, DN_STEPS - 1)


def sums_gpsimd(g, t, ln):
    if ln:
        g.wait_ge(t.col_sums[ln - 1], 1)
    g.memset(t.zsum[:, :], 0.0).then_inc(t.acc[ln], 1)
    g.memset(t.qsum[:, :], 0.0).then_inc(t.acc[ln], 1)
    with g.Fori(0, KD) as m:
        z = t.xt[:, bass.ds(m, 1), :]
        g.wait_ge(t.z_done[ln], 3 + m)
        g.wait_ge(t.acc[ln], 2 + 3 * m)
        g.tensor_tensor(t.sq3, z, z, ALU.mult).then_inc(t.acc[ln], 1)
        g.tensor_tensor(t.zsum3, t.zsum3, z, ALU.add).then_inc(t.acc[ln], 1)
        g.wait_ge(t.acc[ln], 3 + 3 * m)
        g.tensor_tensor(t.qsum3, t.qsum3, t.sq3, ALU.add).then_inc(t.acc[ln], 1)


def norm_tensor(pe, t, ln):
    pe.wait_ge(t.acc[ln], 2 + 3 * KD)
    for half, src in enumerate((t.zsum, t.qsum)):
        for i in range(TT):
            last = pe.matmul(t.bank[6][:, 4 * half + i:4 * half + i + 1], src[:, i * P:i * P + P],
                             t.cst[:, C_INVD:C_INVD + 1], start=True, stop=True)
    last.then_inc(t.col_sums[ln], 1)
    pe.wait_ge(t.col[ln], 5)
    for b, src in ((7, t.rstd), (6, t.nmr)):
        for i in range(TT):
            last = pe.matmul(t.bank[b][:, i * P:i * P + P], src[:, i:i + 1].to_broadcast([P, P]),
                             t.ident[:, :], start=True, stop=True)
        last.then_inc(t.maps[ln], 1)


def norm_scalar(act, t, ln):
    act.wait_ge(t.col[ln], 3)
    act.activation(t.std[:, :], t.var[:, :], ACT.Sqrt).then_inc(t.std_done[ln], 1)
    if ln < 5:
        for k in range(KD):
            act.wait_ge(t.normed[ln], 3 * (k + 1))
            act.activation(t.xh[:, k, :], t.xt[:, k, :], ACT.Copy).then_inc(t.x_hi[ln], 1)


def norm_vector(dve, t, ln):
    eps = LN_EPS * (1 if ln % 3 == 1 else 4)
    c = t.col[ln]
    dve.wait_ge(t.col_sums[ln], 1)
    dve.tensor_copy(t.stats[:, :], t.bank[6][:, 0:8]).then_inc(c, 1)
    dve.wait_ge(c, 1)
    dve.tensor_tensor(t.mu2[:, :], t.stats[:, 0:4], t.stats[:, 0:4], ALU.mult).then_inc(c, 1)
    dve.wait_ge(c, 2)
    dve.scalar_tensor_tensor(t.var[:, :], t.stats[:, 4:8], eps, t.mu2[:, :], ALU.add,
                             ALU.subtract).then_inc(c, 1)
    dve.wait_ge(t.std_done[ln], 1)
    dve.reciprocal(t.rstd[:, :], t.std[:, :]).then_inc(c, 1)
    dve.wait_ge(c, 4)
    dve.scalar_tensor_tensor(t.nmr[:, :], t.stats[:, 0:4], -1.0, t.rstd[:, :], ALU.mult,
                             ALU.mult).then_inc(c, 1)
    n = t.normed[ln]
    which, layer = ln % 3, ln // 3
    for k in range(KD):
        x = t.xt[:, k, :]
        dve.wait_ge(t.maps[ln], 1)
        dve.tensor_tensor(x, x, t.bank[7][:, :], ALU.mult).then_inc(n, 1)
        dve.wait_ge(t.maps[ln], 2)
        dve.wait_ge(n, 3 * k + 1)
        dve.tensor_tensor(x, x, t.bank[6][:, :], ALU.add).then_inc(n, 1)
        dve.wait_ge(n, 3 * k + 2)
        dve.tensor_scalar(x, x, t.gains[:, 2 * which, layer, k:k + 1],
                          t.gains[:, 2 * which + 1, layer, k:k + 1], ALU.mult, ALU.add).then_inc(n, 1)


def norm_gpsimd(g, t, ln):
    for k in range(KD):
        g.wait_ge(t.x_hi[ln], k + 1)
        g.tensor_tensor(t.xl[:, k, :], t.xt[:, k, :], t.xh[:, k, :].bitcast(F32),
                        ALU.subtract).then_inc(t.x_ready[ln], 1)


def out_proj_tile(pe, t, ln, m, wh, wl, oh, ol, tiles, o_ready):
    pe.wait_ge(t.z_done[ln], m + 1)
    pe.wait_ge(o_ready[0], o_ready[1])
    for k in range(tiles):
        b = slice(k * P, k * P + P)
        last = product3(pe, t.bank[4 + m % 2][:, :], wh[:, b], wl[:, b], oh[:, k, :], ol[:, k, :],
                        k == 0, k == tiles - 1)
    return last


def mixer_residual(dve, t, ln, m):
    dve.scalar_tensor_tensor(t.xt[:, m, :], t.xt[:, m, :], ALPHA, t.bank[4 + m % 2][:, :],
                             ALU.mult, ALU.add).then_inc(t.z_done[ln], 1)


T_BANKS = 2
PT_SLOTS = 4


def plan_items(raw_items):
    fill = chunk = 0
    items = []
    for n, it in enumerate(raw_items):
        runs, col = [], 0
        for q, k, d, coef, width in it["runs"]:
            at = 0
            while at < width:
                w = min(width - at, 512 - col % 512)
                runs.append((fill + col // 512, col % 512, col, w, q, k[:, at:at + w], d[:, at:at + w], coef))
                at, col = at + w, col + w
        fills = range(fill, fill + -(-col // 512))
        fill = fills[-1] + 1
        chunks, c0 = [], 0
        for b in range(0, len(it["blocks"]), 4):
            part = it["blocks"][b:b + 4]
            cols, here = c0, []
            for w, v in part:
                here.append((cols, w, v))
                cols += w
            chunks.append((chunk, b, here))
            chunk, c0 = chunk + 1, cols
        item = Store()
        item.n, item.runs, item.fills, item.width, item.chunks = n, runs, fills, col, chunks
        item.n_blocks, item.gate, item.place = len(it["blocks"]), it.get("gate"), it["place"]
        item.first, item.last, item.fill_end = it["first"], it["last"], it["fill_end"]
        items.append(item)
    return items


def scores_tensor(pe, a, it):
    for f in it.fills:
        if f >= len(a.score):
            pe.wait_ge(a.scores_read, f - len(a.score) + 1)
        runs = [r for r in it.runs if r[0] == f]
        for _, bc, _, w, q, k, _, _ in runs:
            last = pe.matmul(a.score[f % len(a.score)][:, bc:bc + w], q, k, start=True, stop=True)
        last.then_inc(a.scores_ready, 1)


def turn_tensor(pe, a, it, c):
    chunk, _, blocks = it.chunks[c]
    pe.wait_ge(a.probs_ready, it.n + 1)
    if chunk >= T_BANKS:
        pe.wait_ge(a.pt_ready, chunk - T_BANKS + 1)
    for j, (col, w, _) in enumerate(blocks):
        last = pe.transpose(a.turn[chunk % T_BANKS][0:w, j * P:j * P + P],
                            a.s[:, it.n % a.slots, col:col + w], a.ident[:, :])
    last.then_inc(a.turned, 1)


def values_tensor(pe, a, it, c):
    chunk, b0, blocks = it.chunks[c]
    pe.wait_ge(a.pt_ready, chunk + 1)
    ofill, row, rows, slot = it.place
    if it.first and c == 0 and slot == 0 and ofill >= len(a.obank):
        pe.wait_ge(a.o_ready, ofill - len(a.obank) + 1)
    for j, (_, w, v) in enumerate(blocks):
        last = pe.matmul(a.obank[ofill % len(a.obank)][row:row + rows, slot * P:slot * P + P], v,
                         a.pt[0:w, chunk % PT_SLOTS, j * P:j * P + P],
                         start=it.first and b0 + j == 0, stop=it.last and b0 + j == it.n_blocks - 1)
    last.then_inc(a.values_done, 1)


def attention_tensor(pe, a, items):
    for it in items[:a.lead]:
        scores_tensor(pe, a, it)
    behind = []
    for it in items:
        if it.n + a.lead < len(items):
            scores_tensor(pe, a, items[it.n + a.lead])
        for c in range(len(it.chunks)):
            turn_tensor(pe, a, it, c)
            behind.append((it, c))
            if len(behind) > 2:
                values_tensor(pe, a, *behind.pop(0))
    for it, c in behind:
        values_tensor(pe, a, it, c)


def attention_vector(dve, a, items, lag, between):
    def softmax_max(it):
        if it.n >= a.slots:
            dve.wait_ge(a.turned, items[it.n - a.slots].chunks[-1][0] + 1)
        for f in it.fills:
            dve.wait_ge(a.scores_ready, f + 1)
            runs = [r for r in it.runs if r[0] == f]
            for _, bc, sc, w, _, _, d, coef in runs:
                last = dve.scalar_tensor_tensor(a.s[:, it.n % a.slots, sc:sc + w], d, coef,
                                                a.score[f % len(a.score)][:, bc:bc + w], ALU.mult, ALU.add)
            last.then_inc(a.scores_read, 1)
        dve.wait_ge(a.scores_read, it.fills[-1] + 1)
        dve.tensor_reduce(a.nmax[:, it.n % a.slots:it.n % a.slots + 1], a.s[:, it.n % a.slots, 0:it.width],
                          AX.X, ALU.max, negate=True).then_inc(a.max_ready, 1)

    def scale(it):
        c = slice(it.n % a.slots, it.n % a.slots + 1)
        dve.wait_ge(a.exp_done, it.n + 1)
        one = dve.reciprocal(a.inv[:, c], a.den[:, c])
        if it.gate is None:
            one.then_inc(a.inv_ready, 2)
        else:
            one.then_inc(a.inv_ready, 1)
            dve.wait_ge(a.inv_ready, 2 * it.n + 1)
            dve.tensor_tensor(a.inv[:, c], a.inv[:, c], it.gate, ALU.mult).then_inc(a.inv_ready, 1)

    def output_lo(it):
        f = it.fill_end
        dve.wait_ge(a.o_hi, f + 1)
        dve.tensor_tensor(a.ol[:, a.ktile[f], :], a.obank[f % len(a.obank)][:, :],
                          a.oh[:, a.ktile[f], :].bitcast(F32), ALU.subtract).then_inc(a.o_ready, 1)

    late = a.out_lag + 1
    for it in items:
        softmax_max(it)
        if it.n >= lag:
            scale(items[it.n - lag])
        between(it.n)
        if it.n >= late and items[it.n - late].fill_end is not None:
            output_lo(items[it.n - late])
    if lag:
        scale(items[-1])
    for it in items[len(items) - late:]:
        if it.fill_end is not None:
            output_lo(it)


def attention_scalar(act, a, items, between):
    def exponent(it):
        c = slice(it.n % a.slots, it.n % a.slots + 1)
        act.wait_ge(a.max_ready, it.n + 1)
        if it.n >= a.slots:
            act.wait_ge(a.inv_ready, 2 * (it.n - a.slots + 1))
        s = a.s[:, it.n % a.slots, 0:it.width]
        act.activation(s, s, ACT.Exp, bias=a.nmax[:, c], accum_out=a.den[:, c]).then_inc(a.exp_done, 1)

    def copy_out(it):
        for chunk, _, blocks in it.chunks:
            w, cols = blocks[0][1], len(blocks) * P
            act.wait_ge(a.turned, chunk + 1)
            if chunk >= PT_SLOTS:
                act.wait_ge(a.values_done, chunk - PT_SLOTS + 1)
            act.activation(a.pt[0:w, chunk % PT_SLOTS, 0:cols], a.turn[chunk % T_BANKS][0:w, 0:cols],
                           ACT.Copy).then_inc(a.pt_ready, 1)

    def output_hi(it):
        f = it.fill_end
        act.wait_ge(a.values_done, it.chunks[-1][0] + 1)
        act.activation(a.oh[:, a.ktile[f], :], a.obank[f % len(a.obank)][:, :], ACT.Copy).then_inc(a.o_hi, 1)

    for it in items:
        exponent(it)
        between(it.n)
        if it.n >= a.copy_lag:
            copy_out(items[it.n - a.copy_lag])
        if it.n >= a.out_lag and items[it.n - a.out_lag].fill_end is not None:
            output_hi(items[it.n - a.out_lag])
    for n in range(len(items), len(items) + a.out_lag):
        if n - a.copy_lag < len(items):
            copy_out(items[n - a.copy_lag])
        if items[n - a.out_lag].fill_end is not None:
            output_hi(items[n - a.out_lag])


def attention_gpsimd(g, a, items):
    for it in items:
        c = slice(it.n % a.slots, it.n % a.slots + 1)
        s = a.s[:, it.n % a.slots, 0:it.width]
        g.wait_ge(a.inv_ready, 2 * (it.n + 1))
        g.tensor_scalar(s, s, a.inv[:, c], 1.0, ALU.mult, ALU.mult).then_inc(a.probs_ready, 1)


CKV, CQ, KPE, XCMP, KSW, QN, VSW, GATE, HCMP, UK, KC, VC, UV, UQ = (
    0, 2, 5, 6, 10, 12, 16, 18, 19, 23, 27, 28, 29, 33)
RMS_AFTER = 8


def emptied(n):
    return n + 1 if n < HCMP else n + 1 - (UK - HCMP)


def even_sync(sp, t):
    e = t.even
    for u in range(EVEN_UNITS):
        if u < 18:
            src = t.ev_in[u]
        elif u == 18:
            src = t.ev_gate
        elif u < 27:
            src = t.ev_w1[u - 19]
        elif u < 29:
            src = (t.ev_uk, t.ev_uv)[u - 27]
        elif u < 33:
            src = t.ev_uq[u - 29]
        else:
            src = t.ev_out[u - 33]
        if u == 6:
            used(sp, t, U_EVEN)
            for dst, mask in ((e.mask[:, :], t.tri_mask), (e.dist[:, :, :], t.causal_mask),
                              (e.distc[:, :, :], t.cmp_mask)):
                sp.dma_start(dst, mask).then_inc(t.masks_in[0], 16)
        load_unit(sp, t, U_EVEN + u, src, EVEN_W[u])


def even_tensor(pe, t, x_ready):
    e = t.even

    def tile(n):
        if HCMP <= n - 4 < UK:
            pe.wait_ge(e.gelu, n - 3 - HCMP)
        elif n >= 4:
            pe.wait_ge(e.evac, emptied(n - 4))
        return t.bank[n % 4]

    def unit(u):
        split_ready(pe, t, U_EVEN + u)
        s = (U_EVEN + u) % SPLIT
        return t.whi[:, s, :], t.wlo[:, s, :]

    for u in range(EVEN_IN_UNITS):
        wh, wl = unit(u)
        bank = tile(u)
        if u < VSW:
            for k in range(KD):
                if u == 0:
                    pe.wait_ge(x_ready, k + 1)
                b = slice(k * P, k * P + P)
                last = product3(pe, bank[:, :], wh[:, b], wl[:, b], t.xh[:, k, :], t.xl[:, k, :],
                                k == 0, k == KD - 1)
        else:
            n = P if u < GATE else 24
            for i in range(TT):
                for k in range(KD):
                    b, tok = slice(k * n, k * n + n), slice(i * P, i * P + P)
                    last = product3(pe, bank[:, i * n:i * n + n], t.xh[:, k, tok], t.xl[:, k, tok],
                                    wh[:, b], wl[:, b], k == 0, k == KD - 1)
        last.then_inc(t.units_used, 1)
        if 3 <= u < 3 + KV + KQ:
            x = u - 3
            pe.wait_ge(e.squared, x + 1)
            pe.matmul(t.bank[4 if x < KV else 5][:, :], (t.ones_kv if x < KV else t.ones_q)[:, :],
                      t.lnbuf[x % 3][:, :], start=x in (0, KV), stop=x in (KV - 1, KV + KQ - 1)
                      ).then_inc(e.rms_sum, 1)
    for kind in range(2):
        for m in range(2):
            bank = tile(HCMP + 2 * kind + m)
            for half in range(2):
                wh, wl = unit(19 + 4 * kind + 2 * m + half)
                for kk in range(8):
                    k = 8 * half + kk
                    b = slice(kk * P, kk * P + P)
                    pe.wait_ge(e.b_lo, kind + 1)
                    last = product3(pe, bank[:, 0:NB], wh[:, b], wl[:, b], e.bh[:, kind, k, :],
                                    e.bl[:, kind, k, :], k == 0, k == CMP_K - 1)
                last.then_inc(t.units_used, 1)
    wh, wl = unit(27)
    for m in range(4):
        bank = tile(UK + m)
        pe.wait_ge(e.c_lo, KV)
        for k in range(KV):
            b = slice(k * 512 + m * P, k * 512 + m * P + P)
            last = product3(pe, bank[:, :], wh[:, b], wl[:, b], e.ch[:, k, :], e.cl[:, k, :],
                            k == 0, k == KV - 1)
        last.then_inc(e.tile_done if m < 3 else t.units_used, 1)
    bank = tile(KC)
    pe.wait_ge(e.gelu, 4)
    for m in range(2):
        last = pe.matmul(bank[:, 0:NB], t.w2k[:, m, :], e.gel[:, 0, m, :], start=m == 0, stop=m == 1)
    last.then_inc(e.tile_done, 1)
    bank = tile(VC)
    for grp in range(2):
        for m in range(2):
            last = pe.matmul(bank[0:NC, grp * DH:grp * DH + DH], e.gel[:, 1, m, grp * NC:grp * NC + NC],
                             t.w2v[:, m, :], start=m == 0, stop=m == 1)
    last.then_inc(e.tile_done, 1)
    wh, wl = unit(28)
    for i in range(TT):
        bank = tile(UV + i)
        for k in range(KV):
            b, tok = slice(k * 512, k * 512 + 512), slice(i * P, i * P + P)
            last = product3(pe, bank[:, :], e.ch[:, k, tok], e.cl[:, k, tok], wh[:, b], wl[:, b],
                            k == 0, k == KV - 1)
        last.then_inc(e.tile_done if i < TT - 1 else t.units_used, 1)
    for v in range(UQ_UNITS):
        wh, wl = unit(29 + v)
        for hh in range(2):
            bank = tile(UQ + 2 * v + hh)
            pe.wait_ge(e.c_lo, KV + KQ)
            for k in range(KQ):
                b = slice((hh * KQ + k) * P, (hh * KQ + k) * P + P)
                last = product3(pe, bank[:, :], wh[:, b], wl[:, b], e.ch[:, KV + k, :],
                                e.cl[:, KV + k, :], k == 0, k == KQ - 1)
            last.then_inc(t.units_used if hh else e.tile_done, 1)
    pe.wait_ge(e.evac, emptied(UQ + H - 1))
    pe.wait_ge(e.k_rot, H)
    attention_tensor(pe, e, e.items)
    pe.sem_inc(t.z_done[1], 2)
    for m in range(KD):
        wh, wl = unit(33 + m)
        out_proj_tile(pe, t, 1, m, wh, wl, t.xh, t.xl, KD, (e.o_ready, KD)).then_inc(t.units_used, 1)


def even_vector(dve, t):
    e = t.even

    def rope(bank, tab, out):
        dve.tensor_tensor(e.ra[64:96, :], bank[64:96, :], tab[64:96, :], ALU.mult).then_inc(e.rope, 1)
        dve.tensor_tensor(e.rb[64:96, :], bank[96:128, :], tab[96:128, :], ALU.mult).then_inc(e.rope, 1)
        e.n_rope += 1
        dve.wait_ge(e.rope, 2 * e.n_rope)
        return dve.tensor_tensor(out, e.ra[64:96, :], e.rb[64:96, :], ALU.add)

    def empty(n, last):
        last.then_inc(e.evac, 1)

    for u in range(EVEN_UNITS - KD):
        split_lo(dve, t, U_EVEN + u + LEAD)
        if u < EVEN_IN_UNITS:
            used(dve, t, U_EVEN + u)
            bank = t.bank[u % 4]
            if u < KPE:
                last = dve.tensor_copy(e.craw[:, u, :], bank[:, :])
            elif u == KPE:
                last = rope(bank, t.rope_k, e.krot[64:96, :])
            elif u < KSW:
                kind, grp = divmod(u - XCMP, 2)
                dve.tensor_copy(e.x[0:64, kind, grp, :], bank[0:64, :])
                last = dve.tensor_copy(e.x[64:128, kind, grp, 0:SEQ - 1], bank[64:128, 1:SEQ])
            elif u < QN:
                last = dve.tensor_copy(e.kn[:, u - KSW, :], bank[:, :])
            elif u < VSW:
                last = dve.tensor_scalar(e.qn[:, u - QN, :], bank[:, :], NSA_SCALE, None, ALU.mult)
            elif u < GATE:
                last = dve.tensor_copy(e.vn[:, u - VSW, :, :], bank[:, :].rearrange("p (i n) -> p i n", i=TT))
            else:
                last = dve.tensor_copy(e.gate[:, :], bank[:, 0:96])
            last.then_inc(e.evac, 1)
            if u in (RMS_AFTER + 1, RMS_AFTER + 2):
                r = u - RMS_AFTER - 1
                dve.wait_ge(e.rms_std, r + 1)
                dve.reciprocal(e.rs[:, r, :], e.rs[:, r, :]).then_inc(e.rms_inv, 1)
            if u == RMS_AFTER + 4:
                dve.wait_ge(e.rms_inv, 2)
                for x in range(KV + KQ):
                    dve.scalar_tensor_tensor(e.craw[:, x, :], e.craw[:, x, :], t.rms_g[:, x:x + 1],
                                             e.rs[:, 0 if x < KV else 1, :], ALU.mult,
                                             ALU.mult).then_inc(e.c_full, 1)
            if u == RMS_AFTER + 6:
                for x in range(KV + KQ):
                    dve.wait_ge(e.c_hi, x + 1)
                    dve.tensor_tensor(e.cl[:, x, :], e.craw[:, x, :], e.ch[:, x, :].bitcast(F32),
                                      ALU.subtract).then_inc(e.c_lo, 1)
            if u == EVEN_IN_UNITS - 1:
                for kind in range(2):
                    dve.wait_ge(e.b_hi, kind + 1)
                    dve.tensor_tensor(e.bl[:, kind, :, :], e.bf[:, kind, :, :],
                                      e.bh[:, kind, :, :].bitcast(F32), ALU.subtract).then_inc(e.b_lo, 1)
        elif u == 27:
            dve.wait_ge(e.gate_exp, 1)
            dve.tensor_scalar(e.gate[:, :], e.gate[:, :], 1.0, None, ALU.add).then_inc(e.gate_step, 1)
            dve.wait_ge(e.gate_step, 1)
            dve.reciprocal(e.gate[:, :], e.gate[:, :]).then_inc(e.gate_step, 1)
            dve.wait_ge(e.gate_step, 2)
            dve.tensor_scalar(e.gate[:, 0:H], e.gate[:, 0:H], t.cmp_valid[:, 0:1], None,
                              ALU.mult).then_inc(e.gate_step, 1)
            for m in range(4):
                if m < 3:
                    dve.wait_ge(e.tile_done, m + 1)
                else:
                    used(dve, t, U_EVEN + u)
                dve.tensor_copy(e.kt[0:64, 2 * m, :], t.bank[(UK + m) % 4][0:64, :])
                dve.tensor_copy(e.kt[0:64, 2 * m + 1, :], t.bank[(UK + m) % 4][64:128, :]).then_inc(e.evac, 1)
            dve.wait_ge(e.tile_done, 4)
            dve.tensor_copy(e.kc[:, :], t.bank[KC % 4][:, 0:NB]).then_inc(e.evac, 1)
            dve.wait_ge(e.tile_done, 5)
            dve.tensor_copy(e.vc[0:NC, :], t.bank[VC % 4][0:NC, 0:2 * DH]).then_inc(e.evac, 1)
        elif u == 28:
            for i in range(TT):
                if i < TT - 1:
                    dve.wait_ge(e.tile_done, 6 + i)
                else:
                    used(dve, t, U_EVEN + u)
                dve.tensor_copy(e.vm[:, i, :], t.bank[(UV + i) % 4][:, :]).then_inc(e.evac, 1)
        elif u >= 29:
            for h in (2 * (u - 29), 2 * (u - 29) + 1):
                bank = t.bank[(UQ + h) % 4]
                if h % 2:
                    used(dve, t, U_EVEN + u)
                else:
                    dve.wait_ge(e.tile_done, 9 + h // 2)
                dve.tensor_scalar(e.qt[0:64, h, :], bank[0:64, :], MLA_SCALE, None, ALU.mult)
                dve.wait_ge(e.evac, emptied(UQ + h - 1))
                rope(bank, t.rope_q, e.qt[64:96, h, :]).then_inc(e.evac, 1)
    dve.wait_ge(t.masks_in[0], 48)
    dve.wait_ge(t.dist_step, 4 * TT)
    dve.wait_ge(e.gate_step, 3)
    attention_vector(dve, e, e.items, 1, lambda n: None)
    for m in range(KD):
        split_lo(dve, t, U_EVEN + EVEN_UNITS - KD + m + LEAD)
        used(dve, t, U_EVEN + EVEN_UNITS - KD + m)
        mixer_residual(dve, t, 1, m)


def even_scalar(act, t):
    e = t.even
    for u in range(EVEN_UNITS - KD):
        split_hi(act, t, U_EVEN + u + LEAD)
        if 1 <= u <= KV + KQ:
            x = u - 1
            act.wait_ge(e.evac, x + 1)
            if x >= 3:
                act.wait_ge(e.rms_sum, x - 2)
            act.activation(t.lnbuf[x % 3][:, :], e.craw[:, x, :], ACT.Square).then_inc(e.squared, 1)
        if u == RMS_AFTER:
            for r in range(2):
                act.wait_ge(e.rms_sum, (KV, KV + KQ)[r])
                act.activation(e.rs[:, r, :], t.bank[4 + r][:, :], ACT.Sqrt,
                               bias=t.cst[:, C_RMS_EPS:C_RMS_EPS + 1]).then_inc(e.rms_std, 1)
        if u == RMS_AFTER + 5:
            for x in range(KV + KQ):
                act.wait_ge(e.c_full, x + 1)
                act.activation(e.ch[:, x, :], e.craw[:, x, :], ACT.Copy).then_inc(e.c_hi, 1)
        if u == 16:
            for kind in range(2):
                act.wait_ge(e.b_full, kind + 1)
                act.activation(e.bh[:, kind, :, :], e.bf[:, kind, :, :], ACT.Copy).then_inc(e.b_hi, 1)
        if u in (20, 22, 24, 26):
            m = (u - 20) // 2
            used(act, t, U_EVEN + u)
            act.activation(e.gel[:, m // 2, m % 2, :], t.bank[(HCMP + m) % 4][:, 0:NB],
                           ACT.Gelu_apprx_tanh).then_inc(e.gelu, 1)
        if u == 26:
            act.wait_ge(e.evac, EVEN_IN_UNITS)
            act.activation(e.gate[:, :], e.gate[:, :], ACT.Exp, scale=-1.0).then_inc(e.gate_exp, 1)
    attention_scalar(act, e, e.items, lambda n: None)
    for m in range(KD):
        split_hi(act, t, U_EVEN + EVEN_UNITS - KD + m + LEAD)


def distances_gpsimd(g, t, out, mask_ready, width, keys):
    for i in range(TT):
        w = width(i)
        if t.n_dist:
            g.wait_ge(t.dist_step, t.n_dist)
        t.n_dist += 1
        g.tensor_scalar(t.dist[:, 0:w], keys(i), t.neg_pos_q[:, i:i + 1], -1.0, ALU.add,
                        ALU.mult).then_inc(t.dist_step, 1)
        g.wait_ge(t.dist_step, t.n_dist)
        g.wait_ge(*mask_ready)
        t.n_dist += 1
        g.tensor_tensor(out[:, i, 0:w], out[:, i, 0:w], t.dist[:, 0:w], ALU.add
                        ).then_inc(t.dist_step, 1)


def even_gpsimd(g, t):
    e = t.even
    for kind in range(2):
        g.wait_ge(e.evac, XCMP + 2 * kind + 2)
        for m in range(CMP_K):
            src = e.x[:, kind, :, 2 * m:2 * m + 16 * (NC - 1) + 1:16]
            last = g.tensor_scalar(e.bf[:, kind, m, :].rearrange("p (a b) -> p a b", a=2), src,
                                   t.cmp_pos[:, m:m + 1], 1.0, ALU.add, ALU.mult)
        last.then_inc(e.b_full, 1)
    distances_gpsimd(g, t, e.dist, (t.masks_in[0], 48), lambda i: SEQ, lambda i: t.pos_k[:, :])
    distances_gpsimd(g, t, e.distc, (t.masks_in[0], 48), lambda i: NC,
                     lambda i: t.pos_k[:, 31:SEQ:16])
    g.wait_ge(t.units_used, SPLIT + U_EVEN + 27)
    g.wait_ge(t.dist_step, t.n_dist)
    for h in range(H):
        g.tensor_copy(e.kt[64:96, h, :], e.krot[64:96, :]).then_inc(e.k_rot, 1)
    g.wait_ge(e.k_rot, H)
    attention_gpsimd(g, e, e.items)


def even_items(t):
    e = t.even
    raw = []
    for pair in range(H // 2):
        for i in range(TT):
            for h in (2 * pair, 2 * pair + 1):
                grp, m = divmod(h, 4)
                r = slice(DH * grp, DH * grp + DH)
                q, L = e.qn[r, m, i * P:i * P + P], (i + 1) * P
                place = (pair, DH * (h % 2), DH, i)
                end = pair if i == TT - 1 and h % 2 else None
                gate = lambda br: e.gate[:, i * 24 + br * H + h:i * 24 + br * H + h + 1]
                slope = -NSA_SLOPES[h]
                raw.append(dict(runs=[(q, e.kc[r, grp * NC:grp * NC + NC], e.distc[:, i, :], slope, NC)],
                                blocks=[(NC, e.vc[0:NC, grp * DH:grp * DH + DH])], gate=gate(0),
                                place=place, first=True, last=False, fill_end=None))
                for br in range(2):
                    raw.append(dict(runs=[(q, e.kn[r, br, 0:L], e.dist[:, i, 0:L], slope, L)],
                                    blocks=[(P, e.vn[:, br, j, grp * DH:grp * DH + DH]) for j in range(i + 1)],
                                    gate=gate(1 + br), place=place, first=False, last=br == 1,
                                    fill_end=end if br else None))
    for pair in range(H // 2):
        for i in range(TT):
            for h in (2 * pair, 2 * pair + 1):
                L = (i + 1) * P
                raw.append(dict(runs=[(e.qt[0:96, h, i * P:i * P + P], e.kt[0:96, h, 0:L], e.mask[:, SEQ - L:SEQ], -1.0, L)],
                                blocks=[(P, e.vm[:, j, h * DH:h * DH + DH]) for j in range(i + 1)],
                                place=(4 + pair, DH * (h % 2), DH, i), first=True, last=True,
                                fill_end=4 + pair if i == TT - 1 and h % 2 else None))
    return plan_items(raw)


HEAD_UNITS = 3 * DG
AHEAD = (2, 2, 2, 3)


def odd_units_after(n):
    hp, i = divmod(n, TT)
    if hp + 1 >= DHEADS:
        return range(0)
    first = HEAD_UNITS * (hp + 1) + sum(AHEAD[:i])
    return range(first, first + AHEAD[i])


def odd_sync(sp, t):
    for u in range(ODD_UNITS):
        if u == 6:
            used(sp, t, U_ODD)
            for n in range(DG):
                sp.dma_start(t.odd.dist[n][:, :, :], t.dil_mask[n]).then_inc(t.masks_in[1], 16)
        src = t.od_in[u] if u < ODD_IN_UNITS else t.od_out[u - ODD_IN_UNITS]
        load_unit(sp, t, U_ODD + u, src, ODD_W[u])


ODD_BANKS = (3, 4)


def odd_tensor(pe, t, x_ready):
    o = t.odd

    def unit(u):
        hp, r = divmod(u, HEAD_UNITS)
        split_ready(pe, t, U_ODD + u)
        s = (U_ODD + u) % SPLIT
        wh, wl = t.whi[:, s, :], t.wlo[:, s, :]
        bank = t.bank[ODD_BANKS[u % 2]]
        if u >= 2:
            pe.wait_ge(o.evac, u - 1)
        for k in range(KD) if r < 2 * DG else ():
            if u == 0:
                pe.wait_ge(x_ready, k + 1)
            b = slice(k * P, k * P + P)
            last = product3(pe, bank[:, :], wh[:, b], wl[:, b], t.xh[:, k, :], t.xl[:, k, :],
                            k == 0, k == KD - 1)
        for i in range(TT) if r >= 2 * DG else ():
            for k in range(KD):
                b, tok = slice(k * P, k * P + P), slice(i * P, i * P + P)
                last = product3(pe, bank[:, tok], t.xh[:, k, tok], t.xl[:, k, tok], wh[:, b], wl[:, b],
                                k == 0, k == KD - 1)
        last.then_inc(t.units_used, 1)

    def between(n):
        for u in odd_units_after(n):
            unit(u)
        if n % TT == TT - 1 and n + 1 < len(o.items):
            pe.wait_ge(o.evac, HEAD_UNITS * (n // TT + 2))

    for u in range(HEAD_UNITS):
        unit(u)
    pe.wait_ge(o.evac, HEAD_UNITS)
    odd_attention_tensor(pe, o, o.items, between)
    pe.sem_inc(t.z_done[4], 2)
    for v in range(KD // 2):
        u = ODD_IN_UNITS + v
        split_ready(pe, t, U_ODD + u)
        s = (U_ODD + u) % SPLIT
        for half in range(2):
            b = slice(half * 4 * P, (half + 1) * 4 * P)
            last = out_proj_tile(pe, t, 4, 2 * v + half, t.whi[:, s, b], t.wlo[:, s, b], o.oh, o.ol,
                                 DHEADS, (o.o_ready, DHEADS))
            last.then_inc(t.units_used if half else o.half_done, 1)


def odd_attention_tensor(pe, a, items, between):
    scores_tensor(pe, a, items[0])
    for it in items:
        between(it.n)
        for c in range(len(it.chunks)):
            turn_tensor(pe, a, it, c)
            if c:
                values_tensor(pe, a, it, c - 1)
        if it.n + 1 < len(items):
            scores_tensor(pe, a, items[it.n + 1])
        values_tensor(pe, a, it, len(it.chunks) - 1)


def odd_vector(dve, t):
    o = t.odd

    def unit(u):
        split_lo(dve, t, U_ODD + u + LEAD)
        hp, r = divmod(u, HEAD_UNITS)
        kind, grp = divmod(r, DG)
        bank, side = t.bank[ODD_BANKS[u % 2]], hp % 2
        if hp >= 2 and r == 0:
            dve.wait_ge(o.values_done, o.items[TT * (hp - 1) - 1].chunks[-1][0] + 1)
        used(dve, t, U_ODD + u)
        if kind == 0:
            last = dve.tensor_scalar(o.q[:, side, grp, :], bank[:, :], DIL_SCALE, None, ALU.mult)
        elif kind == 1:
            last = dve.tensor_copy(o.k[:, side, grp, :], bank[:, :])
        else:
            last = dve.tensor_copy(o.v[:, side, grp, :], bank[:, :])
        last.then_inc(o.evac, 1)

    for u in range(HEAD_UNITS):
        unit(u)

    def between(n):
        for u in odd_units_after(n):
            unit(u)

    dve.wait_ge(t.dist_step, (4 + 2 * DG) * TT)
    attention_vector(dve, o, o.items, 0, between)
    for v in range(KD // 2):
        split_lo(dve, t, U_ODD + ODD_IN_UNITS + v + LEAD)
        dve.wait_ge(o.half_done, v + 1)
        mixer_residual(dve, t, 4, 2 * v)
        used(dve, t, U_ODD + ODD_IN_UNITS + v)
        mixer_residual(dve, t, 4, 2 * v + 1)


def odd_scalar(act, t):
    o = t.odd
    for u in range(HEAD_UNITS):
        split_hi(act, t, U_ODD + u + LEAD)

    def between(n):
        for u in odd_units_after(n):
            split_hi(act, t, U_ODD + u + LEAD)

    attention_scalar(act, o, o.items, between)
    for v in range(KD // 2):
        split_hi(act, t, U_ODD + ODD_IN_UNITS + v + LEAD)


def odd_keys(g, i):
    first = max(i * P - DIL[g][0], 0)
    return first, (i + 1) * P - first


def odd_gpsimd(g, t):
    o = t.odd
    for n in range(DG):
        distances_gpsimd(g, t, o.dist[n], (t.masks_in[1], 48), lambda i: odd_keys(n, i)[1],
                         lambda i: t.pos_k[:, odd_keys(n, i)[0]:(i + 1) * P])
    attention_gpsimd(g, o, o.items)


def odd_items(t):
    o = t.odd
    raw = []
    for hp in range(DHEADS):
        for i in range(TT):
            runs, blocks, side = [], [], hp % 2
            for n in range(DG):
                first, w = odd_keys(n, i)
                runs.append((o.q[:, side, n, i * P:i * P + P], o.k[:, side, n, first:first + w], o.dist[n][:, i, 0:w],
                             -DIL_SLOPES[n * DHEADS + hp], w))
                blocks += [(P, o.v[:, side, n, j * P:j * P + P]) for j in range(first // P, i + 1)]
            raw.append(dict(runs=runs,
                            blocks=blocks, place=(hp, 0, P, i), first=True, last=True,
                            fill_end=hp if i == TT - 1 else None))
    return plan_items(raw)


def start_vector(dve, t):
    c, ang, turns = t.setup, t.lnbuf[0], t.lnbuf[1]
    dve.sem_inc(t.units_split, RAW)
    dve.wait_ge(t.consts_in, t.n_consts)

    def step(n, ins):
        ins.then_inc(c, 1)
        dve.wait_ge(c, n)

    step(1, dve.tensor_scalar(t.neg_pos_q[:, :], t.pos_qi[:, :], -1.0, None, ALU.mult))
    step(2, dve.tensor_copy(t.pos_k[:, :], t.pos_ki[:, :]))
    step(3, dve.tensor_scalar(ang[:, :], t.pos_k[:, :], t.cst[:, C_FREQ:C_FREQ + 1], None, ALU.mult))
    step(4, dve.tensor_scalar(turns[:, :], ang[:, :], 1 / (2 * np.pi), t.cst[:, C_TURN:C_TURN + 1],
                              ALU.mult, ALU.add))
    step(5, dve.tensor_scalar(turns[:, :], turns[:, :], MAGIC, MAGIC, ALU.add, ALU.subtract))
    for n, part in enumerate((PI2_A, PI2_B, PI2_C)):
        step(6 + n, dve.scalar_tensor_tensor(ang[:, :], turns[:, :], -part, ang[:, :], ALU.mult, ALU.add))
    step(9, dve.tensor_scalar(ang[:, :], ang[:, :], t.cst[:, C_PHASE:C_PHASE + 1], PI_SAFE,
                              ALU.add, ALU.min))
    step(10, dve.tensor_scalar(ang[:, :], ang[:, :], -PI_SAFE, None, ALU.max))
    dve.wait_ge(t.sin_done, 1)
    step(11, dve.tensor_scalar(t.rope_q[:, :], t.rope_k[:, :], MLA_SCALE, None, ALU.mult))


def start_scalar(act, t):
    act.wait_ge(t.setup, 10)
    act.activation(t.rope_k[:, :], t.lnbuf[0][:, :], ACT.Sin).then_inc(t.sin_done, 1)


def input_hi(act, t):
    for k in range(KD):
        act.wait_ge(t.x_in[k], 16)
        act.activation(t.xh[:, k, :], t.xt[:, k, :], ACT.Copy).then_inc(t.in_hi, 1)


def input_lo(g, t):
    for k in range(KD):
        g.wait_ge(t.in_hi, k + 1)
        g.tensor_tensor(t.xl[:, k, :], t.xt[:, k, :], t.xh[:, k, :].bitcast(F32),
                        ALU.subtract).then_inc(t.in_ready, 1)


def trunk(nc, d, out):
    t = Store()
    t.n_dist = 0
    t.x_t, t.w_gate, t.w_up, t.w_down = d["x_t"], d["w_gate"], d["w_up"], d["w_down"]
    t.ev_in, t.ev_gate, t.ev_w1, t.ev_uk, t.ev_uv = (d[n] for n in (
        "ev_in", "ev_gate", "ev_w1", "ev_uk", "ev_uv"))
    t.ev_uq, t.ev_out, t.od_in, t.od_out = (d[n] for n in ("ev_uq", "ev_out", "od_in", "od_out"))
    t.tri_mask, t.causal_mask, t.cmp_mask, t.dil_mask = (d[n] for n in (
        "tri_mask", "causal_mask", "cmp_mask", "dil_mask"))
    with ExitStack() as ctx:
        def sb(name, shape, dtype=F32, scope=ctx):
            return scope.enter_context(nc.sbuf_tensor(name, shape, dtype))

        def sem(name):
            return ctx.enter_context(nc.semaphore(name))

        def sems(name, n):
            return [sem(f"{name}_{i}") for i in range(n)]

        t.xt = sb("xt", [P, KD, SEQ])
        t.xh = sb("xh", [P, KD, SEQ], F32R)
        t.xl = sb("xl", [P, KD, SEQ], F32R)
        t.raw = sb("raw", [P, RAW, UNIT])
        t.whi = sb("whi", [P, SPLIT, UNIT], F32R)
        t.wlo = sb("wlo", [P, SPLIT, UNIT], F32R)
        t.rope_k = sb("rope_k", [P, SEQ])
        t.rope_q = sb("rope_q", [P, SEQ])
        t.pos_k = sb("pos_k", [P, SEQ])
        t.neg_pos_q = sb("neg_pos_q", [P, TT])
        t.dist = sb("dist", [P, SEQ])
        t.pos_ki = t.dist[:, :].bitcast(I32)
        t.pos_qi = sb("pos_qi", [P, TT], I32)
        t.zsum, t.qsum, t.sq = t.lnbuf = [sb(n, [P, SEQ]) for n in ("zsum", "qsum", "sq")]
        t.zsum3, t.qsum3, t.sq3 = (b[:, :].rearrange("p (a n) -> p a n", a=1) for b in t.lnbuf)
        t.ident = sb("ident", [P, P])
        t.ones_kv = sb("ones_kv", [P, P])
        t.ones_q = sb("ones_q", [P, P])
        t.gains = sb("gains", [P, 6, DEPTH, KD])
        t.rms_g = sb("rms_g", [P, KV + KQ])
        t.w2k = sb("w2k", [P, 2, P])
        t.w2v = sb("w2v", [P, 2, DH])
        t.cmp_pos = sb("cmp_pos", [P, CMP_K])
        t.cst = sb("cst", [P, 5])
        t.cmp_valid = sb("cmp_valid", [P, 1])
        t.stats = sb("stats", [P, 2 * TT])
        t.mu2, t.var, t.std, t.rstd, t.nmr = (sb(n, [P, TT]) for n in ("mu2", "var", "std", "rstd", "nmr"))
        small = [(t.cst[:, :], d["c_cst"]), (t.pos_qi[:, :], d["c_pos_q"]), (t.pos_ki, d["c_pos_k"]),
                 (t.ident[:, :], d["c_ident"]), (t.gains[:, :, :, :], d["c_gains"]),
                 (t.ones_kv[:, :], d["c_ones_kv"]), (t.ones_q[:, :], d["c_ones_q"]),
                 (t.rms_g[:, :], d["c_rms_g"]), (t.w2k[:, :, :], d["c_w2k"]),
                 (t.w2v[:, :, :], d["c_w2v"]), (t.cmp_pos[:, :], d["c_cmp_pos"]),
                 (t.cmp_valid[:, :], d["c_cmp_valid"])]
        t.n_consts = 16 * len(small)

        with ExitStack() as scope:
            t.hh = sb("hh", [P, KF, SEQ], F32R, scope)
            t.hl = sb("hl", [P, KF, SEQ], F32R, scope)
            t.sg = sb("sg", [P, 2, SEQ], F32, scope)
            t.hf = sb("hf", [P, 2, SEQ], F32, scope)
        e = t.even = Store()
        e.n_rope, e.ident = 0, t.ident
        e.lead, e.slots, e.copy_lag, e.out_lag = 5, 7, 3, 6
        with ExitStack() as scope:
            e.vm = sb("e_vm", [P, TT, H * DH], F32, scope)
            e.qn = sb("e_qn", [P, 4, SEQ], F32, scope)
            e.kn = sb("e_kn", [P, 2, SEQ], F32, scope)
            e.vn = sb("e_vn", [P, 2, TT, P], F32, scope)
            e.dist = sb("e_dist", [P, TT, SEQ], F32, scope)
            e.distc = sb("e_distc", [P, TT, NC], F32, scope)
            e.mask = sb("e_mask", [P, SEQ], F32, scope)
            e.kc = sb("e_kc", [P, NB], F32, scope)
            e.vc = sb("e_vc", [P, 2 * DH], F32, scope)
            e.gate = sb("e_gate", [P, TT * 24], F32, scope)
            e.gel = sb("e_gel", [P, 2, 2, NB], F32, scope)
            e.krot = sb("e_krot", [P, SEQ], F32, scope)
            e.ra = sb("e_ra", [P, SEQ], F32, scope)
            e.rb = sb("e_rb", [P, SEQ], F32, scope)
            e.nmax, e.den, e.inv = (sb(n, [P, e.slots], F32, scope) for n in ("e_nmax", "e_den", "e_inv"))
            with ExitStack() as part:
                e.x = sb("e_x", [P, 2, 2, SEQ], F32, part)
                e.bf = sb("e_bf", [P, 2, CMP_K, NB], F32, part)
                e.bh = sb("e_bh", [P, 2, CMP_K, NB], F32R, part)
                e.bl = sb("e_bl", [P, 2, CMP_K, NB], F32R, part)
            e.qt = sb("e_qt", [P, H, SEQ], F32, scope)
            e.kt = sb("e_kt", [P, H, SEQ], F32, scope)
            with ExitStack() as part:
                e.craw = sb("e_craw", [P, KV + KQ, SEQ], F32, part)
                e.ch = sb("e_ch", [P, KV + KQ, SEQ], F32R, part)
                e.cl = sb("e_cl", [P, KV + KQ, SEQ], F32R, part)
                e.rs = sb("e_rs", [P, 2, SEQ], F32, part)
            e.s = sb("e_s", [P, e.slots, SEQ], F32, scope)
            e.pt = sb("e_pt", [P, PT_SLOTS, 4 * P], F32, scope)
        e.oh, e.ol = t.xh, t.xl
        e.ktile = [4, 5, 6, 7, 0, 1, 2, 3]
        o = t.odd = Store()
        o.ident, o.slots, o.copy_lag, o.out_lag = t.ident, 3, 0, 0
        with ExitStack() as scope:
            o.q = sb("o_q", [P, 2, DG, SEQ], F32, scope)
            o.k = sb("o_k", [P, 2, DG, SEQ], F32, scope)
            o.v = sb("o_v", [P, 2, DG, SEQ], F32, scope)
            o.dist = [sb(f"o_dist{n}", [P, TT, 2 * P if n == 0 else SEQ], F32, scope) for n in range(DG)]
            o.s = sb("o_s", [P, o.slots, 10 * P], F32, scope)
            o.pt = sb("o_pt", [P, PT_SLOTS, 4 * P], F32, scope)
            o.oh = sb("o_oh", [P, DHEADS, SEQ], F32R, scope)
            o.ol = sb("o_ol", [P, DHEADS, SEQ], F32R, scope)
            o.nmax, o.den, o.inv = (sb(n, [P, o.slots], F32, scope) for n in ("o_nmax", "o_den", "o_inv"))
        o.ktile = [0, 1, 2, 3]

        t.bank = [ctx.enter_context(nc.psum_tensor(f"bank{i}", [P, 512], F32)) for i in range(8)]
        e.score, e.turn, e.obank = t.bank[0:4], t.bank[4:6], t.bank[6:8]
        o.score, o.obank, o.turn = t.bank[0:3], t.bank[5:6], t.bank[6:8]

        t.consts_in, t.out_stored = sem("consts_in"), sem("out_stored")
        t.setup, t.sin_done, t.in_hi, t.in_ready = (sem(n) for n in ("setup", "sin_done", "in_hi", "in_ready"))
        t.units_hi, t.units_split, t.units_used = (sem(n) for n in ("units_hi", "units_split", "units_used"))
        t.dist_step = sem("dist_step")
        t.x_in, t.raw_landed, t.masks_in = sems("x_in", KD), sems("raw_landed", RAW), sems("masks_in", 2)
        t.h_mul, t.h_hi, t.h_ready, t.silu_done = (sems(n, 4) for n in ("h_mul", "h_hi", "h_ready", "silu_done"))
        t.z_done, t.acc, t.col_sums, t.col, t.std_done = (sems(n, 6) for n in (
            "z_done", "acc", "col_sums", "col", "std_done"))
        t.maps, t.normed, t.x_hi, t.x_ready = (sems(n, 6) for n in ("maps", "normed", "x_hi", "x_ready"))
        for a, name in ((e, "e"), (o, "o")):
            a.scores_ready, a.scores_read = sem(name + "_scores_ready"), sem(name + "_scores_read")
            a.max_ready, a.exp_done, a.inv_ready, a.probs_ready = (sem(f"{name}_{n}") for n in (
                "max_ready", "exp_done", "inv_ready", "probs_ready"))
            a.turned, a.pt_ready, a.values_done = (sem(f"{name}_{n}") for n in ("turned", "pt_ready", "values_done"))
            a.o_hi, a.o_ready, a.evac = (sem(f"{name}_{n}") for n in ("o_hi", "o_ready", "evac"))
        e.tile_done, e.squared, e.rms_sum, e.rms_std, e.rms_inv = (sem("e_" + n) for n in (
            "tile_done", "squared", "rms_sum", "rms_std", "rms_inv"))
        e.c_full, e.c_hi, e.c_lo, e.b_full, e.b_hi, e.b_lo = (sem("e_" + n) for n in (
            "c_full", "c_hi", "c_lo", "b_full", "b_hi", "b_lo"))
        e.gelu, e.gate_exp, e.gate_step, e.rope, e.k_rot = (sem("e_" + n) for n in (
            "gelu", "gate_exp", "gate_step", "rope", "k_rot"))
        o.half_done = sem("o_half_done")
        e.items, o.items = even_items(t), odd_items(t)

        block = ctx.enter_context(nc.Block())

        @block.sync
        def _(sp):
            for dst, src in small:
                sp.dma_start(dst, src).then_inc(t.consts_in, 16)
            for k in range(KD):
                sp.dma_start(t.xt[:, k, :], t.x_t[k]).then_inc(t.x_in[k], 16)
            ffn_sync(sp, t, 0)
            even_sync(sp, t)
            ffn_sync(sp, t, 1)
            ffn_sync(sp, t, 2)
            odd_sync(sp, t)
            ffn_sync(sp, t, 3)
            for k in range(KD):
                sp.wait_ge(t.normed[5], 3 * (k + 1))
                sp.dma_start(out[k], t.xt[:, k, :]).then_inc(t.out_stored, 16)
            sp.wait_ge(t.out_stored, 16 * KD)

        @block.tensor
        def _(pe):
            pe.sem_inc(t.units_used, SPLIT)
            pe.wait_ge(t.consts_in, t.n_consts)
            ffn_tensor(pe, t, 0, t.in_ready)
            norm_tensor(pe, t, 0)
            even_tensor(pe, t, t.x_ready[0])
            norm_tensor(pe, t, 1)
            ffn_tensor(pe, t, 1, t.x_ready[1])
            norm_tensor(pe, t, 2)
            ffn_tensor(pe, t, 2, t.x_ready[2])
            norm_tensor(pe, t, 3)
            odd_tensor(pe, t, t.x_ready[3])
            norm_tensor(pe, t, 4)
            ffn_tensor(pe, t, 3, t.x_ready[4])
            norm_tensor(pe, t, 5)

        @block.scalar
        def _(act):
            for u in range(LEAD):
                split_hi(act, t, u)
            input_hi(act, t)
            start_scalar(act, t)
            ffn_scalar(act, t, 0)
            norm_scalar(act, t, 0)
            even_scalar(act, t)
            norm_scalar(act, t, 1)
            ffn_scalar(act, t, 1)
            norm_scalar(act, t, 2)
            ffn_scalar(act, t, 2)
            norm_scalar(act, t, 3)
            odd_scalar(act, t)
            norm_scalar(act, t, 4)
            ffn_scalar(act, t, 3)
            norm_scalar(act, t, 5)

        @block.vector
        def _(dve):
            start_vector(dve, t)
            for u in range(LEAD):
                split_lo(dve, t, u)
            ffn_vector(dve, t, 0)
            norm_vector(dve, t, 0)
            even_vector(dve, t)
            norm_vector(dve, t, 1)
            ffn_vector(dve, t, 1)
            norm_vector(dve, t, 2)
            ffn_vector(dve, t, 2)
            norm_vector(dve, t, 3)
            odd_vector(dve, t)
            norm_vector(dve, t, 4)
            ffn_vector(dve, t, 3)
            norm_vector(dve, t, 5)

        @block.gpsimd
        def _(g):
            input_lo(g, t)
            g.wait_ge(t.setup, 11)
            sums_gpsimd(g, t, 0)
            norm_gpsimd(g, t, 0)
            even_gpsimd(g, t)
            sums_gpsimd(g, t, 1)
            norm_gpsimd(g, t, 1)
            sums_gpsimd(g, t, 2)
            norm_gpsimd(g, t, 2)
            sums_gpsimd(g, t, 3)
            norm_gpsimd(g, t, 3)
            odd_gpsimd(g, t)
            sums_gpsimd(g, t, 4)
            norm_gpsimd(g, t, 4)
            sums_gpsimd(g, t, 5)


def constants():
    q, k = np.arange(SEQ)[:, None], np.arange(SEQ)[None, :]
    by_tile = lambda m: np.ascontiguousarray(
        np.where(m, 0.0, BIG).astype(np.float32).reshape(TT, P, -1).transpose(1, 0, 2))
    tri = np.zeros((P, SEQ), np.float32)
    tri[:, SEQ - P:] = np.where(np.arange(P)[:, None] >= np.arange(P)[None, :], 0.0, BIG)
    win = np.zeros((P, TT, 2 * P), np.float32)
    full = by_tile((q >= k) & (q - k <= DIL[0][0]))
    for i in range(TT):
        first, w = odd_keys(0, i)
        win[:, i, :w] = full[:, i, first:first + w]
    half = ROPE // 2
    freq = (10000.0 ** (-np.arange(half, dtype=np.float32) / half)).astype(np.float32)
    cst = np.zeros((P, 5), np.float32)
    cst[:, C_INVD] = 1 / D_MODEL
    cst[:, C_RMS_EPS] = RMS_EPS
    cst[:, C_FREQ] = np.tile(freq, P // half)
    turn = np.zeros(P)
    turn[64:96], turn[96:112] = 0.25, 0.5
    cst[:, C_TURN] = turn
    cst[:, C_PHASE] = 2 * np.pi * turn
    return {
        "c_cst": cst, "c_ident": np.eye(P, dtype=np.float32),
        "c_ones_kv": np.full((P, P), 1 / KV_RANK, np.float32),
        "c_ones_q": np.full((P, P), 1 / Q_RANK, np.float32),
        "c_cmp_valid": (np.arange(P) >= 31).astype(np.float32)[:, None],
        "tri_mask": tri, "causal_mask": by_tile(q >= k),
        "cmp_mask": by_tile(16 * np.arange(NC)[None, :] + 31 <= q),
        "dil_mask0": win, "dil_mask1": by_tile((q >= k) & ((q - k) % DIL[1][1] == 0)),
        "dil_mask2": by_tile((q >= k) & ((q - k) % DIL[2][1] == 0)),
    }


def blocks(w):
    k, m = w.shape
    return np.ascontiguousarray(w.reshape(k // P, P, m // P, P).transpose(2, 1, 0, 3)).reshape(m // P, P, -1)


def rows(w):
    k, m = w.shape
    return np.ascontiguousarray(w.reshape(k // P, P, m).transpose(1, 0, 2)).reshape(P, -1)


def layouts(inp):
    a = {}
    a["x_t"] = np.ascontiguousarray(inp["x"][0].T).reshape(KD, P, SEQ)
    pos = inp["positions"][0]
    a["c_pos_k"] = np.ascontiguousarray(np.broadcast_to(pos, (P, SEQ)))
    a["c_pos_q"] = np.ascontiguousarray(pos.reshape(TT, P).T)
    norms = [inp[f"ln{n}_{c}"] for n in (1, 2, 3) for c in "gb"]
    a["c_gains"] = np.ascontiguousarray(np.stack(norms).reshape(6, DEPTH, KD, P).transpose(3, 0, 1, 2))
    for f in range(4):
        n, layer = 1 + f % 2, f // 2
        a[f"w_gate{f}"] = blocks(inp[f"ffn{n}_w_gate"][layer])
        a[f"w_up{f}"] = blocks(inp[f"ffn{n}_w_up"][layer])
        a[f"w_down{f}"] = blocks(inp[f"ffn{n}_w_down"][layer])
    w = inp["mix_in_even"][0]
    cut = np.split(w, np.cumsum([Q_RANK, KV_RANK, ROPE, H * DH] + [2 * DH] * 6), axis=1)
    c_q, c_kv, k_pe, q, k_c, v_c, k_s, v_s, k_w, v_w, gate = cut
    half = ROPE // 2
    swap = lambda m: np.concatenate([m[:, half:], m[:, :half]], axis=1)
    tiles = [c_kv, c_q, np.concatenate([k_pe, swap(k_pe)] * 2, axis=1)]
    tiles += [np.concatenate([m[:, s:s + DH]] * 2, axis=1) for m in (k_c, v_c) for s in (0, DH)]
    tiles += [k_s, k_w]
    tiles += [np.concatenate([q[:, m * DH:m * DH + DH], q[:, (4 + m) * DH:(5 + m) * DH]], axis=1)
              for m in range(4)]
    tiles += [v_s, v_w]
    a["ev_in"] = blocks(np.concatenate(tiles, axis=1))
    a["ev_gate"] = rows(gate)
    w1 = []
    for kind in "kv":
        w1 += list(blocks(inp[f"nsa_cmp_{kind}_w1"][0]).reshape(2, P, 2, UNIT).transpose(0, 2, 1, 3).reshape(4, P, UNIT))
    a["ev_w1"] = np.ascontiguousarray(np.stack(w1))
    w2k, w2v = inp["nsa_cmp_k_w2"][0], inp["nsa_cmp_v_w2"][0]
    a["c_w2k"] = rows(np.concatenate([w2k, w2k], axis=1)).reshape(P, 2, P)
    a["c_w2v"] = rows(w2v).reshape(P, 2, DH)
    a["c_cmp_pos"] = np.ascontiguousarray(inp["nsa_cmp_pos"][0].reshape(CMP_K, P).T)
    a["ev_uk"], a["ev_uv"] = rows(inp["mla_w_uk"][0]), rows(inp["mla_w_uv"][0])
    uq = inp["mla_w_uq"][0].reshape(Q_RANK, H, NOPE + ROPE)
    uq = np.concatenate([uq, uq[..., NOPE + half:], uq[..., NOPE:NOPE + half]], axis=2)
    a["ev_uq"] = np.ascontiguousarray(blocks(uq.reshape(Q_RANK, H * P)).reshape(UQ_UNITS, 2, P, -1)
                                      .transpose(0, 2, 1, 3)).reshape(UQ_UNITS, P, -1)
    a["c_rms_g"] = np.ascontiguousarray(np.concatenate([inp["mla_kv_norm"][0], inp["mla_q_norm"][0]])
                                        .reshape(KV + KQ, P).T)
    a["ev_out"] = blocks(inp["mix_out_even"][0])
    od = inp["mix_in_odd"][0].reshape(D_MODEL, 3, DG, DHEADS, P).transpose(0, 3, 1, 2, 4)
    a["od_in"] = blocks(od.reshape(D_MODEL, -1))
    a["od_out"] = np.ascontiguousarray(blocks(inp["mix_out_odd"][0]).reshape(KD // 2, 2, P, -1)
                                       .transpose(0, 2, 1, 3)).reshape(KD // 2, P, -1)
    return a


def build(nc, arrays):
    d = {n: nc.dram_tensor(n, a.shape, mybir.dt.from_np(a.dtype), kind="ExternalInput").ap()
         for n, a in arrays.items()}
    for n in ("w_gate", "w_up", "w_down"):
        d[n] = [d[f"{n}{f}"] for f in range(4)]
    d["dil_mask"] = [d[f"dil_mask{n}"] for n in range(DG)]
    out = nc.dram_tensor("out_t", (KD, P, SEQ), F32, kind="ExternalOutput").ap()
    trunk(nc, d, out)


def kernel(**inputs):
    import concourse.bacc as bacc
    from concourse.bass_utils import run_bass_kernel_spmd

    arrays = {**layouts({n: np.asarray(v) for n, v in inputs.items()}), **constants()}
    nc = bacc.Bacc("TRN2", target_bir_lowering=False, num_devices=1)
    build(nc, arrays)
    r = run_bass_kernel_spmd(nc, [arrays], core_ids=[0])
    out = np.asarray(r.results[0]["out_t"]).reshape(D_MODEL, SEQ)
    return np.ascontiguousarray(out.T)[None]
```

```python
from contextlib import ExitStack

import numpy as np

import concourse.bass as bass
from concourse import mybir

F32 = mybir.dt.float32
F32R = mybir.dt.float32r
I32 = mybir.dt.int32
ACT = mybir.ActivationFunctionType
ALU = mybir.AluOpType
AX = mybir.AxisListType

P = 128
D_MODEL, SEQ, DEPTH, D_FF = 1024, 512, 2, 2816
KD = D_MODEL // P
KF = D_FF // P
TT = SEQ // P
ALPHA = (2 * DEPTH) ** 0.25
LN_EPS, RMS_EPS = 1e-5, 1e-6
BIG = 1e30

H = 8
Q_RANK, KV_RANK, NOPE, ROPE = 384, 256, 64, 32
KQ, KV = Q_RANK // P, KV_RANK // P
MLA_SCALE = (NOPE + ROPE) ** -0.5
DH = 64
NSA_SCALE = DH ** -0.5
NC = SEQ // 16 - 1
CMP_K = 16
NB = 2 * NC
DIL = ((128, 1), (512, 4), (2048, 16))
DG, DHEADS = 3, 4
DIL_SCALE = P ** -0.5
NSA_SLOPES = [2.0 ** (-8.0 * (n + 1) / H) for n in range(H)]
DIL_SLOPES = [2.0 ** (-8.0 * (n + 1) / (DG * DHEADS)) for n in range(DG * DHEADS)]

C_INVD, C_RMS_EPS, C_FREQ, C_TURN, C_PHASE = range(5)
MAGIC = 1.5 * 2.0 ** 23
PI2_A = 6.28125
PI2_B = float(np.float32(2 * np.pi - PI2_A) // 2.0 ** -20 * 2.0 ** -20)
PI2_C = float(2 * np.pi - PI2_A - PI2_B)
PI_SAFE = float(np.nextafter(np.float32(np.pi), np.float32(0)))



class Store:
    pass


RAW, SPLIT = 4, 2
UNIT = KD * P
LEAD = SPLIT

EVEN_IN_UNITS, EVEN_CMP_UNITS, UQ_UNITS = 19, 8, 4
EVEN_UNITS = EVEN_IN_UNITS + EVEN_CMP_UNITS + 2 + UQ_UNITS + KD
ODD_IN_UNITS = 3 * DG * DHEADS
ODD_UNITS = ODD_IN_UNITS + KD // 2
DN_BLOCKS = (8, 7, 7)
DN_STARTS = (0, 8, 15)
FFN_W = [KD * P] * (2 * KF) + [b * P for b in DN_BLOCKS] * KD
VG = 2 * 2 * DH + 24
VG_TILES = ((0, 3), (3, 6), (6, 8))
EVEN_W = ([KD * P] * 16 + [(b - a) * VG for a, b in VG_TILES] + [KD * P] * EVEN_CMP_UNITS + [KV * 512] * 2
          + [2 * KQ * P] * UQ_UNITS + [KD * P] * KD)
ODD_W = [KD * P] * ODD_UNITS
WIDTH = FFN_W + EVEN_W + FFN_W + FFN_W + ODD_W + FFN_W
U_FFN = [0, len(FFN_W) + EVEN_UNITS, 2 * len(FFN_W) + EVEN_UNITS,
         3 * len(FFN_W) + EVEN_UNITS + ODD_UNITS]
U_EVEN = len(FFN_W)
U_ODD = 3 * len(FFN_W) + EVEN_UNITS
N_UNITS = len(WIDTH)
LN_OF_FFN = (0, 2, 3, 5)
GU_STEPS = KF // 2
DN_STEPS = 2
DN_UNITS = 12


def load_unit(sp, t, u, src, width, d=0):
    sp.wait_ge(t.units_split, d + (u + 1))
    sp.dma_start(t.raw[:, u % RAW, :width], src).then_inc(t.raw_landed[u % RAW], 16)


def split_hi(act, t, u, d=0):
    if u >= N_UNITS:
        return
    act.wait_ge(t.raw_landed[u % RAW], d * (16 // RAW) + 16 * (u // RAW + 1))
    act.wait_ge(t.units_used, d + (u + 1))
    act.activation(t.whi[:, u % SPLIT, :WIDTH[u]], t.raw[:, u % RAW, :WIDTH[u]],
                   ACT.Copy).then_inc(t.units_hi, 1)


def split_lo(dve, t, u, d=0):
    if u >= N_UNITS:
        return
    dve.wait_ge(t.units_hi, d + (u + 1))
    dve.tensor_tensor(t.wlo[:, u % SPLIT, :WIDTH[u]], t.raw[:, u % RAW, :WIDTH[u]],
                      t.whi[:, u % SPLIT, :WIDTH[u]].bitcast(F32), ALU.subtract
                      ).then_inc(t.units_split, 1)


def split_ready(pe, t, u, d=0):
    pe.wait_ge(t.units_split, d + (RAW + u + 1))


def used(eng, t, u, d=0):
    eng.wait_ge(t.units_used, d + (SPLIT + u + 1))


def product3(pe, out, wh, wl, xh, xl, start, stop):
    pe.matmul(out, wl, xh, start=start, stop=False)
    pe.matmul(out, wh, xl, start=False, stop=False)
    return pe.matmul(out, wh, xh, start=False, stop=stop)


def ffn_sync(sp, t, f):
    u0 = U_FFN[f]
    with sp.Fori(0, GU_STEPS) as i:
        for j in range(4):
            w = (t.w_gate, t.w_up)[j % 2][f]
            load_unit(sp, t, u0 + j, w[bass.ds(2 * i + j // 2, 1)].rearrange("a p n -> p (a n)"),
                      UNIT, 4 * i)
    with sp.Fori(0, DN_STEPS) as i:
        for j in range(DN_UNITS):
            m, part = divmod(j, 3)
            row = t.w_down[f][bass.ds(4 * i + m, 1)].rearrange("a p n -> p (a n)")
            at, w = DN_STARTS[part] * P, DN_BLOCKS[part] * P
            load_unit(sp, t, u0 + 2 * KF + j, row[:, at:at + w], w, DN_UNITS * i)


def first_pair(pe, t, u0, banks, x_ready):
    split_ready(pe, t, u0 + 1)
    for k in range(KD):
        pe.wait_ge(x_ready, k + 1)
        b = slice(k * P, k * P + P)
        for j in range(2):
            s = (u0 + j) % SPLIT
            last = product3(pe, banks[j][:, :], t.whi[:, s, b], t.wlo[:, s, b],
                            t.xh[:, k, :], t.xl[:, k, :], k == 0, k == KD - 1)
            if k == KD - 1:
                last.then_inc(t.units_used, 1)


def ffn_tensor(pe, t, f, x_ready):
    u0, ln = U_FFN[f], LN_OF_FFN[f]
    pe.sem_inc(t.h_mul[f], 2)
    pe.sem_inc(t.z_done[ln], 2)
    def gate_up(j, i):
        split_ready(pe, t, u0 + j, 4 * i)
        if j % 2 == 0:
            pe.wait_ge(t.h_mul[f], 2 * i + (j // 2 + 1))
        for k in range(KD):
            b = slice(k * P, k * P + P)
            s = (u0 + j) % SPLIT
            last = product3(pe, t.bank[j][:, :], t.whi[:, s, b], t.wlo[:, s, b],
                            t.xh[:, k, :], t.xl[:, k, :], k == 0, k == KD - 1)
        last.then_inc(t.units_used, 1)

    first_pair(pe, t, u0, t.bank[0:2], x_ready)
    gate_up(2, 0)
    gate_up(3, 0)
    with pe.Fori(1, GU_STEPS) as i:
        for j in range(4):
            gate_up(j, i)
    u1 = u0 + 2 * KF
    with pe.Fori(0, DN_STEPS) as i:
        for j in range(DN_UNITS):
            m, part = divmod(j, 3)
            split_ready(pe, t, u1 + j, DN_UNITS * i)
            if part == 0:
                pe.wait_ge(t.z_done[ln], 4 * i + (m + 1))
            for kk in range(DN_BLOCKS[part]):
                k = DN_STARTS[part] + kk
                if m == 0:
                    pe.wait_ge(t.h_ready[f], k + 1)
                b = slice(kk * P, kk * P + P)
                s = (u1 + j) % SPLIT
                last = product3(pe, t.bank[4 + m % 2][:, :], t.whi[:, s, b], t.wlo[:, s, b],
                                t.hh[:, k, :], t.hl[:, k, :], k == 0, k == KF - 1)
            last.then_inc(t.units_used, 1)


def ffn_scalar(act, t, f):
    u0, u1 = U_FFN[f], U_FFN[f] + 2 * KF
    u2 = u1 + 3 * KD

    def silu(j, i):
        if j % 2 == 0:
            used(act, t, u0 + j, 4 * i)
            act.wait_ge(t.h_mul[f], 2 * i + (j // 2 + 1))
            act.activation(t.sg[:, j // 2, :], t.bank[j][:, :], ACT.Silu).then_inc(t.silu_done[f], 1)

    with act.Fori(0, GU_STEPS - 1) as i:
        for j in range(4):
            split_hi(act, t, u0 + j + LEAD, 4 * i)
            silu(j, i)
    for j in range(4):
        split_hi(act, t, u1 - 4 + j + LEAD)
        silu(j, GU_STEPS - 1)
    with act.Fori(0, DN_STEPS - 1) as i:
        for j in range(DN_UNITS):
            split_hi(act, t, u1 + j + LEAD, DN_UNITS * i)
    for j in range(DN_UNITS):
        split_hi(act, t, u2 - DN_UNITS + j + LEAD)


def ffn_vector(dve, t, f):
    u0, u1, ln = U_FFN[f], U_FFN[f] + 2 * KF, LN_OF_FFN[f]
    u2 = u1 + 3 * KD

    def hidden(j, i):
        if j % 2 == 0:
            return
        p = j // 2
        dve.wait_ge(t.silu_done[f], 2 * i + (p + 1))
        used(dve, t, u0 + j, 4 * i)
        dve.tensor_tensor(t.hf[:, p, :], t.sg[:, p, :], t.bank[j][:, :], ALU.mult).then_inc(t.h_mul[f], 1)
        dve.wait_ge(t.h_mul[f], 2 * i + (p + 3))
        dst = bass.ds(2 * i + p, 1)
        dve.tensor_copy(t.hh[:, dst, :], t.hf[:, p:p + 1, :]).then_inc(t.h_hi[f], 1)
        dve.wait_ge(t.h_hi[f], 2 * i + (p + 1))
        dve.tensor_tensor(t.hl[:, dst, :], t.hf[:, p:p + 1, :], t.hh[:, dst, :].bitcast(F32),
                          ALU.subtract).then_inc(t.h_ready[f], 1)

    def residual(j, i):
        m, part = divmod(j, 3)
        if part < 2:
            return
        used(dve, t, u1 + j, DN_UNITS * i)
        dst = bass.ds(4 * i + m, 1)
        dve.scalar_tensor_tensor(t.xt[:, dst, :], t.xt[:, dst, :], 2 * ALPHA,
                                 t.bank[4 + m % 2][:, :].rearrange("p (a n) -> p a n", a=1),
                                 ALU.mult, ALU.add).then_inc(t.z_done[ln], 1)

    with dve.Fori(0, GU_STEPS - 1) as i:
        for j in range(4):
            split_lo(dve, t, u0 + j + LEAD, 4 * i)
            hidden(j, i)
    for j in range(4):
        split_lo(dve, t, u1 - 4 + j + LEAD)
        hidden(j, GU_STEPS - 1)
    with dve.Fori(0, DN_STEPS - 1) as i:
        for j in range(DN_UNITS):
            split_lo(dve, t, u1 + j + LEAD, DN_UNITS * i)
            residual(j, i)
    for j in range(DN_UNITS):
        split_lo(dve, t, u2 - DN_UNITS + j + LEAD)
        residual(j, DN_STEPS - 1)


SUMMED = KD - 1


def sums_gpsimd(g, t, ln):
    if ln:
        g.wait_ge(t.maps, 2 * (ln - 1) + 2)
        g.wait_ge(t.norm_b, KD * (ln - 1) + KD)
        g.wait_ge(t.norm_c, KD * (ln - 1) + KD)
        g.wait_ge(t.x_hi[ln - 1], KD)
    g.memset(t.zsum[:, :], 0.0).then_inc(t.acc[ln], 1)
    g.memset(t.qsum[:, :], 0.0).then_inc(t.acc[ln], 1)
    with g.Fori(0, SUMMED) as m:
        z = t.xt[:, bass.ds(m, 1), :]
        g.wait_ge(t.z_done[ln], m + 3)
        g.wait_ge(t.acc[ln], 3 * m + 2)
        g.tensor_tensor(t.sq3, z, z, ALU.mult).then_inc(t.acc[ln], 1)
        g.tensor_tensor(t.zsum3, t.zsum3, z, ALU.add).then_inc(t.acc[ln], 1)
        g.wait_ge(t.acc[ln], 3 * m + 3)
        g.tensor_tensor(t.qsum3, t.qsum3, t.sq3, ALU.add).then_inc(t.acc[ln], 1)


def norm_tensor(pe, t, ln):
    def by_token(bank, at, src):
        for i in range(TT):
            last = pe.matmul(bank[:, at + i:at + i + 1], src[:, i * P:i * P + P],
                             t.cst[:, C_INVD:C_INVD + 1], start=True, stop=True)
        last.then_inc(t.col_sums, 1)

    if ln == 0:
        pe.wait_ge(t.consts_in, t.n_consts)
    pe.wait_ge(t.acc[ln], 2 + 3 * SUMMED)
    by_token(t.bank[6], 0, t.zsum)
    by_token(t.bank[6], 4, t.qsum)
    pe.wait_ge(t.z_done[ln], KD + 2)
    by_token(t.bank[7], 0, t.xt[:, KD - 1, :])
    pe.wait_ge(t.last_sq, ln + 1)
    by_token(t.bank[7], 4, t.sq)
    for n, (b, src) in enumerate(((7, t.zsum), (6, t.sq))):
        pe.wait_ge(t.diag, TT * 2 * ln + TT * (n + 1))
        pe.matmul(t.bank[b][:, :], t.ones[:, :], src[:, :], start=True, stop=True).then_inc(t.maps, 1)


def norm_scalar(act, t, ln):
    if ln == 0:
        act.wait_ge(t.consts_in, t.n_consts)
    act.wait_ge(t.acc[ln], 2 + 3 * SUMMED)
    act.wait_ge(t.z_done[ln], KD + 2)
    act.activation(t.sq[:, :], t.xt[:, KD - 1, :], ACT.Square).then_inc(t.last_sq, 1)
    act.wait_ge(t.col, 6 * ln + 4)
    act.activation(t.std[:, :], t.var[:, :], ACT.Sqrt).then_inc(t.std_done, 1)
    which, layer = ln % 3, ln // 3
    for k in range(KD) if ln < 5 else ():
        act.wait_ge(t.norm_b, KD * ln + k + 1)
        act.activation(t.xh[:, k, :], t.norm_tmp[k % 2][:, :], ACT.Identity,
                       bias=t.gains[:, 2 * which + 1, layer, k:k + 1],
                       scale=t.gains[:, 2 * which, layer, k:k + 1]).then_inc(t.x_hi[ln], 1)


def norm_vector(dve, t, ln):
    eps = LN_EPS * (1 if ln % 3 == 1 else 4)
    c = t.col
    dve.wait_ge(t.col_sums, 4 * ln + 2)
    dve.tensor_copy(t.part_stats[:, :], t.bank[6][:, 0:8]).then_inc(c, 1)
    dve.wait_ge(t.col_sums, 4 * ln + 4)
    dve.wait_ge(c, 6 * ln + 1)
    dve.tensor_tensor(t.stats[:, :], t.part_stats[:, :], t.bank[7][:, 0:8], ALU.add).then_inc(c, 1)
    dve.wait_ge(c, 6 * ln + 2)
    dve.tensor_tensor(t.mu2[:, :], t.stats[:, 0:4], t.stats[:, 0:4], ALU.mult).then_inc(c, 1)
    dve.wait_ge(c, 6 * ln + 3)
    dve.scalar_tensor_tensor(t.var[:, :], t.stats[:, 4:8], eps, t.mu2[:, :], ALU.add,
                             ALU.subtract).then_inc(c, 1)
    dve.wait_ge(t.std_done, ln + 1)
    dve.reciprocal(t.rstd[:, :], t.std[:, :]).then_inc(c, 1)
    dve.wait_ge(c, 6 * ln + 5)
    for i in range(TT):
        dve.tensor_scalar(t.zsum[:, i * P:i * P + P], t.ident[:, :], t.rstd[:, i:i + 1], None,
                          ALU.mult).then_inc(t.diag, 1)
    dve.scalar_tensor_tensor(t.nmr[:, :], t.stats[:, 0:4], -1.0, t.rstd[:, :], ALU.mult,
                             ALU.mult).then_inc(c, 1)
    dve.wait_ge(c, 6 * ln + 6)
    for i in range(TT):
        dve.tensor_scalar(t.sq[:, i * P:i * P + P], t.ident[:, :], t.nmr[:, i:i + 1], None,
                          ALU.mult).then_inc(t.diag, 1)
    which, layer = ln % 3, ln // 3
    for k in range(KD + 2):
        if k < KD:
            dve.wait_ge(t.maps, 2 * ln + 1)
            dve.tensor_tensor(t.xt[:, k, :], t.xt[:, k, :], t.bank[7][:, :], ALU.mult).then_inc(t.norm_a, 1)
        if 1 <= k <= KD:
            n = k - 1
            dve.wait_ge(t.maps, 2 * ln + 2)
            dve.wait_ge(t.norm_a, KD * ln + n + 1)
            if n >= 2:
                dve.wait_ge(t.norm_c, KD * ln + n - 1)
                if ln < 5:
                    dve.wait_ge(t.x_hi[ln], n - 1)
            dve.tensor_tensor(t.norm_tmp[n % 2][:, :], t.xt[:, n, :], t.bank[6][:, :],
                              ALU.add).then_inc(t.norm_b, 1)
        if k >= 2:
            n = k - 2
            dve.wait_ge(t.norm_b, KD * ln + n + 1)
            dve.tensor_scalar(t.xt[:, n, :], t.norm_tmp[n % 2][:, :], t.gains[:, 2 * which, layer, n:n + 1],
                              t.gains[:, 2 * which + 1, layer, n:n + 1], ALU.mult,
                              ALU.add).then_inc(t.norm_c, 1)


def norm_gpsimd(g, t, ln):
    for k in range(KD):
        g.wait_ge(t.x_hi[ln], k + 1)
        g.wait_ge(t.norm_c, KD * ln + k + 1)
        g.tensor_tensor(t.xl[:, k, :], t.xt[:, k, :], t.xh[:, k, :].bitcast(F32),
                        ALU.subtract).then_inc(t.x_ready[ln], 1)


def out_proj_tile(pe, t, ln, m, wh, wl, oh, ol, tiles, o_ready):
    pe.wait_ge(t.z_done[ln], m + 1)
    pe.wait_ge(o_ready[0], o_ready[1])
    for k in range(tiles):
        b = slice(k * P, k * P + P)
        last = product3(pe, t.bank[4 + m % 2][:, :], wh[:, b], wl[:, b], oh[:, k, :], ol[:, k, :],
                        k == 0, k == tiles - 1)
    return last


def mixer_residual(dve, t, ln, m):
    dve.scalar_tensor_tensor(t.xt[:, m, :], t.xt[:, m, :], ALPHA, t.bank[4 + m % 2][:, :],
                             ALU.mult, ALU.add).then_inc(t.z_done[ln], 1)


T_BANKS = 2
PT_SLOTS = 4


def plan_items(raw_items):
    fill = chunk = 0
    items = []
    for n, it in enumerate(raw_items):
        runs, col = [], 0
        for q, k, d, coef, width in it["runs"]:
            at = 0
            while at < width:
                w = min(width - at, 512 - col % 512)
                runs.append((fill + col // 512, col % 512, col, w, q, k[:, at:at + w], d[:, at:at + w], coef))
                at, col = at + w, col + w
        fills = range(fill, fill + -(-col // 512))
        fill = fills[-1] + 1
        chunks, c0 = [], 0
        for b in range(0, len(it["blocks"]), 4):
            part = it["blocks"][b:b + 4]
            cols, here = c0, []
            for w, v in part:
                here.append((cols, w, v))
                cols += w
            chunks.append((chunk, b, here))
            chunk, c0 = chunk + 1, cols
        item = Store()
        item.n, item.runs, item.fills, item.width, item.chunks = n, runs, fills, col, chunks
        item.n_blocks, item.gate, item.place = len(it["blocks"]), it.get("gate"), it["place"]
        item.first, item.last, item.fill_end = it["first"], it["last"], it["fill_end"]
        items.append(item)
    return items


def scores_tensor(pe, a, it):
    for f in it.fills:
        if f >= len(a.score):
            pe.wait_ge(a.scores_read, f - len(a.score) + 1)
        runs = [r for r in it.runs if r[0] == f]
        for _, bc, _, w, q, k, _, _ in runs:
            last = pe.matmul(a.score[f % len(a.score)][:, bc:bc + w], q, k, start=True, stop=True)
        last.then_inc(a.scores_ready, 1)


def turn_tensor(pe, a, it, c):
    chunk, _, blocks = it.chunks[c]
    pe.wait_ge(a.probs_ready, it.n + 1)
    if chunk >= T_BANKS:
        pe.wait_ge(a.pt_ready, chunk - T_BANKS + 1)
    for j, (col, w, _) in enumerate(blocks):
        last = pe.transpose(a.turn[chunk % T_BANKS][0:w, j * P:j * P + P],
                            a.s[:, it.n % a.slots, col:col + w], a.ident[:, :])
    last.then_inc(a.turned, 1)


def values_tensor(pe, a, it, c):
    chunk, b0, blocks = it.chunks[c]
    pe.wait_ge(a.pt_ready, chunk + 1)
    ofill, row, rows, slot = it.place
    if it.first and c == 0 and slot == 0 and ofill >= len(a.obank):
        pe.wait_ge(a.o_ready, ofill - len(a.obank) + 1)
    for j, (_, w, v) in enumerate(blocks):
        last = pe.matmul(a.obank[ofill % len(a.obank)][row:row + rows, slot * P:slot * P + P], v,
                         a.pt[0:w, chunk % PT_SLOTS, j * P:j * P + P],
                         start=it.first and b0 + j == 0, stop=it.last and b0 + j == it.n_blocks - 1)
    last.then_inc(a.values_done, 1)


def attention_tensor(pe, a, items):
    for it in items[:a.lead]:
        scores_tensor(pe, a, it)
    behind = []
    for it in items:
        if it.n + a.lead < len(items):
            scores_tensor(pe, a, items[it.n + a.lead])
        for c in range(len(it.chunks)):
            turn_tensor(pe, a, it, c)
            behind.append((it, c))
            if len(behind) > 2:
                values_tensor(pe, a, *behind.pop(0))
    for it, c in behind:
        values_tensor(pe, a, it, c)


def attention_vector(dve, a, items, lag, between):
    def softmax_max(it):
        if it.n >= a.slots:
            dve.wait_ge(a.turned, items[it.n - a.slots].chunks[-1][0] + 1)
        for f in it.fills:
            dve.wait_ge(a.scores_ready, f + 1)
            runs = [r for r in it.runs if r[0] == f]
            for _, bc, sc, w, _, _, d, coef in runs:
                last = dve.scalar_tensor_tensor(a.s[:, it.n % a.slots, sc:sc + w], d, coef,
                                                a.score[f % len(a.score)][:, bc:bc + w], ALU.mult, ALU.add)
            last.then_inc(a.scores_read, 1)
        dve.wait_ge(a.scores_read, it.fills[-1] + 1)
        dve.tensor_reduce(a.nmax[:, it.n % a.slots:it.n % a.slots + 1], a.s[:, it.n % a.slots, 0:it.width],
                          AX.X, ALU.max, negate=True).then_inc(a.max_ready, 1)

    def scale(it):
        c = slice(it.n % a.slots, it.n % a.slots + 1)
        dve.wait_ge(a.exp_done, it.n + 1)
        one = dve.reciprocal(a.inv[:, c], a.den[:, c])
        if it.gate is None:
            one.then_inc(a.inv_ready, 2)
        else:
            one.then_inc(a.inv_ready, 1)
            dve.wait_ge(a.inv_ready, 2 * it.n + 1)
            dve.tensor_tensor(a.inv[:, c], a.inv[:, c], it.gate, ALU.mult).then_inc(a.inv_ready, 1)

    def output_lo(it):
        f = it.fill_end
        dve.wait_ge(a.o_hi, f + 1)
        dve.tensor_tensor(a.ol[:, a.ktile[f], :], a.obank[f % len(a.obank)][:, :],
                          a.oh[:, a.ktile[f], :].bitcast(F32), ALU.subtract).then_inc(a.o_ready, 1)

    late = a.out_lag + 1
    for it in items:
        softmax_max(it)
        if it.n >= lag:
            scale(items[it.n - lag])
        between(it.n)
        if it.n >= late and items[it.n - late].fill_end is not None:
            output_lo(items[it.n - late])
    if lag:
        scale(items[-1])
    for it in items[len(items) - late:]:
        if it.fill_end is not None:
            output_lo(it)


def attention_scalar(act, a, items, between):
    def exponent(it):
        c = slice(it.n % a.slots, it.n % a.slots + 1)
        act.wait_ge(a.max_ready, it.n + 1)
        if it.n >= a.slots:
            act.wait_ge(a.inv_ready, 2 * (it.n - a.slots + 1))
        s = a.s[:, it.n % a.slots, 0:it.width]
        act.activation(s, s, ACT.Exp, bias=a.nmax[:, c], accum_out=a.den[:, c]).then_inc(a.exp_done, 1)

    def copy_out(it):
        for chunk, _, blocks in it.chunks:
            w, cols = blocks[0][1], len(blocks) * P
            act.wait_ge(a.turned, chunk + 1)
            if chunk >= PT_SLOTS:
                act.wait_ge(a.values_done, chunk - PT_SLOTS + 1)
            act.activation(a.pt[0:w, chunk % PT_SLOTS, 0:cols], a.turn[chunk % T_BANKS][0:w, 0:cols],
                           ACT.Copy).then_inc(a.pt_ready, 1)

    def output_hi(it):
        f = it.fill_end
        act.wait_ge(a.values_done, it.chunks[-1][0] + 1)
        act.activation(a.oh[:, a.ktile[f], :], a.obank[f % len(a.obank)][:, :], ACT.Copy).then_inc(a.o_hi, 1)

    for it in items:
        exponent(it)
        between(it.n)
        if it.n >= a.copy_lag:
            copy_out(items[it.n - a.copy_lag])
        if it.n >= a.out_lag and items[it.n - a.out_lag].fill_end is not None:
            output_hi(items[it.n - a.out_lag])
    for n in range(len(items), len(items) + a.out_lag):
        if n - a.copy_lag < len(items):
            copy_out(items[n - a.copy_lag])
        if items[n - a.out_lag].fill_end is not None:
            output_hi(items[n - a.out_lag])


def attention_gpsimd(g, a, items):
    for it in items:
        c = slice(it.n % a.slots, it.n % a.slots + 1)
        s = a.s[:, it.n % a.slots, 0:it.width]
        g.wait_ge(a.inv_ready, 2 * (it.n + 1))
        g.tensor_scalar(s, s, a.inv[:, c], 1.0, ALU.mult, ALU.mult).then_inc(a.probs_ready, 1)


KPE, XCMP, KSW, QN, VSW, HCMP, UK, KC, VC, UV, UQ = 5, 6, 10, 12, 16, 20, 24, 28, 29, 30, 34
RMS_AFTER = 8


def emptied(n):
    return n + 1 if n < HCMP else n + 1 - (UK - HCMP)


def even_sync(sp, t):
    e = t.even
    for u in range(EVEN_UNITS):
        if u < VSW:
            src = t.ev_in[u]
        elif u < 19:
            src = t.ev_vg[:, VG_TILES[u - VSW][0] * VG:VG_TILES[u - VSW][1] * VG]
        elif u < 27:
            src = t.ev_w1[u - 19]
        elif u < 29:
            src = (t.ev_uk, t.ev_uv)[u - 27]
        elif u < 33:
            src = t.ev_uq[u - 29]
        else:
            src = t.ev_out[u - 33]
        if u == 6:
            used(sp, t, U_EVEN)
            for dst, mask in ((e.mask[:, :], t.tri_mask), (e.dist[:, :, :], t.causal_mask),
                              (e.distc[:, :, :], t.cmp_mask)):
                sp.dma_start(dst, mask).then_inc(t.masks_in[0], 16)
        load_unit(sp, t, U_EVEN + u, src, EVEN_W[u])


def even_tensor(pe, t, x_ready):
    e = t.even

    def tile(n):
        if HCMP <= n - 4 < UK:
            pe.wait_ge(e.gelu, n - 3 - HCMP)
        elif n >= 4:
            pe.wait_ge(e.evac, emptied(n - 4))
        return t.bank[n % 4]

    def unit(u):
        split_ready(pe, t, U_EVEN + u)
        s = (U_EVEN + u) % SPLIT
        return t.whi[:, s, :], t.wlo[:, s, :]

    first_pair(pe, t, U_EVEN, t.bank[0:2], x_ready)
    for u in range(2, EVEN_IN_UNITS):
        wh, wl = unit(u)
        if u < VSW:
            bank = tile(u)
            for k in range(KD):
                b = slice(k * P, k * P + P)
                last = product3(pe, bank[:, :], wh[:, b], wl[:, b], t.xh[:, k, :], t.xl[:, k, :],
                                k == 0, k == KD - 1)
        else:
            k0, k1 = VG_TILES[u - VSW]
            for i in range(TT):
                bank = tile(VSW + i) if u == VSW else t.bank[i]
                for k in range(k0, k1):
                    b, tok = slice((k - k0) * VG, (k - k0 + 1) * VG), slice(i * P, i * P + P)
                    last = product3(pe, bank[:, 0:VG], t.xh[:, k, tok], t.xl[:, k, tok],
                                    wh[:, b], wl[:, b], k == 0, k == KD - 1)
        last.then_inc(t.units_used, 1)
        if 3 <= u < 3 + KV + KQ:
            x = u - 3
            pe.wait_ge(e.squared, x + 1)
            pe.matmul(t.bank[4 if x < KV else 5][:, :], (t.ones_kv if x < KV else t.ones_q)[:, :],
                      t.lnbuf[x % 3][:, :], start=x in (0, KV), stop=x in (KV - 1, KV + KQ - 1)
                      ).then_inc(e.rms_sum, 1)
    for kind in range(2):
        for m in range(2):
            bank = tile(HCMP + 2 * kind + m)
            for half in range(2):
                wh, wl = unit(19 + 4 * kind + 2 * m + half)
                for kk in range(8):
                    k = 8 * half + kk
                    b = slice(kk * P, kk * P + P)
                    pe.wait_ge(e.b_lo, kind + 1)
                    last = product3(pe, bank[:, 0:NB], wh[:, b], wl[:, b], e.bh[:, kind, k, :],
                                    e.bl[:, kind, k, :], k == 0, k == CMP_K - 1)
                last.then_inc(t.units_used, 1)
    wh, wl = unit(27)
    for m in range(4):
        bank = tile(UK + m)
        pe.wait_ge(e.c_lo, KV)
        for k in range(KV):
            b = slice(k * 512 + m * P, k * 512 + m * P + P)
            last = product3(pe, bank[:, :], wh[:, b], wl[:, b], e.ch[:, k, :], e.cl[:, k, :],
                            k == 0, k == KV - 1)
        last.then_inc(e.tile_done if m < 3 else t.units_used, 1)
    bank = tile(KC)
    pe.wait_ge(e.gelu, 4)
    for m in range(2):
        last = pe.matmul(bank[:, 0:NB], t.w2k[:, m, :], e.gel[:, 0, m, :], start=m == 0, stop=m == 1)
    last.then_inc(e.tile_done, 1)
    bank = tile(VC)
    for grp in range(2):
        for m in range(2):
            last = pe.matmul(bank[0:NC, grp * DH:grp * DH + DH], e.gel[:, 1, m, grp * NC:grp * NC + NC],
                             t.w2v[:, m, :], start=m == 0, stop=m == 1)
    last.then_inc(e.tile_done, 1)
    wh, wl = unit(28)
    for i in range(TT):
        bank = tile(UV + i)
        for k in range(KV):
            b, tok = slice(k * 512, k * 512 + 512), slice(i * P, i * P + P)
            last = product3(pe, bank[:, :], e.ch[:, k, tok], e.cl[:, k, tok], wh[:, b], wl[:, b],
                            k == 0, k == KV - 1)
        last.then_inc(e.tile_done if i < TT - 1 else t.units_used, 1)
    for v in range(UQ_UNITS):
        wh, wl = unit(29 + v)
        for hh in range(2):
            bank = tile(UQ + 2 * v + hh)
            pe.wait_ge(e.c_lo, KV + KQ)
            for k in range(KQ):
                b = slice((hh * KQ + k) * P, (hh * KQ + k) * P + P)
                last = product3(pe, bank[:, :], wh[:, b], wl[:, b], e.ch[:, KV + k, :],
                                e.cl[:, KV + k, :], k == 0, k == KQ - 1)
            last.then_inc(t.units_used if hh else e.tile_done, 1)
    pe.wait_ge(e.evac, emptied(UQ + H - 1))
    pe.wait_ge(e.k_rot, H)
    attention_tensor(pe, e, e.items)
    pe.sem_inc(t.z_done[1], 2)
    for m in range(KD):
        wh, wl = unit(33 + m)
        out_proj_tile(pe, t, 1, m, wh, wl, t.xh, t.xl, KD, (e.o_ready, KD)).then_inc(t.units_used, 1)


def even_vector(dve, t):
    e = t.even

    def rope(bank, tab, out):
        dve.tensor_tensor(e.ra[64:96, :], bank[64:96, :], tab[64:96, :], ALU.mult).then_inc(e.rope, 1)
        dve.tensor_tensor(e.rb[64:96, :], bank[96:128, :], tab[96:128, :], ALU.mult).then_inc(e.rope, 1)
        e.n_rope += 1
        dve.wait_ge(e.rope, 2 * e.n_rope)
        return dve.tensor_tensor(out, e.ra[64:96, :], e.rb[64:96, :], ALU.add)

    def empty(n, last):
        last.then_inc(e.evac, 1)

    for u in range(EVEN_UNITS - KD):
        split_lo(dve, t, U_EVEN + u + LEAD)
        if u < EVEN_IN_UNITS:
            used(dve, t, U_EVEN + u)
            bank = t.bank[u % 4]
            if u < KPE:
                last = dve.tensor_copy(e.craw[:, u, :], bank[:, :])
            elif u == KPE:
                last = rope(bank, t.rope_k, e.krot[64:96, :])
            elif u < KSW:
                kind, grp = divmod(u - XCMP, 2)
                dve.tensor_copy(e.x[0:64, kind, grp, :], bank[0:64, :])
                last = dve.tensor_copy(e.x[64:128, kind, grp, 0:SEQ - 1], bank[64:128, 1:SEQ])
            elif u < QN:
                last = dve.tensor_copy(e.kn[:, u - KSW, :], bank[:, :])
            elif u < VSW:
                last = dve.tensor_scalar(e.qn[:, u - QN, :], bank[:, :], NSA_SCALE, None, ALU.mult)
            if u < VSW:
                last.then_inc(e.evac, 1)
            for i in range(TT) if u == EVEN_IN_UNITS - 1 else ():
                dve.tensor_copy(e.vn[:, :, i, :], t.bank[i][:, 0:2 * P].rearrange("p (a n) -> p a n", a=2))
                dve.tensor_copy(e.gate[:, i * 24:i * 24 + 24], t.bank[i][:, 2 * P:VG]).then_inc(e.evac, 1)
            if u in (RMS_AFTER + 1, RMS_AFTER + 2):
                r = u - RMS_AFTER - 1
                dve.wait_ge(e.rms_std, r + 1)
                dve.reciprocal(e.rs[:, r, :], e.rs[:, r, :]).then_inc(e.rms_inv, 1)
            if u == RMS_AFTER + 4:
                dve.wait_ge(e.rms_inv, 2)
                for x in range(KV + KQ):
                    dve.scalar_tensor_tensor(e.craw[:, x, :], e.craw[:, x, :], t.rms_g[:, x:x + 1],
                                             e.rs[:, 0 if x < KV else 1, :], ALU.mult,
                                             ALU.mult).then_inc(e.c_full, 1)
            if u == RMS_AFTER + 6:
                for x in range(KV + KQ):
                    dve.wait_ge(e.c_hi, x + 1)
                    dve.tensor_tensor(e.cl[:, x, :], e.craw[:, x, :], e.ch[:, x, :].bitcast(F32),
                                      ALU.subtract).then_inc(e.c_lo, 1)
            if u == EVEN_IN_UNITS - 1:
                for kind in range(2):
                    dve.wait_ge(e.b_hi, kind + 1)
                    dve.tensor_tensor(e.bl[:, kind, :, :], e.bf[:, kind, :, :],
                                      e.bh[:, kind, :, :].bitcast(F32), ALU.subtract).then_inc(e.b_lo, 1)
        elif u == 27:
            dve.wait_ge(e.gate_exp, 1)
            dve.tensor_scalar(e.gate[:, :], e.gate[:, :], 1.0, None, ALU.add).then_inc(e.gate_step, 1)
            dve.wait_ge(e.gate_step, 1)
            dve.reciprocal(e.gate[:, :], e.gate[:, :]).then_inc(e.gate_step, 1)
            dve.wait_ge(e.gate_step, 2)
            dve.tensor_scalar(e.gate[:, 0:H], e.gate[:, 0:H], t.cmp_valid[:, 0:1], None,
                              ALU.mult).then_inc(e.gate_step, 1)
            for m in range(4):
                if m < 3:
                    dve.wait_ge(e.tile_done, m + 1)
                else:
                    used(dve, t, U_EVEN + u)
                dve.tensor_copy(e.kt[0:64, 2 * m, :], t.bank[(UK + m) % 4][0:64, :])
                dve.tensor_copy(e.kt[0:64, 2 * m + 1, :], t.bank[(UK + m) % 4][64:128, :]).then_inc(e.evac, 1)
            dve.wait_ge(e.tile_done, 4)
            dve.tensor_copy(e.kc[:, :], t.bank[KC % 4][:, 0:NB]).then_inc(e.evac, 1)
            dve.wait_ge(e.tile_done, 5)
            dve.tensor_copy(e.vc[0:NC, :], t.bank[VC % 4][0:NC, 0:2 * DH]).then_inc(e.evac, 1)
        elif u == 28:
            for i in range(TT):
                if i < TT - 1:
                    dve.wait_ge(e.tile_done, 6 + i)
                else:
                    used(dve, t, U_EVEN + u)
                dve.tensor_copy(e.vm[:, i, :], t.bank[(UV + i) % 4][:, :]).then_inc(e.evac, 1)
        elif u >= 29:
            for h in (2 * (u - 29), 2 * (u - 29) + 1):
                bank = t.bank[(UQ + h) % 4]
                if h % 2:
                    used(dve, t, U_EVEN + u)
                else:
                    dve.wait_ge(e.tile_done, 9 + h // 2)
                dve.tensor_scalar(e.qt[0:64, h, :], bank[0:64, :], MLA_SCALE, None, ALU.mult)
                dve.wait_ge(e.evac, emptied(UQ + h - 1))
                rope(bank, t.rope_q, e.qt[64:96, h, :]).then_inc(e.evac, 1)
    dve.wait_ge(t.masks_in[0], 48)
    dve.wait_ge(t.dist_step, 4 * TT)
    dve.wait_ge(e.gate_step, 3)
    attention_vector(dve, e, e.items, 1, lambda n: None)
    for m in range(KD):
        split_lo(dve, t, U_EVEN + EVEN_UNITS - KD + m + LEAD)
        used(dve, t, U_EVEN + EVEN_UNITS - KD + m)
        mixer_residual(dve, t, 1, m)


def even_scalar(act, t):
    e = t.even
    for u in range(EVEN_UNITS - KD):
        split_hi(act, t, U_EVEN + u + LEAD)
        if 1 <= u <= KV + KQ:
            x = u - 1
            act.wait_ge(e.evac, x + 1)
            if x >= 3:
                act.wait_ge(e.rms_sum, x - 2)
            act.activation(t.lnbuf[x % 3][:, :], e.craw[:, x, :], ACT.Square).then_inc(e.squared, 1)
        if u == RMS_AFTER:
            for r in range(2):
                act.wait_ge(e.rms_sum, (KV, KV + KQ)[r])
                act.activation(e.rs[:, r, :], t.bank[4 + r][:, :], ACT.Sqrt,
                               bias=t.cst[:, C_RMS_EPS:C_RMS_EPS + 1]).then_inc(e.rms_std, 1)
        if u == RMS_AFTER + 5:
            for x in range(KV + KQ):
                act.wait_ge(e.c_full, x + 1)
                act.activation(e.ch[:, x, :], e.craw[:, x, :], ACT.Copy).then_inc(e.c_hi, 1)
        if u == 16:
            for kind in range(2):
                act.wait_ge(e.b_full, kind + 1)
                act.activation(e.bh[:, kind, :, :], e.bf[:, kind, :, :], ACT.Copy).then_inc(e.b_hi, 1)
        if u in (20, 22, 24, 26):
            m = (u - 20) // 2
            used(act, t, U_EVEN + u)
            act.activation(e.gel[:, m // 2, m % 2, :], t.bank[(HCMP + m) % 4][:, 0:NB],
                           ACT.Gelu_apprx_tanh).then_inc(e.gelu, 1)
        if u == 26:
            act.wait_ge(e.evac, HCMP)
            act.activation(e.gate[:, :], e.gate[:, :], ACT.Exp, scale=-1.0).then_inc(e.gate_exp, 1)
    attention_scalar(act, e, e.items, lambda n: None)
    for m in range(KD):
        split_hi(act, t, U_EVEN + EVEN_UNITS - KD + m + LEAD)


def distances_gpsimd(g, t, out, mask_ready, width, keys):
    for i in range(TT):
        w = width(i)
        if t.n_dist:
            g.wait_ge(t.dist_step, t.n_dist)
        t.n_dist += 1
        g.tensor_scalar(t.dist[:, 0:w], keys(i), t.neg_pos_q[:, i:i + 1], -1.0, ALU.add,
                        ALU.mult).then_inc(t.dist_step, 1)
        g.wait_ge(t.dist_step, t.n_dist)
        g.wait_ge(*mask_ready)
        t.n_dist += 1
        g.tensor_tensor(out[:, i, 0:w], out[:, i, 0:w], t.dist[:, 0:w], ALU.add
                        ).then_inc(t.dist_step, 1)


def even_gpsimd(g, t):
    e = t.even
    for kind in range(2):
        g.wait_ge(e.evac, XCMP + 2 * kind + 2)
        for m in range(CMP_K):
            src = e.x[:, kind, :, 2 * m:2 * m + 16 * (NC - 1) + 1:16]
            last = g.tensor_scalar(e.bf[:, kind, m, :].rearrange("p (a b) -> p a b", a=2), src,
                                   t.cmp_pos[:, m:m + 1], 1.0, ALU.add, ALU.mult)
        last.then_inc(e.b_full, 1)
    distances_gpsimd(g, t, e.dist, (t.masks_in[0], 48), lambda i: SEQ, lambda i: t.pos_k[:, :])
    distances_gpsimd(g, t, e.distc, (t.masks_in[0], 48), lambda i: NC,
                     lambda i: t.pos_k[:, 31:SEQ:16])
    g.wait_ge(t.units_used, SPLIT + U_EVEN + 27)
    g.wait_ge(t.dist_step, t.n_dist)
    for h in range(H):
        g.tensor_copy(e.kt[64:96, h, :], e.krot[64:96, :]).then_inc(e.k_rot, 1)
    g.wait_ge(e.k_rot, H)
    attention_gpsimd(g, e, e.items)


def even_items(t):
    e = t.even
    raw = []
    for pair in range(H // 2):
        for i in range(TT):
            for h in (2 * pair, 2 * pair + 1):
                grp, m = divmod(h, 4)
                r = slice(DH * grp, DH * grp + DH)
                q, L = e.qn[r, m, i * P:i * P + P], (i + 1) * P
                place = (pair, DH * (h % 2), DH, i)
                end = pair if i == TT - 1 and h % 2 else None
                gate = lambda br: e.gate[:, i * 24 + br * H + h:i * 24 + br * H + h + 1]
                slope = -NSA_SLOPES[h]
                raw.append(dict(runs=[(q, e.kc[r, grp * NC:grp * NC + NC], e.distc[:, i, :], slope, NC)],
                                blocks=[(NC, e.vc[0:NC, grp * DH:grp * DH + DH])], gate=gate(0),
                                place=place, first=True, last=False, fill_end=None))
                for br in range(2):
                    raw.append(dict(runs=[(q, e.kn[r, br, 0:L], e.dist[:, i, 0:L], slope, L)],
                                    blocks=[(P, e.vn[:, br, j, grp * DH:grp * DH + DH]) for j in range(i + 1)],
                                    gate=gate(1 + br), place=place, first=False, last=br == 1,
                                    fill_end=end if br else None))
    for pair in range(H // 2):
        for i in range(TT):
            for h in (2 * pair, 2 * pair + 1):
                L = (i + 1) * P
                raw.append(dict(runs=[(e.qt[0:96, h, i * P:i * P + P], e.kt[0:96, h, 0:L], e.mask[:, SEQ - L:SEQ], -1.0, L)],
                                blocks=[(P, e.vm[:, j, h * DH:h * DH + DH]) for j in range(i + 1)],
                                place=(4 + pair, DH * (h % 2), DH, i), first=True, last=True,
                                fill_end=4 + pair if i == TT - 1 and h % 2 else None))
    return plan_items(raw)


HEAD_UNITS = 2 * DG
V_UNITS = 4 * DG
AHEAD = (1, 1, 2, 2)


def odd_units_after(n):
    hp, i = divmod(n, TT)
    if hp + 1 >= DHEADS:
        return range(0)
    first = HEAD_UNITS * (hp + 1) + sum(AHEAD[:i])
    return range(first, first + AHEAD[i])


def odd_sync(sp, t):
    for u in range(ODD_UNITS):
        if u == 6:
            used(sp, t, U_ODD)
            for n in range(DG):
                sp.dma_start(t.odd.dist[n][:, :, :], t.dil_mask[n]).then_inc(t.masks_in[1], 16)
        if u < V_UNITS:
            src = t.od_v[u]
        else:
            src = t.od_qk[u - V_UNITS] if u < ODD_IN_UNITS else t.od_out[u - ODD_IN_UNITS]
        load_unit(sp, t, U_ODD + u, src, ODD_W[u])


ODD_BANKS = (3, 4)


def odd_tensor(pe, t, x_ready):
    o = t.odd

    for u in range(V_UNITS):
        n, part = divmod(u, 4)
        split_ready(pe, t, U_ODD + u)
        s = (U_ODD + u) % SPLIT
        if n == 2 and part == 0:
            pe.wait_ge(o.evac, TT)
        for kk in range(2):
            k = 2 * part + kk
            if n == 0:
                pe.wait_ge(x_ready, k + 1)
            for i in range(TT):
                b, tok = slice(kk * 512, kk * 512 + 512), slice(i * P, i * P + P)
                last = product3(pe, t.bank[4 * (n % 2) + i][:, :], t.xh[:, k, tok], t.xl[:, k, tok],
                                t.whi[:, s, b], t.wlo[:, s, b], k == 0, k == KD - 1)
        last.then_inc(t.units_used, 1)

    def unit(u):
        split_ready(pe, t, U_ODD + V_UNITS + u)
        s = (U_ODD + V_UNITS + u) % SPLIT
        bank = t.bank[ODD_BANKS[u % 2]]
        pe.wait_ge(o.evac, DG * TT + max(u - 1, 0))
        for k in range(KD):
            b = slice(k * P, k * P + P)
            last = product3(pe, bank[:, :], t.whi[:, s, b], t.wlo[:, s, b], t.xh[:, k, :],
                            t.xl[:, k, :], k == 0, k == KD - 1)
        last.then_inc(t.units_used, 1)

    def between(n):
        for u in odd_units_after(n):
            unit(u)
        if n % TT == TT - 1 and n + 1 < len(o.items):
            pe.wait_ge(o.evac, DG * TT + HEAD_UNITS * (n // TT + 2))

    for u in range(HEAD_UNITS):
        unit(u)
    pe.wait_ge(o.evac, DG * TT + HEAD_UNITS)
    odd_attention_tensor(pe, o, o.items, between)
    pe.sem_inc(t.z_done[4], 2)
    for v in range(KD // 2):
        u = ODD_IN_UNITS + v
        split_ready(pe, t, U_ODD + u)
        s = (U_ODD + u) % SPLIT
        for half in range(2):
            b = slice(half * 4 * P, (half + 1) * 4 * P)
            last = out_proj_tile(pe, t, 4, 2 * v + half, t.whi[:, s, b], t.wlo[:, s, b], o.oh, o.ol,
                                 DHEADS, (o.o_ready, DHEADS))
            last.then_inc(t.units_used if half else o.half_done, 1)


def odd_attention_tensor(pe, a, items, between):
    scores_tensor(pe, a, items[0])
    for it in items:
        between(it.n)
        for c in range(len(it.chunks)):
            turn_tensor(pe, a, it, c)
            if c:
                values_tensor(pe, a, it, c - 1)
        if it.n + 1 < len(items):
            scores_tensor(pe, a, items[it.n + 1])
        values_tensor(pe, a, it, len(it.chunks) - 1)


def odd_vector(dve, t):
    o = t.odd
    for u in range(V_UNITS):
        split_lo(dve, t, U_ODD + u + LEAD)
        if u % 4 == 3:
            used(dve, t, U_ODD + u)
            for i in range(TT):
                dve.tensor_copy(o.v[:, i, u // 4, :], t.bank[4 * (u // 4 % 2) + i][:, :]).then_inc(o.evac, 1)

    def unit(u):
        split_lo(dve, t, U_ODD + V_UNITS + u + LEAD)
        hp, r = divmod(u, HEAD_UNITS)
        kind, grp = divmod(r, DG)
        bank, side = t.bank[ODD_BANKS[u % 2]], hp % 2
        if hp >= 2 and r == 0:
            dve.wait_ge(o.values_done, o.items[TT * (hp - 1) - 1].chunks[-1][0] + 1)
        used(dve, t, U_ODD + V_UNITS + u)
        if kind == 0:
            last = dve.tensor_scalar(o.q[:, side, grp, :], bank[:, :], DIL_SCALE, None, ALU.mult)
        else:
            last = dve.tensor_copy(o.k[:, side, grp, :], bank[:, :])
        last.then_inc(o.evac, 1)

    for u in range(HEAD_UNITS):
        unit(u)

    def between(n):
        for u in odd_units_after(n):
            unit(u)

    dve.wait_ge(t.dist_step, (4 + 2 * DG) * TT)
    attention_vector(dve, o, o.items, 0, between)
    for v in range(KD // 2):
        split_lo(dve, t, U_ODD + ODD_IN_UNITS + v + LEAD)
        dve.wait_ge(o.half_done, v + 1)
        mixer_residual(dve, t, 4, 2 * v)
        used(dve, t, U_ODD + ODD_IN_UNITS + v)
        mixer_residual(dve, t, 4, 2 * v + 1)


def odd_scalar(act, t):
    o = t.odd
    for u in range(V_UNITS + HEAD_UNITS):
        split_hi(act, t, U_ODD + u + LEAD)

    def between(n):
        for u in odd_units_after(n):
            split_hi(act, t, U_ODD + V_UNITS + u + LEAD)

    attention_scalar(act, o, o.items, between)
    for v in range(KD // 2):
        split_hi(act, t, U_ODD + ODD_IN_UNITS + v + LEAD)


def odd_keys(g, i):
    first = max(i * P - DIL[g][0], 0)
    return first, (i + 1) * P - first


def odd_gpsimd(g, t):
    o = t.odd
    for n in range(DG):
        distances_gpsimd(g, t, o.dist[n], (t.masks_in[1], 48), lambda i: odd_keys(n, i)[1],
                         lambda i: t.pos_k[:, odd_keys(n, i)[0]:(i + 1) * P])
    attention_gpsimd(g, o, o.items)


def odd_items(t):
    o = t.odd
    raw = []
    for hp in range(DHEADS):
        for i in range(TT):
            runs, blocks, side = [], [], hp % 2
            for n in range(DG):
                first, w = odd_keys(n, i)
                runs.append((o.q[:, side, n, i * P:i * P + P], o.k[:, side, n, first:first + w], o.dist[n][:, i, 0:w],
                             -DIL_SLOPES[n * DHEADS + hp], w))
                blocks += [(P, o.v[:, j, n, hp * P:hp * P + P]) for j in range(first // P, i + 1)]
            raw.append(dict(runs=runs,
                            blocks=blocks, place=(hp, 0, P, i), first=True, last=True,
                            fill_end=hp if i == TT - 1 else None))
    return plan_items(raw)


def start_vector(dve, t):
    c, ang, turns = t.setup, t.lnbuf[0], t.lnbuf[1]
    dve.wait_ge(t.consts_in, t.n_consts)

    def step(n, ins):
        ins.then_inc(c, 1)
        dve.wait_ge(c, n)

    step(1, dve.tensor_scalar(t.neg_pos_q[:, :], t.pos_qi[:, :], -1.0, None, ALU.mult))
    step(2, dve.tensor_copy(t.pos_k[:, :], t.pos_ki[:, :]))
    step(3, dve.tensor_scalar(ang[:, :], t.pos_k[:, :], t.cst[:, C_FREQ:C_FREQ + 1], None, ALU.mult))
    step(4, dve.tensor_scalar(turns[:, :], ang[:, :], 1 / (2 * np.pi), t.cst[:, C_TURN:C_TURN + 1],
                              ALU.mult, ALU.add))
    step(5, dve.tensor_scalar(turns[:, :], turns[:, :], MAGIC, MAGIC, ALU.add, ALU.subtract))
    for n, part in enumerate((PI2_A, PI2_B, PI2_C)):
        step(6 + n, dve.scalar_tensor_tensor(ang[:, :], turns[:, :], -part, ang[:, :], ALU.mult, ALU.add))
    step(9, dve.tensor_scalar(ang[:, :], ang[:, :], t.cst[:, C_PHASE:C_PHASE + 1], PI_SAFE,
                              ALU.add, ALU.min))
    step(10, dve.tensor_scalar(ang[:, :], ang[:, :], -PI_SAFE, None, ALU.max))
    dve.wait_ge(t.sin_done, 1)
    step(11, dve.tensor_scalar(t.rope_q[:, :], t.rope_k[:, :], MLA_SCALE, None, ALU.mult))


def start_scalar(act, t):
    act.wait_ge(t.setup, 10)
    act.activation(t.rope_k[:, :], t.lnbuf[0][:, :], ACT.Sin).then_inc(t.sin_done, 1)


def input_hi(act, t):
    for k in range(KD):
        act.wait_ge(t.x_in[k], 16)
        act.activation(t.xh[:, k, :], t.xt[:, k, :], ACT.Copy).then_inc(t.in_hi, 1)


def input_lo(g, t):
    for k in range(KD):
        g.wait_ge(t.in_hi, k + 1)
        g.tensor_tensor(t.xl[:, k, :], t.xt[:, k, :], t.xh[:, k, :].bitcast(F32),
                        ALU.subtract).then_inc(t.in_ready, 1)


def trunk(nc, d, out):
    t = Store()
    t.n_dist = 0
    t.x_t, t.w_gate, t.w_up, t.w_down = d["x_t"], d["w_gate"], d["w_up"], d["w_down"]
    t.ev_in, t.ev_vg, t.ev_w1, t.ev_uk, t.ev_uv = (d[n] for n in (
        "ev_in", "ev_vg", "ev_w1", "ev_uk", "ev_uv"))
    t.ev_uq, t.ev_out = d["ev_uq"], d["ev_out"]
    t.od_v, t.od_qk, t.od_out = d["od_v"], d["od_qk"], d["od_out"]
    t.tri_mask, t.causal_mask, t.cmp_mask, t.dil_mask = (d[n] for n in (
        "tri_mask", "causal_mask", "cmp_mask", "dil_mask"))
    with ExitStack() as ctx:
        def sb(name, shape, dtype=F32, scope=ctx):
            return scope.enter_context(nc.sbuf_tensor(name, shape, dtype))

        def sem(name):
            return ctx.enter_context(nc.semaphore(name))

        def sems(name, n):
            return [sem(f"{name}_{i}") for i in range(n)]

        t.xt = sb("xt", [P, KD, SEQ])
        t.xh = sb("xh", [P, KD, SEQ], F32R)
        t.xl = sb("xl", [P, KD, SEQ], F32R)
        t.raw = sb("raw", [P, RAW, UNIT])
        t.whi = sb("whi", [P, SPLIT, UNIT], F32R)
        t.wlo = sb("wlo", [P, SPLIT, UNIT], F32R)
        t.rope_k = sb("rope_k", [P, SEQ])
        t.rope_q = sb("rope_q", [P, SEQ])
        t.pos_k = sb("pos_k", [P, SEQ])
        t.neg_pos_q = sb("neg_pos_q", [P, TT])
        t.dist = sb("dist", [P, SEQ])
        t.pos_ki = t.dist[:, :].bitcast(I32)
        t.pos_qi = sb("pos_qi", [P, TT], I32)
        t.zsum, t.qsum, t.sq = t.lnbuf = [sb(n, [P, SEQ]) for n in ("zsum", "qsum", "sq")]
        t.norm_tmp = (t.dist, t.qsum)
        t.zsum3, t.qsum3, t.sq3 = (b[:, :].rearrange("p (a n) -> p a n", a=1) for b in t.lnbuf)
        t.ident = sb("ident", [P, P])
        t.ones = sb("ones", [P, P])
        t.ones_kv = sb("ones_kv", [P, P])
        t.ones_q = sb("ones_q", [P, P])
        t.gains = sb("gains", [P, 6, DEPTH, KD])
        t.rms_g = sb("rms_g", [P, KV + KQ])
        t.w2k = sb("w2k", [P, 2, P])
        t.w2v = sb("w2v", [P, 2, DH])
        t.cmp_pos = sb("cmp_pos", [P, CMP_K])
        t.cst = sb("cst", [P, 5])
        t.cmp_valid = sb("cmp_valid", [P, 1])
        t.stats = sb("stats", [P, 2 * TT])
        t.part_stats = sb("part_stats", [P, 2 * TT])
        t.mu2, t.var, t.std, t.rstd, t.nmr = (sb(n, [P, TT]) for n in ("mu2", "var", "std", "rstd", "nmr"))
        small = [(t.cst[:, :], d["c_cst"]), (t.pos_qi[:, :], d["c_pos_q"]), (t.pos_ki, d["c_pos_k"]),
                 (t.ident[:, :], d["c_ident"]), (t.gains[:, :, :, :], d["c_gains"]),
                 (t.ones[:, :], d["c_ones"]), (t.ones_kv[:, :], d["c_ones_kv"]), (t.ones_q[:, :], d["c_ones_q"]),
                 (t.rms_g[:, :], d["c_rms_g"]), (t.w2k[:, :, :], d["c_w2k"]),
                 (t.w2v[:, :, :], d["c_w2v"]), (t.cmp_pos[:, :], d["c_cmp_pos"]),
                 (t.cmp_valid[:, :], d["c_cmp_valid"])]
        t.n_consts = 16 * len(small)

        with ExitStack() as scope:
            t.hh = sb("hh", [P, KF, SEQ], F32R, scope)
            t.hl = sb("hl", [P, KF, SEQ], F32R, scope)
            t.sg = sb("sg", [P, 2, SEQ], F32, scope)
            t.hf = sb("hf", [P, 2, SEQ], F32, scope)
        e = t.even = Store()
        e.n_rope, e.ident = 0, t.ident
        e.lead, e.slots, e.copy_lag, e.out_lag = 5, 7, 3, 6
        with ExitStack() as scope:
            e.vm = sb("e_vm", [P, TT, H * DH], F32, scope)
            e.qn = sb("e_qn", [P, 4, SEQ], F32, scope)
            e.kn = sb("e_kn", [P, 2, SEQ], F32, scope)
            e.vn = sb("e_vn", [P, 2, TT, P], F32, scope)
            e.dist = sb("e_dist", [P, TT, SEQ], F32, scope)
            e.distc = sb("e_distc", [P, TT, NC], F32, scope)
            e.mask = sb("e_mask", [P, SEQ], F32, scope)
            e.kc = sb("e_kc", [P, NB], F32, scope)
            e.vc = sb("e_vc", [P, 2 * DH], F32, scope)
            e.gate = sb("e_gate", [P, TT * 24], F32, scope)
            e.gel = sb("e_gel", [P, 2, 2, NB], F32, scope)
            e.krot = sb("e_krot", [P, SEQ], F32, scope)
            e.ra = sb("e_ra", [P, SEQ], F32, scope)
            e.rb = sb("e_rb", [P, SEQ], F32, scope)
            e.nmax, e.den, e.inv = (sb(n, [P, e.slots], F32, scope) for n in ("e_nmax", "e_den", "e_inv"))
            with ExitStack() as part:
                e.x = sb("e_x", [P, 2, 2, SEQ], F32, part)
                e.bf = sb("e_bf", [P, 2, CMP_K, NB], F32, part)
                e.bh = sb("e_bh", [P, 2, CMP_K, NB], F32R, part)
                e.bl = sb("e_bl", [P, 2, CMP_K, NB], F32R, part)
            e.qt = sb("e_qt", [P, H, SEQ], F32, scope)
            e.kt = sb("e_kt", [P, H, SEQ], F32, scope)
            with ExitStack() as part:
                e.craw = sb("e_craw", [P, KV + KQ, SEQ], F32, part)
                e.ch = sb("e_ch", [P, KV + KQ, SEQ], F32R, part)
                e.cl = sb("e_cl", [P, KV + KQ, SEQ], F32R, part)
                e.rs = sb("e_rs", [P, 2, SEQ], F32, part)
            e.s = sb("e_s", [P, e.slots, SEQ], F32, scope)
            e.pt = sb("e_pt", [P, PT_SLOTS, 4 * P], F32, scope)
        e.oh, e.ol = t.xh, t.xl
        e.ktile = [4, 5, 6, 7, 0, 1, 2, 3]
        o = t.odd = Store()
        o.ident, o.slots, o.copy_lag, o.out_lag = t.ident, 3, 0, 0
        with ExitStack() as scope:
            o.q = sb("o_q", [P, 2, DG, SEQ], F32, scope)
            o.k = sb("o_k", [P, 2, DG, SEQ], F32, scope)
            o.v = sb("o_v", [P, TT, DG, DHEADS * P], F32, scope)
            o.dist = [sb(f"o_dist{n}", [P, TT, 2 * P if n == 0 else SEQ], F32, scope) for n in range(DG)]
            o.s = sb("o_s", [P, o.slots, 10 * P], F32, scope)
            o.pt = sb("o_pt", [P, PT_SLOTS, 4 * P], F32, scope)
            o.oh = sb("o_oh", [P, DHEADS, SEQ], F32R, scope)
            o.ol = sb("o_ol", [P, DHEADS, SEQ], F32R, scope)
            o.nmax, o.den, o.inv = (sb(n, [P, o.slots], F32, scope) for n in ("o_nmax", "o_den", "o_inv"))
        o.ktile = [0, 1, 2, 3]

        t.bank = [ctx.enter_context(nc.psum_tensor(f"bank{i}", [P, 512], F32)) for i in range(8)]
        e.score, e.turn, e.obank = t.bank[0:4], t.bank[4:6], t.bank[6:8]
        o.score, o.obank, o.turn = t.bank[0:3], t.bank[5:6], t.bank[6:8]

        t.consts_in, t.out_stored = sem("consts_in"), sem("out_stored")
        t.setup, t.sin_done, t.in_hi, t.in_ready = (sem(n) for n in ("setup", "sin_done", "in_hi", "in_ready"))
        t.units_hi, t.units_split, t.units_used = (sem(n) for n in ("units_hi", "units_split", "units_used"))
        t.dist_step = sem("dist_step")
        t.x_in, t.raw_landed, t.masks_in = sems("x_in", KD), sems("raw_landed", RAW), sems("masks_in", 2)
        t.h_mul, t.h_hi, t.h_ready, t.silu_done = (sems(n, 4) for n in ("h_mul", "h_hi", "h_ready", "silu_done"))
        t.z_done, t.acc = (sems(n, 6) for n in ("z_done", "acc"))
        t.x_hi, t.x_ready = (sems(n, 6) for n in ("x_hi", "x_ready"))
        t.col_sums, t.col, t.std_done, t.last_sq, t.diag, t.maps = (sem(n) for n in (
            "col_sums", "col", "std_done", "last_sq", "diag", "maps"))
        t.norm_a, t.norm_b, t.norm_c = (sem(n) for n in ("norm_a", "norm_b", "norm_c"))
        for a, name in ((e, "e"), (o, "o")):
            a.scores_ready, a.scores_read = sem(name + "_scores_ready"), sem(name + "_scores_read")
            a.max_ready, a.exp_done, a.inv_ready, a.probs_ready = (sem(f"{name}_{n}") for n in (
                "max_ready", "exp_done", "inv_ready", "probs_ready"))
            a.turned, a.pt_ready, a.values_done = (sem(f"{name}_{n}") for n in ("turned", "pt_ready", "values_done"))
            a.o_hi, a.o_ready, a.evac = (sem(f"{name}_{n}") for n in ("o_hi", "o_ready", "evac"))
        e.tile_done, e.squared, e.rms_sum, e.rms_std, e.rms_inv = (sem("e_" + n) for n in (
            "tile_done", "squared", "rms_sum", "rms_std", "rms_inv"))
        e.c_full, e.c_hi, e.c_lo, e.b_full, e.b_hi, e.b_lo = (sem("e_" + n) for n in (
            "c_full", "c_hi", "c_lo", "b_full", "b_hi", "b_lo"))
        e.gelu, e.gate_exp, e.gate_step, e.rope, e.k_rot = (sem("e_" + n) for n in (
            "gelu", "gate_exp", "gate_step", "rope", "k_rot"))
        o.half_done = sem("o_half_done")
        e.items, o.items = even_items(t), odd_items(t)

        block = ctx.enter_context(nc.Block())

        @block.sync
        def _(sp):
            ffn_sync(sp, t, 0)
            even_sync(sp, t)
            ffn_sync(sp, t, 1)
            ffn_sync(sp, t, 2)
            odd_sync(sp, t)
            ffn_sync(sp, t, 3)
            for k in range(KD):
                sp.wait_ge(t.norm_c, KD * 5 + k + 1)
                sp.dma_start(out[k], t.xt[:, k, :]).then_inc(t.out_stored, 16)
            sp.wait_ge(t.out_stored, 16 * KD)

        @block.tensor
        def _(pe):
            pe.sem_inc(t.units_used, SPLIT)
            ffn_tensor(pe, t, 0, t.in_ready)
            norm_tensor(pe, t, 0)
            even_tensor(pe, t, t.x_ready[0])
            norm_tensor(pe, t, 1)
            ffn_tensor(pe, t, 1, t.x_ready[1])
            norm_tensor(pe, t, 2)
            ffn_tensor(pe, t, 2, t.x_ready[2])
            norm_tensor(pe, t, 3)
            odd_tensor(pe, t, t.x_ready[3])
            norm_tensor(pe, t, 4)
            ffn_tensor(pe, t, 3, t.x_ready[4])
            norm_tensor(pe, t, 5)

        @block.scalar
        def _(act):
            for k in range(KD):
                act.dma_start(t.xt[:, k, :], t.x_t[k]).then_inc(t.x_in[k], 16)
            for u in range(LEAD):
                split_hi(act, t, u)
            input_hi(act, t)
            start_scalar(act, t)
            ffn_scalar(act, t, 0)
            norm_scalar(act, t, 0)
            even_scalar(act, t)
            norm_scalar(act, t, 1)
            ffn_scalar(act, t, 1)
            norm_scalar(act, t, 2)
            ffn_scalar(act, t, 2)
            norm_scalar(act, t, 3)
            odd_scalar(act, t)
            norm_scalar(act, t, 4)
            ffn_scalar(act, t, 3)
            norm_scalar(act, t, 5)

        @block.vector
        def _(dve):
            dve.sem_inc(t.units_split, RAW)
            for u in range(LEAD):
                split_lo(dve, t, u)
            start_vector(dve, t)
            ffn_vector(dve, t, 0)
            norm_vector(dve, t, 0)
            even_vector(dve, t)
            norm_vector(dve, t, 1)
            ffn_vector(dve, t, 1)
            norm_vector(dve, t, 2)
            ffn_vector(dve, t, 2)
            norm_vector(dve, t, 3)
            odd_vector(dve, t)
            norm_vector(dve, t, 4)
            ffn_vector(dve, t, 3)
            norm_vector(dve, t, 5)

        @block.gpsimd
        def _(g):
            for dst, src in small:
                g.dma_start(dst, src).then_inc(t.consts_in, 16)
            input_lo(g, t)
            g.wait_ge(t.setup, 11)
            sums_gpsimd(g, t, 0)
            norm_gpsimd(g, t, 0)
            even_gpsimd(g, t)
            sums_gpsimd(g, t, 1)
            norm_gpsimd(g, t, 1)
            sums_gpsimd(g, t, 2)
            norm_gpsimd(g, t, 2)
            sums_gpsimd(g, t, 3)
            norm_gpsimd(g, t, 3)
            odd_gpsimd(g, t)
            sums_gpsimd(g, t, 4)
            norm_gpsimd(g, t, 4)
            sums_gpsimd(g, t, 5)


def constants():
    q, k = np.arange(SEQ)[:, None], np.arange(SEQ)[None, :]
    by_tile = lambda m: np.ascontiguousarray(
        np.where(m, 0.0, BIG).astype(np.float32).reshape(TT, P, -1).transpose(1, 0, 2))
    tri = np.zeros((P, SEQ), np.float32)
    tri[:, SEQ - P:] = np.where(np.arange(P)[:, None] >= np.arange(P)[None, :], 0.0, BIG)
    win = np.zeros((P, TT, 2 * P), np.float32)
    full = by_tile((q >= k) & (q - k <= DIL[0][0]))
    for i in range(TT):
        first, w = odd_keys(0, i)
        win[:, i, :w] = full[:, i, first:first + w]
    half = ROPE // 2
    freq = (10000.0 ** (-np.arange(half, dtype=np.float32) / half)).astype(np.float32)
    cst = np.zeros((P, 5), np.float32)
    cst[:, C_INVD] = 1 / D_MODEL
    cst[:, C_RMS_EPS] = RMS_EPS
    cst[:, C_FREQ] = np.tile(freq, P // half)
    turn = np.zeros(P)
    turn[64:96], turn[96:112] = 0.25, 0.5
    cst[:, C_TURN] = turn
    cst[:, C_PHASE] = 2 * np.pi * turn
    return {
        "c_cst": cst, "c_ident": np.eye(P, dtype=np.float32),
        "c_ones": np.ones((P, P), np.float32),
        "c_ones_kv": np.full((P, P), 1 / KV_RANK, np.float32),
        "c_ones_q": np.full((P, P), 1 / Q_RANK, np.float32),
        "c_cmp_valid": (np.arange(P) >= 31).astype(np.float32)[:, None],
        "tri_mask": tri, "causal_mask": by_tile(q >= k),
        "cmp_mask": by_tile(16 * np.arange(NC)[None, :] + 31 <= q),
        "dil_mask0": win, "dil_mask1": by_tile((q >= k) & ((q - k) % DIL[1][1] == 0)),
        "dil_mask2": by_tile((q >= k) & ((q - k) % DIL[2][1] == 0)),
    }


def blocks(w):
    k, m = w.shape
    return np.ascontiguousarray(w.reshape(k // P, P, m // P, P).transpose(2, 1, 0, 3)).reshape(m // P, P, -1)


def rows(w):
    k, m = w.shape
    return np.ascontiguousarray(w.reshape(k // P, P, m).transpose(1, 0, 2)).reshape(P, -1)


def layouts(inp):
    a = {}
    a["x_t"] = np.ascontiguousarray(inp["x"][0].T).reshape(KD, P, SEQ)
    pos = inp["positions"][0]
    a["c_pos_k"] = np.ascontiguousarray(np.broadcast_to(pos, (P, SEQ)))
    a["c_pos_q"] = np.ascontiguousarray(pos.reshape(TT, P).T)
    norms = [inp[f"ln{n}_{c}"] for n in (1, 2, 3) for c in "gb"]
    a["c_gains"] = np.ascontiguousarray(np.stack(norms).reshape(6, DEPTH, KD, P).transpose(3, 0, 1, 2))
    for f in range(4):
        n, layer = 1 + f % 2, f // 2
        a[f"w_gate{f}"] = blocks(inp[f"ffn{n}_w_gate"][layer])
        a[f"w_up{f}"] = blocks(inp[f"ffn{n}_w_up"][layer])
        a[f"w_down{f}"] = blocks(inp[f"ffn{n}_w_down"][layer])
    w = inp["mix_in_even"][0]
    cut = np.split(w, np.cumsum([Q_RANK, KV_RANK, ROPE, H * DH] + [2 * DH] * 6), axis=1)
    c_q, c_kv, k_pe, q, k_c, v_c, k_s, v_s, k_w, v_w, gate = cut
    half = ROPE // 2
    swap = lambda m: np.concatenate([m[:, half:], m[:, :half]], axis=1)
    tiles = [c_kv, c_q, np.concatenate([k_pe, swap(k_pe)] * 2, axis=1)]
    tiles += [np.concatenate([m[:, s:s + DH]] * 2, axis=1) for m in (k_c, v_c) for s in (0, DH)]
    tiles += [k_s, k_w]
    tiles += [np.concatenate([q[:, m * DH:m * DH + DH], q[:, (4 + m) * DH:(5 + m) * DH]], axis=1)
              for m in range(4)]
    a["ev_in"] = blocks(np.concatenate(tiles, axis=1))
    a["ev_vg"] = rows(np.concatenate([v_s, v_w, gate], axis=1))
    w1 = []
    for kind in "kv":
        w1 += list(blocks(inp[f"nsa_cmp_{kind}_w1"][0]).reshape(2, P, 2, UNIT).transpose(0, 2, 1, 3).reshape(4, P, UNIT))
    a["ev_w1"] = np.ascontiguousarray(np.stack(w1))
    w2k, w2v = inp["nsa_cmp_k_w2"][0], inp["nsa_cmp_v_w2"][0]
    a["c_w2k"] = rows(np.concatenate([w2k, w2k], axis=1)).reshape(P, 2, P)
    a["c_w2v"] = rows(w2v).reshape(P, 2, DH)
    a["c_cmp_pos"] = np.ascontiguousarray(inp["nsa_cmp_pos"][0].reshape(CMP_K, P).T)
    a["ev_uk"], a["ev_uv"] = rows(inp["mla_w_uk"][0]), rows(inp["mla_w_uv"][0])
    uq = inp["mla_w_uq"][0].reshape(Q_RANK, H, NOPE + ROPE)
    uq = np.concatenate([uq, uq[..., NOPE + half:], uq[..., NOPE:NOPE + half]], axis=2)
    a["ev_uq"] = np.ascontiguousarray(blocks(uq.reshape(Q_RANK, H * P)).reshape(UQ_UNITS, 2, P, -1)
                                      .transpose(0, 2, 1, 3)).reshape(UQ_UNITS, P, -1)
    a["c_rms_g"] = np.ascontiguousarray(np.concatenate([inp["mla_kv_norm"][0], inp["mla_q_norm"][0]])
                                        .reshape(KV + KQ, P).T)
    a["ev_out"] = blocks(inp["mix_out_even"][0])
    od = inp["mix_in_odd"][0].reshape(D_MODEL, 3, DG, DHEADS, P)
    a["od_qk"] = blocks(od[:, :2].transpose(0, 3, 1, 2, 4).reshape(D_MODEL, -1))
    a["od_v"] = np.ascontiguousarray(od[:, 2].reshape(4, 2, P, DG, DHEADS * P).transpose(3, 0, 2, 1, 4)
                                     ).reshape(V_UNITS, P, 2 * DHEADS * P)
    a["od_out"] = np.ascontiguousarray(blocks(inp["mix_out_odd"][0]).reshape(KD // 2, 2, P, -1)
                                       .transpose(0, 2, 1, 3)).reshape(KD // 2, P, -1)
    return a


def build(nc, arrays):
    d = {n: nc.dram_tensor(n, a.shape, mybir.dt.from_np(a.dtype), kind="ExternalInput").ap()
         for n, a in arrays.items()}
    for n in ("w_gate", "w_up", "w_down"):
        d[n] = [d[f"{n}{f}"] for f in range(4)]
    d["dil_mask"] = [d[f"dil_mask{n}"] for n in range(DG)]
    out = nc.dram_tensor("out_t", (KD, P, SEQ), F32, kind="ExternalOutput").ap()
    trunk(nc, d, out)


def kernel(**inputs):
    import concourse.bacc as bacc
    from concourse.bass_utils import run_bass_kernel_spmd

    arrays = {**layouts({n: np.asarray(v) for n, v in inputs.items()}), **constants()}
    nc = bacc.Bacc("TRN2", target_bir_lowering=False, num_devices=1)
    build(nc, arrays)
    r = run_bass_kernel_spmd(nc, [arrays], core_ids=[0])
    out = np.asarray(r.results[0]["out_t"]).reshape(D_MODEL, SEQ)
    return np.ascontiguousarray(out.T)[None]
```

```python
from contextlib import ExitStack

import numpy as np

import concourse.bass as bass
from concourse import mybir

F32 = mybir.dt.float32
F32R = mybir.dt.float32r
I32 = mybir.dt.int32
ACT = mybir.ActivationFunctionType
ALU = mybir.AluOpType
AX = mybir.AxisListType

P = 128
D_MODEL, SEQ, DEPTH, D_FF = 1024, 512, 2, 2816
KD = D_MODEL // P
KF = D_FF // P
TT = SEQ // P
ALPHA = (2 * DEPTH) ** 0.25
LN_EPS, RMS_EPS = 1e-5, 1e-6
BIG = 1e30

H = 8
Q_RANK, KV_RANK, NOPE, ROPE = 384, 256, 64, 32
KQ, KV = Q_RANK // P, KV_RANK // P
MLA_SCALE = (NOPE + ROPE) ** -0.5
DH = 64
NSA_SCALE = DH ** -0.5
NC = SEQ // 16 - 1
CMP_K = 16
NB = 2 * NC
DIL = ((128, 1), (512, 4), (2048, 16))
DG, DHEADS = 3, 4
DIL_SCALE = P ** -0.5
NSA_SLOPES = [2.0 ** (-8.0 * (n + 1) / H) for n in range(H)]
DIL_SLOPES = [2.0 ** (-8.0 * (n + 1) / (DG * DHEADS)) for n in range(DG * DHEADS)]

C_INVD, C_RMS_EPS, C_FREQ, C_TURN, C_PHASE, C_QN = range(6)
N_CST = C_QN + H // 2
MAGIC = 1.5 * 2.0 ** 23
PI2_A = 6.28125
PI2_B = float(np.float32(2 * np.pi - PI2_A) // 2.0 ** -20 * 2.0 ** -20)
PI2_C = float(2 * np.pi - PI2_A - PI2_B)
PI_SAFE = float(np.nextafter(np.float32(np.pi), np.float32(0)))



class Store:
    pass


RAW, SPLIT = 4, 2
UNIT = KD * P
LEAD = SPLIT

EVEN_IN_UNITS, EVEN_CMP_UNITS, UQ_UNITS = 19, 8, 4
EVEN_UNITS = EVEN_IN_UNITS + EVEN_CMP_UNITS + 2 + UQ_UNITS + KD
ODD_IN_UNITS = 3 * DG * DHEADS
ODD_OUT_UNITS = KD // 2 + 1
ODD_UNITS = ODD_IN_UNITS + ODD_OUT_UNITS
DN_BLOCKS = (8, 7, 7)
DN_STARTS = (0, 8, 15)
FFN_W = [KD * P] * (2 * KF) + [b * P for b in DN_BLOCKS] * KD
VG = 2 * 2 * DH + 24
VG_TILES = ((0, 3), (3, 6), (6, 8))
EVEN_W = ([KD * P] * 16 + [(b - a) * VG for a, b in VG_TILES] + [KD * P] * EVEN_CMP_UNITS + [KV * 512] * 2
          + [2 * KQ * P] * UQ_UNITS + [KD * P] * KD)
ODD_W = [KD * P] * ODD_IN_UNITS + [2 * (DHEADS - 1) * P] * (KD // 2) + [KD * P]
WIDTH = FFN_W + EVEN_W + FFN_W + FFN_W + ODD_W + FFN_W
U_FFN = [0, len(FFN_W) + EVEN_UNITS, 2 * len(FFN_W) + EVEN_UNITS,
         3 * len(FFN_W) + EVEN_UNITS + ODD_UNITS]
U_EVEN = len(FFN_W)
U_ODD = 3 * len(FFN_W) + EVEN_UNITS
N_UNITS = len(WIDTH)
LN_OF_FFN = (0, 2, 3, 5)
GU_STEPS = KF // 2
DN_STEPS = 2
DN_UNITS = 12


def load_unit(sp, t, u, src, width, d=0):
    sp.wait_ge(t.units_split, d + (u + 1))
    sp.dma_start(t.raw[:, u % RAW, :width], src).then_inc(t.raw_landed[u % RAW], 16)


def split_hi(act, t, u, d=0):
    if u >= N_UNITS:
        return
    act.wait_ge(t.raw_landed[u % RAW], d * (16 // RAW) + 16 * (u // RAW + 1))
    act.wait_ge(t.units_used, d + (u + 1))
    act.activation(t.whi[:, u % SPLIT, :WIDTH[u]], t.raw[:, u % RAW, :WIDTH[u]],
                   ACT.Copy).then_inc(t.units_hi, 1)


def split_lo(dve, t, u, d=0):
    if u >= N_UNITS:
        return
    dve.wait_ge(t.units_hi, d + (u + 1))
    dve.tensor_tensor(t.wlo[:, u % SPLIT, :WIDTH[u]], t.raw[:, u % RAW, :WIDTH[u]],
                      t.whi[:, u % SPLIT, :WIDTH[u]].bitcast(F32), ALU.subtract
                      ).then_inc(t.units_split, 1)


def split_ready(pe, t, u, d=0):
    pe.wait_ge(t.units_split, d + (RAW + u + 1))


def used(eng, t, u, d=0):
    eng.wait_ge(t.units_used, d + (SPLIT + u + 1))


def product3(pe, out, wh, wl, xh, xl, start, stop):
    pe.matmul(out, wl, xh, start=start, stop=False)
    pe.matmul(out, wh, xl, start=False, stop=False)
    return pe.matmul(out, wh, xh, start=False, stop=stop)


def ffn_sync(sp, t, f):
    u0 = U_FFN[f]

    def gate_up(i):
        for j in range(4):
            w = (t.w_gate, t.w_up)[j % 2][f]
            load_unit(sp, t, u0 + j, w[bass.ds(2 * i + j // 2, 1)].rearrange("a p n -> p (a n)"),
                      UNIT, 4 * i)

    gate_up(0)
    if f == 0:
        for dst, src in t.small:
            sp.dma_start(dst, src).then_inc(t.consts_in, 16)
    with sp.Fori(1, GU_STEPS) as i:
        gate_up(i)
    with sp.Fori(0, DN_STEPS) as i:
        for j in range(DN_UNITS):
            m, part = divmod(j, 3)
            row = t.w_down[f][bass.ds(4 * i + m, 1)].rearrange("a p n -> p (a n)")
            at, w = DN_STARTS[part] * P, DN_BLOCKS[part] * P
            load_unit(sp, t, u0 + 2 * KF + j, row[:, at:at + w], w, DN_UNITS * i)


def first_pair(pe, t, u0, banks, x_ready):
    split_ready(pe, t, u0 + 1)
    for k in range(KD):
        pe.wait_ge(x_ready, k + 1)
        b = slice(k * P, k * P + P)
        for j in range(2):
            s = (u0 + j) % SPLIT
            last = product3(pe, banks[j][:, :], t.whi[:, s, b], t.wlo[:, s, b],
                            t.xh[:, k, :], t.xl[:, k, :], k == 0, k == KD - 1)
            if k == KD - 1:
                last.then_inc(t.units_used, 1)


def ffn_tensor(pe, t, f, x_ready):
    u0, ln = U_FFN[f], LN_OF_FFN[f]
    pe.sem_inc(t.h_mul[f], 2)
    pe.sem_inc(t.z_done[ln], 2)
    def gate_up(j, i):
        split_ready(pe, t, u0 + j, 4 * i)
        if j % 2 == 0:
            pe.wait_ge(t.h_mul[f], 2 * i + (j // 2 + 1))
        for k in range(KD):
            b = slice(k * P, k * P + P)
            s = (u0 + j) % SPLIT
            last = product3(pe, t.bank[j][:, :], t.whi[:, s, b], t.wlo[:, s, b],
                            t.xh[:, k, :], t.xl[:, k, :], k == 0, k == KD - 1)
        last.then_inc(t.units_used, 1)

    first_pair(pe, t, u0, t.bank[0:2], x_ready)
    gate_up(2, 0)
    gate_up(3, 0)
    with pe.Fori(1, GU_STEPS) as i:
        for j in range(4):
            gate_up(j, i)
    u1 = u0 + 2 * KF
    with pe.Fori(0, DN_STEPS) as i:
        for j in range(DN_UNITS):
            m, part = divmod(j, 3)
            split_ready(pe, t, u1 + j, DN_UNITS * i)
            if part == 0:
                pe.wait_ge(t.z_done[ln], 4 * i + (m + 1))
            for kk in range(DN_BLOCKS[part]):
                k = DN_STARTS[part] + kk
                if m == 0:
                    pe.wait_ge(t.h_ready[f], k + 1)
                b = slice(kk * P, kk * P + P)
                s = (u1 + j) % SPLIT
                last = product3(pe, t.bank[4 + m % 2][:, :], t.whi[:, s, b], t.wlo[:, s, b],
                                t.hh[:, k, :], t.hl[:, k, :], k == 0, k == KF - 1)
            last.then_inc(t.units_used, 1)


def ffn_scalar(act, t, f):
    u0, u1 = U_FFN[f], U_FFN[f] + 2 * KF
    u2 = u1 + 3 * KD

    def silu(j, i):
        if j % 2 == 0:
            used(act, t, u0 + j, 4 * i)
            act.wait_ge(t.h_mul[f], 2 * i + (j // 2 + 1))
            act.activation(t.sg[:, j // 2, :], t.bank[j][:, :], ACT.Silu).then_inc(t.silu_done[f], 1)

    with act.Fori(0, GU_STEPS - 1) as i:
        for j in range(4):
            split_hi(act, t, u0 + j + LEAD, 4 * i)
            silu(j, i)
    for j in range(4):
        split_hi(act, t, u1 - 4 + j + LEAD)
        silu(j, GU_STEPS - 1)
    with act.Fori(0, DN_STEPS - 1) as i:
        for j in range(DN_UNITS):
            split_hi(act, t, u1 + j + LEAD, DN_UNITS * i)
    for j in range(DN_UNITS):
        split_hi(act, t, u2 - DN_UNITS + j + LEAD)


def ffn_vector(dve, t, f):
    u0, u1, ln = U_FFN[f], U_FFN[f] + 2 * KF, LN_OF_FFN[f]
    u2 = u1 + 3 * KD

    def hidden(j, i):
        if j % 2 == 0:
            return
        p = j // 2
        dve.wait_ge(t.silu_done[f], 2 * i + (p + 1))
        used(dve, t, u0 + j, 4 * i)
        dve.tensor_tensor(t.hf[:, p, :], t.sg[:, p, :], t.bank[j][:, :], ALU.mult).then_inc(t.h_mul[f], 1)
        dve.wait_ge(t.h_mul[f], 2 * i + (p + 3))
        dst = bass.ds(2 * i + p, 1)
        dve.tensor_copy(t.hh[:, dst, :], t.hf[:, p:p + 1, :]).then_inc(t.h_hi[f], 1)
        dve.wait_ge(t.h_hi[f], 2 * i + (p + 1))
        dve.tensor_tensor(t.hl[:, dst, :], t.hf[:, p:p + 1, :], t.hh[:, dst, :].bitcast(F32),
                          ALU.subtract).then_inc(t.h_ready[f], 1)

    def residual(j, i):
        m, part = divmod(j, 3)
        if part < 2:
            return
        used(dve, t, u1 + j, DN_UNITS * i)
        dst = bass.ds(4 * i + m, 1)
        dve.scalar_tensor_tensor(t.xt[:, dst, :], t.xt[:, dst, :], 2 * ALPHA,
                                 t.bank[4 + m % 2][:, :].rearrange("p (a n) -> p a n", a=1),
                                 ALU.mult, ALU.add).then_inc(t.z_done[ln], 1)

    with dve.Fori(0, GU_STEPS - 1) as i:
        for j in range(4):
            split_lo(dve, t, u0 + j + LEAD, 4 * i)
            hidden(j, i)
    for j in range(4):
        split_lo(dve, t, u1 - 4 + j + LEAD)
        hidden(j, GU_STEPS - 1)
    with dve.Fori(0, DN_STEPS - 1) as i:
        for j in range(DN_UNITS):
            split_lo(dve, t, u1 + j + LEAD, DN_UNITS * i)
            residual(j, i)
    for j in range(DN_UNITS):
        split_lo(dve, t, u2 - DN_UNITS + j + LEAD)
        residual(j, DN_STEPS - 1)


NORM_SLOTS = 4
KEEP_WARM_BANK = 2
DIRECT = 4
SUMMED = KD - 1


def sums_gpsimd(g, t, ln):
    if ln:
        g.wait_ge(t.maps, 2 * (ln - 1) + 2)
        g.wait_ge(t.norm_b, KD * (ln - 1) + KD)
        g.wait_ge(t.norm_c, KD * (ln - 1) + KD)
    g.memset(t.zsum[:, :], 0.0).then_inc(t.acc[ln], 1)
    g.memset(t.qsum[:, :], 0.0).then_inc(t.acc[ln], 1)
    with g.Fori(0, SUMMED) as m:
        z = t.xt[:, bass.ds(m, 1), :]
        g.wait_ge(t.z_done[ln], m + 3)
        g.wait_ge(t.acc[ln], 3 * m + 2)
        g.tensor_tensor(t.sq3, z, z, ALU.mult).then_inc(t.acc[ln], 1)
        g.tensor_tensor(t.zsum3, t.zsum3, z, ALU.add).then_inc(t.acc[ln], 1)
        g.wait_ge(t.acc[ln], 3 * m + 3)
        g.tensor_tensor(t.qsum3, t.qsum3, t.sq3, ALU.add).then_inc(t.acc[ln], 1)


def keep_warm(pe, t, count):
    for _ in range(count):
        pe.matmul(t.bank[KEEP_WARM_BANK][:, 0:P], t.ones[:, :], t.ident[:, :], start=True, stop=True)


def norm_tensor(pe, t, ln):
    def by_token(bank, at, src):
        for i in range(TT):
            last = pe.matmul(bank[:, at + i:at + i + 1], src[:, i * P:i * P + P],
                             t.cst[:, C_INVD:C_INVD + 1], start=True, stop=True)
        last.then_inc(t.col_sums, 1)

    if ln == 0:
        pe.wait_ge(t.consts_in, t.n_consts)
    if ln == DIRECT:
        norm_maps(pe, t, ln)
        return
    pe.wait_ge(t.acc[ln], 2 + 3 * SUMMED)
    by_token(t.bank[6], 0, t.zsum)
    by_token(t.bank[6], 4, t.qsum)
    keep_warm(pe, t, 7)
    pe.wait_ge(t.z_done[ln], KD + 2)
    by_token(t.bank[7], 0, t.xt[:, KD - 1, :])
    pe.wait_ge(t.last_sq, ln + 1 - (ln > DIRECT))
    by_token(t.bank[7], 4, t.sq)
    norm_maps(pe, t, ln)


SQ_PARTS = 5


def direct_squares(pe, t, part):
    pairs = SQ_PARTS - 2
    if part < pairs:
        pe.wait_ge(t.direct_pair, part + 1)
    else:
        pe.wait_ge(t.direct_sq, pairs + part + 1)
    src = t.direct_slots[2 * part if part < pairs else pairs + part]
    for i in range(TT):
        at = TT + i * SQ_PARTS + part
        last = pe.matmul(t.bank[6][:, at:at + 1], src[:, i * P:i * P + P],
                         t.cst[:, C_INVD:C_INVD + 1], start=True, stop=True)
    last.then_inc(t.direct_summed, 1)


def direct_means(pe, t):
    pe.wait_ge(t.direct_z, KD - 1)
    for i in range(TT):
        last = pe.matmul(t.bank[6][:, i:i + 1], t.zsum[:, i * P:i * P + P],
                         t.cst[:, C_INVD:C_INVD + 1], start=True, stop=True)
    last.then_inc(t.direct_summed, 1)


def direct_add(dve, t, m):
    dve.wait_ge(t.z_done[DIRECT], m + 3)
    if m > 1:
        dve.wait_ge(t.direct_z, m - 1)
    dve.tensor_tensor(t.zsum[:, :], t.xt[:, 0, :] if m == 1 else t.zsum[:, :], t.xt[:, m, :], ALU.add
                      ).then_inc(t.direct_z, 1)


def direct_pairs(g, t):
    for p in range(SQ_PARTS - 2):
        g.wait_ge(t.direct_sq, 2 * p + 2)
        a, b = t.direct_slots[2 * p], t.direct_slots[2 * p + 1]
        g.tensor_tensor(a, a, b, ALU.add).then_inc(t.direct_pair, 1)


def norm_maps(pe, t, ln):
    for n, (b, src) in enumerate(((7, t.zsum), (6, t.sq))):
        if n == 0:
            keep_warm(pe, t, 7)
        pe.wait_ge(t.diag, TT * 2 * ln + TT * (n + 1))
        pe.matmul(t.bank[b][:, :], t.ones[:, :], src[:, :], start=True, stop=True).then_inc(t.maps, 1)
    if ln < 5:
        keep_warm(pe, t, 12)


def norm_scalar(act, t, ln):
    if ln == 0:
        act.wait_ge(t.consts_in, t.n_consts)
    if ln != DIRECT:
        act.wait_ge(t.acc[ln], 2 + 3 * SUMMED)
        act.wait_ge(t.z_done[ln], KD + 2)
        act.activation(t.sq[:, :], t.xt[:, KD - 1, :], ACT.Square).then_inc(t.last_sq, 1)
    act.wait_ge(t.col, 6 * ln + 4)
    act.activation(t.std[:, :], t.var[:, :], ACT.Sqrt).then_inc(t.std_done, 1)
    which, layer = ln % 3, ln // 3
    for k in range(KD):
        act.wait_ge(t.norm_b, KD * ln + k + 1)
        tmp = t.norm_tmp[k % NORM_SLOTS][:, :]
        gain, bias = (t.gains[:, 2 * which + n, layer, k:k + 1] for n in range(2))
        if ln < 5:
            act.activation(t.xh[:, k, :], tmp, ACT.Identity, bias=bias, scale=gain).then_inc(t.x_hi[ln], 1)
        act.activation(t.xt[:, k, :], tmp, ACT.Identity, bias=bias, scale=gain).then_inc(t.norm_c, 1)


def norm_vector(dve, t, ln):
    eps = LN_EPS * (1 if ln % 3 == 1 else 4)
    c = t.col
    if ln == DIRECT:
        dve.wait_ge(t.direct_summed, SQ_PARTS + 1)
        dve.tensor_copy(t.stats[:, 0:TT], t.bank[6][:, 0:TT]).then_inc(c, 1)
        dve.tensor_reduce(t.stats[:, TT:], t.bank[6][:, TT:TT + TT * SQ_PARTS].rearrange(
            "p (a n) -> p a n", n=SQ_PARTS), AX.X, ALU.add).then_inc(c, 1)
    else:
        before = ln - (ln > DIRECT)
        dve.wait_ge(t.col_sums, 4 * before + 2)
        dve.tensor_copy(t.part_stats[:, :], t.bank[6][:, 0:8]).then_inc(c, 1)
        dve.wait_ge(t.col_sums, 4 * before + 4)
        dve.wait_ge(c, 6 * ln + 1)
        dve.tensor_tensor(t.stats[:, :], t.part_stats[:, :], t.bank[7][:, 0:8], ALU.add).then_inc(c, 1)
    dve.wait_ge(c, 6 * ln + 2)
    dve.tensor_tensor(t.mu2[:, :], t.stats[:, 0:4], t.stats[:, 0:4], ALU.mult).then_inc(c, 1)
    dve.wait_ge(c, 6 * ln + 3)
    dve.scalar_tensor_tensor(t.var[:, :], t.stats[:, 4:8], eps, t.mu2[:, :], ALU.add,
                             ALU.subtract).then_inc(c, 1)
    dve.wait_ge(t.std_done, ln + 1)
    dve.reciprocal(t.rstd[:, :], t.std[:, :]).then_inc(c, 1)
    dve.wait_ge(c, 6 * ln + 5)
    for i in range(TT):
        dve.tensor_scalar(t.zsum[:, i * P:i * P + P], t.ident[:, :], t.rstd[:, i:i + 1], None,
                          ALU.mult).then_inc(t.diag, 1)
    dve.scalar_tensor_tensor(t.nmr[:, :], t.stats[:, 0:4], -1.0, t.rstd[:, :], ALU.mult,
                             ALU.mult).then_inc(c, 1)
    dve.wait_ge(c, 6 * ln + 6)
    for i in range(TT):
        dve.tensor_scalar(t.sq[:, i * P:i * P + P], t.ident[:, :], t.nmr[:, i:i + 1], None,
                          ALU.mult).then_inc(t.diag, 1)
    for k in range(KD + 1):
        if k < KD:
            dve.wait_ge(t.maps, 2 * ln + 1)
            dve.tensor_tensor(t.xt[:, k, :], t.xt[:, k, :], t.bank[7][:, :], ALU.mult).then_inc(t.norm_a, 1)
        if k >= 1:
            n = k - 1
            dve.wait_ge(t.maps, 2 * ln + 2)
            dve.wait_ge(t.norm_a, KD * ln + n + 1)
            if n >= NORM_SLOTS:
                dve.wait_ge(t.norm_c, KD * ln + n - NORM_SLOTS + 1)
            dve.tensor_tensor(t.norm_tmp[n % NORM_SLOTS][:, :], t.xt[:, n, :], t.bank[6][:, :],
                              ALU.add).then_inc(t.norm_b, 1)


def norm_gpsimd(g, t, ln):
    for k in range(KD):
        g.wait_ge(t.norm_c, KD * ln + k + 1)
        g.tensor_tensor(t.xl[:, k, :], t.xt[:, k, :], t.xh[:, k, :].bitcast(F32),
                        ALU.subtract).then_inc(t.x_ready[ln], 1)


def mixer_residual(dve, t, ln, m):
    dve.scalar_tensor_tensor(t.xt[:, m, :], t.xt[:, m, :], ALPHA, t.bank[4 + m % 2][:, :],
                             ALU.mult, ALU.add).then_inc(t.z_done[ln], 1)


T_BANKS = 2
PT_SLOTS = 4


def plan_items(raw_items):
    fill = chunk = 0
    items = []
    for n, it in enumerate(raw_items):
        runs, col = [], 0
        for q, k, d, coef, width in it["runs"]:
            at = 0
            while at < width:
                w = min(width - at, 512 - col % 512)
                runs.append((fill + col // 512, col % 512, col, w, q, k[:, at:at + w], d[:, at:at + w], coef))
                at, col = at + w, col + w
        fills = range(fill, fill + -(-col // 512))
        fill = fills[-1] + 1
        chunks, c0 = [], 0
        for b in range(0, len(it["blocks"]), 4):
            part = it["blocks"][b:b + 4]
            cols, here = c0, []
            for w, v in part:
                here.append((cols, w, v))
                cols += w
            chunks.append((chunk, b, here))
            chunk, c0 = chunk + 1, cols
        item = Store()
        item.n, item.runs, item.fills, item.width, item.chunks = n, runs, fills, col, chunks
        item.n_blocks, item.place = len(it["blocks"]), it["place"]
        item.opens, item.fill_end = it["opens"], it["fill_end"]
        items.append(item)
    return items


def scores_tensor(pe, a, it):
    for f in it.fills:
        if f >= len(a.score):
            pe.wait_ge(a.scores_read, f - len(a.score) + 1)
        runs = [r for r in it.runs if r[0] == f]
        for _, bc, _, w, q, k, _, _ in runs:
            last = pe.matmul(a.score[f % len(a.score)][:, bc:bc + w], q, k, start=True, stop=True)
        last.then_inc(a.scores_ready, 1)


def turn_tensor(pe, a, it, c):
    chunk, _, blocks = it.chunks[c]
    pe.wait_ge(a.probs_ready, it.n + 1)
    if chunk >= T_BANKS:
        pe.wait_ge(a.pt_ready, chunk - T_BANKS + 1)
    for j, (col, w, _) in enumerate(blocks):
        last = pe.transpose(a.turn[chunk % T_BANKS][0:w, j * P:j * P + P],
                            a.s[:, it.n % a.slots, col:col + w], a.ident[:, :])
    last.then_inc(a.turned, 1)


def values_tensor(pe, a, it, c):
    chunk, b0, blocks = it.chunks[c]
    pe.wait_ge(a.pt_ready, chunk + 1)
    ofill, i = it.place
    if it.opens and c == 0 and ofill >= len(a.obank):
        pe.wait_ge(a.o_ready, ofill - len(a.obank) + 1)
    for j, (_, w, v) in enumerate(blocks):
        last = pe.matmul(a.obank[ofill % len(a.obank)][:, i * P:i * P + P], v,
                         a.pt[0:w, chunk % PT_SLOTS, j * P:j * P + P],
                         start=b0 + j == 0, stop=b0 + j == it.n_blocks - 1)
    last.then_inc(a.values_done, 1)


def softmax_max(dve, a, it):
    if it.n >= a.slots:
        dve.wait_ge(a.turned, a.items[it.n - a.slots].chunks[-1][0] + 1)
    for f in it.fills:
        dve.wait_ge(a.scores_ready, f + 1)
        runs = [r for r in it.runs if r[0] == f]
        for _, bc, sc, w, _, _, d, coef in runs:
            last = dve.scalar_tensor_tensor(a.s[:, it.n % a.slots, sc:sc + w], d, coef,
                                            a.score[f % len(a.score)][:, bc:bc + w], ALU.mult, ALU.add)
        last.then_inc(a.scores_read, 1)
    dve.wait_ge(a.scores_read, it.fills[-1] + 1)
    dve.tensor_reduce(a.nmax[:, it.n % a.slots:it.n % a.slots + 1], a.s[:, it.n % a.slots, 0:it.width],
                      AX.X, ALU.max, negate=True).then_inc(a.max_ready, 1)


def softmax_scale(dve, a, it):
    c = slice(it.n % a.slots, it.n % a.slots + 1)
    dve.wait_ge(a.exp_done, it.n + 1)
    dve.reciprocal(a.inv[:, c], a.den[:, c]).then_inc(a.inv_ready, 1)
    dve.wait_ge(a.inv_ready, it.n + 1)
    s = a.s[:, it.n % a.slots, 0:it.width]
    dve.tensor_scalar(s, s, a.inv[:, c], None, ALU.mult).then_inc(a.probs_ready, 1)


def output_lo(dve, a, it):
    f = it.fill_end
    if f is not None:
        dve.wait_ge(a.o_hi, f + 1)
        dve.tensor_tensor(a.ol[:, a.ktile[f], :], a.obank[f % len(a.obank)][:, :],
                          a.oh[:, a.ktile[f], :].bitcast(F32), ALU.subtract).then_inc(a.o_ready, 1)


def exponent(act, a, it):
    c = slice(it.n % a.slots, it.n % a.slots + 1)
    act.wait_ge(a.max_ready, it.n + 1)
    if it.n >= a.slots:
        act.wait_ge(a.inv_ready, it.n - a.slots + 1)
    s = a.s[:, it.n % a.slots, 0:it.width]
    act.activation(s, s, ACT.Exp, bias=a.nmax[:, c], accum_out=a.den[:, c]).then_inc(a.exp_done, 1)


def copy_out(act, a, it):
    for chunk, _, blocks in it.chunks:
        w, cols = blocks[0][1], len(blocks) * P
        act.wait_ge(a.turned, chunk + 1)
        if chunk >= PT_SLOTS:
            act.wait_ge(a.values_done, chunk - PT_SLOTS + 1)
        act.activation(a.pt[0:w, chunk % PT_SLOTS, 0:cols], a.turn[chunk % T_BANKS][0:w, 0:cols],
                       ACT.Copy).then_inc(a.pt_ready, 1)


def output_hi(act, a, it):
    f = it.fill_end
    if f is not None:
        act.wait_ge(a.values_done, it.chunks[-1][0] + 1)
        act.activation(a.oh[:, a.ktile[f], :], a.obank[f % len(a.obank)][:, :], ACT.Copy).then_inc(a.o_hi, 1)


KPE, XCMP, KSW, QN, VSW, HCMP, UK, HT, UV, KC, VC, UQ = 5, 6, 10, 12, 16, 20, 22, 26, 28, 32, 33, 34
HID = 2 * P
RMS_AFTER = 8


def emptied(n):
    by_scalar = (0 if n < HCMP else 2 if n < HT else 4) + (min(n - UV + 1, TT) // 2 if n >= UV else 0)
    return n + 1 - by_scalar


def shared(n):
    if n < HT:
        return n - UK + 1
    return TT + (n - UV + 1) // 2 if n < KC else TT + TT // 2 + n - UQ + 1


def even_sync(sp, t):
    e = t.even
    for u in range(EVEN_UNITS):
        if u < VSW:
            src = t.ev_in[u]
        elif u < 19:
            src = t.ev_vg[:, VG_TILES[u - VSW][0] * VG:VG_TILES[u - VSW][1] * VG]
        elif u < 27:
            src = t.ev_w1[u - 19]
        elif u < 29:
            src = (t.ev_uk, t.ev_uv)[u - 27]
        elif u < 33:
            src = t.ev_uq[u - 29]
        else:
            src = t.ev_out[u - 33]
        if u == 6:
            used(sp, t, U_EVEN)
            for dst, mask in ((e.mask[:, :], t.tri_mask), (e.dist[:, :, :], t.causal_mask),
                              (e.distc[:, :, :], t.cmp_mask)):
                sp.dma_start(dst, mask).then_inc(t.masks_in[0], 16)
        load_unit(sp, t, U_EVEN + u, src, EVEN_W[u])


def even_tensor(pe, t, x_ready):
    e = t.even

    def tile(n):
        before = n - 4
        if HCMP <= before < UK:
            pe.wait_ge(e.gelu, before - HCMP + 1)
        elif HT <= before < UV:
            pe.wait_ge(e.gelu, before - HT + 3)
        elif before >= 0:
            pe.wait_ge(e.evac, emptied(before))
            if before >= UK and before not in (KC, VC):
                pe.wait_ge(e.half_out, shared(before))
        return t.bank[n % 4]

    def unit(u):
        split_ready(pe, t, U_EVEN + u)
        s = (U_EVEN + u) % SPLIT
        return t.whi[:, s, :], t.wlo[:, s, :]

    first_pair(pe, t, U_EVEN, t.bank[0:2], x_ready)
    for u in range(2, EVEN_IN_UNITS):
        wh, wl = unit(u)
        if u < VSW:
            bank = tile(u)
            for k in range(KD):
                b = slice(k * P, k * P + P)
                last = product3(pe, bank[:, :], wh[:, b], wl[:, b], t.xh[:, k, :], t.xl[:, k, :],
                                k == 0, k == KD - 1)
        else:
            k0, k1 = VG_TILES[u - VSW]
            for i in range(TT):
                bank = tile(VSW + i) if u == VSW else t.bank[i]
                for k in range(k0, k1):
                    b, tok = slice((k - k0) * VG, (k - k0 + 1) * VG), slice(i * P, i * P + P)
                    last = product3(pe, bank[:, 0:VG], t.xh[:, k, tok], t.xl[:, k, tok],
                                    wh[:, b], wl[:, b], k == 0, k == KD - 1)
        last.then_inc(t.units_used, 1)
        if 3 <= u < 3 + KV + KQ:
            x = u - 3
            pe.wait_ge(e.squared, x + 1)
            pe.matmul(t.bank[4 if x < KV else 5][:, :], (t.ones_kv if x < KV else t.ones_q)[:, :],
                      t.lnbuf[x % 3][:, :], start=x in (0, KV), stop=x in (KV - 1, KV + KQ - 1)
                      ).then_inc(e.rms_sum, 1)
    for kind in range(2):
        bank = tile(HCMP + kind)
        pe.wait_ge(e.b_lo, kind + 1)
        for part in range(4):
            wh, wl = unit(19 + 4 * kind + part)
            for kk in range(4):
                k, b = 4 * part + kk, slice(kk * HID, kk * HID + HID)
                last = product3(pe, bank[0:NB, 0:HID], e.bh[:, kind, k, :], e.bl[:, kind, k, :],
                                wh[:, b], wl[:, b], k == 0, k == CMP_K - 1)
            last.then_inc(t.units_used, 1)
    wh, wl = unit(27)
    for m in range(4):
        bank = tile(UK + m)
        pe.wait_ge(e.c_lo, KV)
        for k in range(KV):
            b = slice(k * 512 + m * P, k * 512 + m * P + P)
            last = product3(pe, bank[:, :], wh[:, b], wl[:, b], e.ch[:, k, :], e.cl[:, k, :],
                            k == 0, k == KV - 1)
        last.then_inc(e.tile_done if m < 3 else t.units_used, 1)
    for kind in range(2):
        bank = tile(HT + kind)
        pe.wait_ge(e.gelu, kind + 1)
        for m in range(2):
            last = pe.transpose(bank[:, m * DH:m * DH + NB], e.hid[0:NB, kind, m * P:m * P + P],
                                t.ident[0:NB, 0:NB])
        last.then_inc(e.tile_done, 1)
    wh, wl = unit(28)
    for i in range(TT):
        bank = tile(UV + i)
        for k in range(KV):
            b, tok = slice(k * 512, k * 512 + 512), slice(i * P, i * P + P)
            last = product3(pe, bank[:, :], e.ch[:, k, tok], e.cl[:, k, tok], wh[:, b], wl[:, b],
                            k == 0, k == KV - 1)
        last.then_inc(e.tile_done if i < TT - 1 else t.units_used, 1)
    bank = tile(KC)
    pe.wait_ge(e.gelu, 4)
    for m in range(2):
        last = pe.matmul(bank[:, 0:NB], t.w2k[:, m, :], e.gel[:, 0, m, :], start=m == 0, stop=m == 1)
    last.then_inc(e.tile_done, 1)
    bank = tile(VC)
    for grp in range(2):
        for m in range(2):
            last = pe.matmul(bank[0:NC, grp * DH:grp * DH + DH], e.gel[:, 1, m, grp * NC:grp * NC + NC],
                             t.w2v[:, m, :], start=m == 0, stop=m == 1)
    last.then_inc(e.tile_done, 1)
    for v in range(UQ_UNITS):
        if v == UQ_UNITS - 1:
            pe.wait_ge(e.n_lo, 6)
            pe.wait_ge(e.evac, emptied(VC))
            for it in e.items[:EARLY]:
                even_scores(pe, e, it)
        wh, wl = unit(29 + v)
        for hh in range(2):
            bank = tile(UQ + 2 * v + hh)
            pe.wait_ge(e.c_lo, KV + KQ)
            for k in range(KQ):
                b = slice((hh * KQ + k) * P, (hh * KQ + k) * P + P)
                last = product3(pe, bank[:, :], wh[:, b], wl[:, b], e.ch[:, KV + k, :],
                                e.cl[:, KV + k, :], k == 0, k == KQ - 1)
            last.then_inc(t.units_used if hh else e.tile_done, 1)
    even_attention_tensor(pe, t)
    pe.sem_inc(t.z_done[1], 2)
    for m in range(KD):
        wh, wl = unit(33 + m)
        pe.wait_ge(t.z_done[1], m + 1)
        pe.wait_ge(e.o_ready, KD)
        for k in range(KD):
            b, f = slice(k * P, k * P + P), (k + 4) % KD
            last = product3(pe, t.bank[4 + m % 2][:, :], wh[:, b], wl[:, b], e.out_h[f], e.out_l[f],
                            k == 0, k == KD - 1)
        last.then_inc(t.units_used, 1)


def even_vector(dve, t):
    e = t.even

    def rope(bank, tab, out):
        dve.tensor_tensor(e.ra[64:96, :], bank[64:96, :], tab[64:96, :], ALU.mult).then_inc(e.rope, 1)
        dve.tensor_tensor(e.rb[64:96, :], bank[96:128, :], tab[96:128, :], ALU.mult).then_inc(e.rope, 1)
        dve.wait_ge(e.rope, 2)
        return dve.tensor_tensor(out, e.ra[64:96, :], e.rb[64:96, :], ALU.add)

    for u in range(EVEN_UNITS - KD):
        if u < 27 and u != EVEN_IN_UNITS - 1:
            split_lo(dve, t, U_EVEN + u + LEAD)
        if u < EVEN_IN_UNITS:
            used(dve, t, U_EVEN + u)
            bank = t.bank[u % 4]
            if u < KPE:
                last = dve.tensor_copy(e.craw[:, u, :], bank[:, :])
            elif u == KPE:
                last = rope(bank, t.rope_k, e.krot[64:96, :])
            elif u < KSW:
                kind, grp = divmod(u - XCMP, 2)
                dve.tensor_copy(e.x[0:64, kind, grp, :], bank[0:64, :])
                last = dve.tensor_copy(e.x[64:128, kind, grp, 0:SEQ - 1], bank[64:128, 1:SEQ])
            elif u < QN:
                last = dve.tensor_copy(e.kn[:, u - KSW, :], bank[:, :])
            elif u < VSW:
                last = dve.tensor_scalar(e.qn[:, u - QN, :], bank[:, :], t.cst[:, C_QN + u - QN:C_QN + u - QN + 1],
                                         None, ALU.mult)
            if u < VSW:
                last.then_inc(e.evac, 1)
            for i in range(TT) if u == EVEN_IN_UNITS - 1 else ():
                dve.tensor_copy(e.vn[:, :, i, :], t.bank[i][:, 0:2 * P].rearrange("p (a n) -> p a n", a=2))
                dve.tensor_copy(e.gate[:, i * 24:i * 24 + 24], t.bank[i][:, 2 * P:VG]).then_inc(e.evac, 1)
            if u == EVEN_IN_UNITS - 1:
                split_lo(dve, t, U_EVEN + u + LEAD)
            if u in (RMS_AFTER + 1, RMS_AFTER + 2):
                r = u - RMS_AFTER - 1
                dve.wait_ge(e.rms_std, r + 1)
                dve.reciprocal(e.rs[:, r, :], e.rs[:, r, :]).then_inc(e.rms_inv, 1)
            if u == RMS_AFTER + 4:
                dve.wait_ge(e.rms_inv, 2)
                for x in range(KV + KQ):
                    dve.scalar_tensor_tensor(e.craw[:, x, :], e.craw[:, x, :], t.rms_g[:, x:x + 1],
                                             e.rs[:, 0 if x < KV else 1, :], ALU.mult,
                                             ALU.mult).then_inc(e.c_full, 1)
            if u == RMS_AFTER + 6:
                for x in range(KV + KQ):
                    dve.wait_ge(e.c_hi, x + 1)
                    dve.tensor_tensor(e.cl[:, x, :], e.craw[:, x, :], e.ch[:, x, :].bitcast(F32),
                                      ALU.subtract).then_inc(e.c_lo, 1)
            if u == EVEN_IN_UNITS - 2:
                for kind in range(2):
                    dve.wait_ge(e.b_hi, kind + 1)
                    dve.tensor_tensor(e.bl[:, kind, :, :], e.bf[:, kind, :, :],
                                      e.bh[:, kind, :, :].bitcast(F32), ALU.subtract).then_inc(e.b_lo, 1)
        elif u == 27:
            dve.wait_ge(e.gate_exp, 1)
            dve.tensor_scalar(e.gate[:, :], e.gate[:, :], 1.0, None, ALU.add).then_inc(e.gate_step, 1)
            dve.wait_ge(e.gate_step, 1)
            dve.reciprocal(e.gate[:, :], e.gate[:, :]).then_inc(e.gate_step, 1)
            dve.wait_ge(e.gate_step, 2)
            dve.tensor_scalar(e.gate[:, 0:H], e.gate[:, 0:H], t.cmp_valid[:, 0:1], None,
                              ALU.mult).then_inc(e.gate_step, 1)
            for m in range(4):
                if m < 3:
                    dve.wait_ge(e.tile_done, m + 1)
                else:
                    used(dve, t, U_EVEN + u)
                dve.tensor_copy(e.kt[0:64, 2 * m, :], t.bank[(UK + m) % 4][0:64, :]).then_inc(e.evac, 1)
            split_lo(dve, t, U_EVEN + u + LEAD)
        elif u == 28:
            for i in range(0, TT, 2):
                dve.wait_ge(e.tile_done, 6 + i)
                dve.tensor_copy(e.vm[:, i, :], t.bank[(UV + i) % 4][:, :]).then_inc(e.evac, 1)
            split_lo(dve, t, U_EVEN + u + LEAD)
            dve.wait_ge(e.tile_done, 9)
            dve.tensor_copy(e.kch[:, :], t.bank[KC % 4][:, 0:NB]).then_inc(e.kc_hi, 1)
            dve.wait_ge(e.kc_hi, 1)
            dve.tensor_tensor(e.kcl[:, :], t.bank[KC % 4][:, 0:NB], e.kch[:, :].bitcast(F32), ALU.subtract
                              ).then_inc(e.evac, 1)
            dve.wait_ge(e.tile_done, 10)
            dve.tensor_copy(e.vc[0:NC, :], t.bank[VC % 4][0:NC, 0:2 * DH]).then_inc(e.evac, 1)
        elif u >= 29:
            if u == 28 + UQ_UNITS:
                dve.wait_ge(t.masks_in[0], 48)
                dve.wait_ge(t.dist_step, 4 * TT)
                dve.wait_ge(e.gate_step, 3)
                for it in e.items[:EARLY]:
                    even_minimum(dve, e, it)
            for h in (2 * (u - 29), 2 * (u - 29) + 1):
                bank = t.bank[(UQ + h) % 4]
                if h % 2:
                    used(dve, t, U_EVEN + u)
                else:
                    dve.wait_ge(e.tile_done, 11 + h // 2)
                c = slice(*((64, 96), (96, 128))[h % 2])
                if h >= 2:
                    dve.wait_ge(e.q_rot, h - 1)
                dve.tensor_tensor(e.ra[c, :], bank[64:96, :], t.rope_q[64:96, :], ALU.mult)
                dve.tensor_tensor(e.rb[c, :], bank[96:128, :], t.rope_q[96:128, :], ALU.mult
                                  ).then_inc(e.evac, 1)
            split_lo(dve, t, U_EVEN + u + LEAD)
    dve.wait_ge(e.q_rot, H)
    even_attention_vector(dve, t)
    for m in range(KD):
        split_lo(dve, t, U_EVEN + EVEN_UNITS - KD + m + LEAD)
        used(dve, t, U_EVEN + EVEN_UNITS - KD + m)
        mixer_residual(dve, t, 1, m)


def even_scalar(act, t):
    e = t.even
    for u in range(EVEN_UNITS - KD):
        if u < 27:
            split_hi(act, t, U_EVEN + u + LEAD)
        if 1 <= u <= KV + KQ:
            x = u - 1
            act.wait_ge(e.evac, x + 1)
            if x >= 3:
                act.wait_ge(e.rms_sum, x - 2)
            act.activation(t.lnbuf[x % 3][:, :], e.craw[:, x, :], ACT.Square).then_inc(e.squared, 1)
        if u == RMS_AFTER:
            for r in range(2):
                act.wait_ge(e.rms_sum, (KV, KV + KQ)[r])
                act.activation(e.rs[:, r, :], t.bank[4 + r][:, :], ACT.Sqrt,
                               bias=t.cst[:, C_RMS_EPS:C_RMS_EPS + 1]).then_inc(e.rms_std, 1)
        if u == RMS_AFTER + 5:
            for x in range(KV + KQ):
                act.wait_ge(e.c_full, x + 1)
                act.activation(e.ch[:, x, :], e.craw[:, x, :], ACT.Copy).then_inc(e.c_hi, 1)
        if u == 16:
            for kind in range(2):
                act.wait_ge(e.b_full, kind + 1)
                act.activation(e.bh[:, kind, :, :], e.bf[:, kind, :, :], ACT.Copy).then_inc(e.b_hi, 1)
        if 19 <= u < 25:
            x = u - 19
            used(act, t, U_EVEN + 18)
            act.wait_ge(e.evac, HCMP)
            src = e.qn[:, x, :] if x < 4 else e.kn[:, x - 4, :]
            act.activation(t.xh[:, x, :], src, ACT.Copy).then_inc(e.n_hi, 1)
        if u in (22, 26):
            kind = (u - 22) // 4
            used(act, t, U_EVEN + u)
            act.activation(e.hid[0:NB, kind, :], t.bank[(HCMP + kind) % 4][0:NB, 0:HID],
                           ACT.Gelu_apprx_tanh).then_inc(e.gelu, 1)
        if u == 26:
            act.wait_ge(e.evac, HCMP)
            act.activation(e.gate[:, :], e.gate[:, :], ACT.Exp, scale=-1.0).then_inc(e.gate_exp, 1)
        if u == 27:
            for m in range(4):
                if m < 3:
                    act.wait_ge(e.tile_done, m + 1)
                else:
                    used(act, t, U_EVEN + u)
                    split_hi(act, t, U_EVEN + u + LEAD)
                act.activation(e.kt[0:64, 2 * m + 1, :], t.bank[(UK + m) % 4][64:128, :],
                               ACT.Copy).then_inc(e.half_out, 1)
            for kind in range(2):
                act.wait_ge(e.tile_done, 4 + kind)
                act.activation(e.gel[:, kind, :, :],
                               t.bank[(HT + kind) % 4][:, 0:2 * DH].rearrange("p (a n) -> p a n", a=2)[:, :, 0:NB],
                               ACT.Copy).then_inc(e.gelu, 1)
        if u == 28:
            for i in range(1, TT, 2):
                if i < TT - 1:
                    act.wait_ge(e.tile_done, 6 + i)
                else:
                    used(act, t, U_EVEN + u)
                    split_hi(act, t, U_EVEN + u + LEAD)
                act.activation(e.vm[:, i, :], t.bank[(UV + i) % 4][:, :], ACT.Copy).then_inc(e.half_out, 1)
        if u >= 29:
            if u == 28 + UQ_UNITS:
                for it in e.items[:EARLY]:
                    even_exp(act, e, it)
            for h in (2 * (u - 29), 2 * (u - 29) + 1):
                if h % 2:
                    used(act, t, U_EVEN + u)
                    split_hi(act, t, U_EVEN + u + LEAD)
                else:
                    act.wait_ge(e.tile_done, 11 + h // 2)
                act.activation(e.qt[0:64, h, :], t.bank[(UQ + h) % 4][0:64, :], ACT.Copy,
                               scale=-MLA_SCALE).then_inc(e.half_out, 1)
    even_attention_scalar(act, t)
    for m in range(KD):
        split_hi(act, t, U_EVEN + EVEN_UNITS - KD + m + LEAD)


def distances_gpsimd(g, t, out, mask_ready, width, keys):
    for i in range(TT):
        w = width(i)
        if t.n_dist:
            g.wait_ge(t.dist_step, t.n_dist)
        t.n_dist += 1
        g.tensor_scalar(t.dist[:, 0:w], keys(i), t.neg_pos_q[:, i:i + 1], -1.0, ALU.add,
                        ALU.mult).then_inc(t.dist_step, 1)
        g.wait_ge(t.dist_step, t.n_dist)
        g.wait_ge(*mask_ready)
        t.n_dist += 1
        g.tensor_tensor(out[:, i, 0:w], out[:, i, 0:w], t.dist[:, 0:w], ALU.add
                        ).then_inc(t.dist_step, 1)


def even_gpsimd(g, t):
    e = t.even
    for kind in range(2):
        g.wait_ge(e.evac, XCMP + 2 * kind + 2)
        for m in range(CMP_K):
            src = e.x[:, kind, :, 2 * m:2 * m + 16 * (NC - 1) + 1:16]
            last = g.tensor_scalar(e.bf[:, kind, m, :].rearrange("p (a b) -> p a b", a=2), src,
                                   t.cmp_pos[:, m:m + 1], 1.0, ALU.add, ALU.mult)
        last.then_inc(e.b_full, 1)
    distances_gpsimd(g, t, e.dist, (t.masks_in[0], 48), lambda i: SEQ, lambda i: t.pos_k[:, :])
    distances_gpsimd(g, t, e.distc, (t.masks_in[0], 48), lambda i: NC,
                     lambda i: t.pos_k[:, 31:SEQ:16])
    for x in range(6):
        g.wait_ge(e.n_hi, x + 1)
        src = e.qn[:, x, :] if x < 4 else e.kn[:, x - 4, :]
        g.tensor_tensor(t.xl[:, x, :], src, t.xh[:, x, :].bitcast(F32), ALU.subtract).then_inc(e.n_lo, 1)
    g.wait_ge(e.n_lo, 6)
    for h in range(H):
        c = slice(*((64, 96), (96, 128))[h % 2])
        g.wait_ge(e.evac, emptied(UQ + h))
        if h:
            g.wait_ge(e.q_rot, h)
        g.tensor_tensor(e.qt[64:96, h, :], e.ra[c, :], e.rb[c, :], ALU.add).then_inc(e.q_rot, 1)
    g.wait_ge(e.q_rot, H)
    even_attention_gpsimd(g, t)


EARLY = 3
S_LEAD = 4
V_LAG = 2
TURN_LAG = 5
COPY_LAG, HI_LAG = 3, 8
SUM_LAG, LO_LAG = 6, 9
S_SLOTS, COLS, ACC_SLOTS = 5, 8, 4


def even_items(t):
    e = t.even
    items = []

    def add(q, k, d, coef, width, blocks, side, branch, gate, group, tile, group_end, needs, skip=0):
        it = Store()
        it.n, it.slot = len(items), slice(len(items) % COLS, len(items) % COLS + 1)
        it.q, it.k, it.d, it.coef, it.width = q, k, d, coef, width
        it.blocks, it.side, it.branch, it.gate, it.skip = blocks, side, branch, gate, skip
        it.group, it.tile, it.group_end, it.needs = group, tile, group_end, needs
        items.append(it)

    for pair in range(H // 2):
        for i in reversed(range(TT)):
            for h in (2 * pair, 2 * pair + 1):
                grp, m = divmod(h, 4)
                r = slice(DH * grp, DH * grp + DH)
                q, L = [x[r, m, i * P:i * P + P] for x in (e.nqh, e.nql)], (i + 1) * P
                for br in range(3):
                    if br == 0:
                        keys, w, d = slice(grp * (NC - 1), grp * (NC - 1) + NC + 1), NC, e.distc[:, i, :]
                        k = [x[r, keys] for x in (e.kch, e.kcl)]
                        blocks = [(NC, e.vc[0:NC, grp * DH:grp * DH + DH])]
                    else:
                        keys, w, d = slice(0, max(L, 2 * P)), L, e.dist[:, i, 0:L]
                        k = [x[r, br - 1, keys] for x in (e.nkh, e.nkl)]
                        blocks = [(P, e.vn[:, br - 1, j, grp * DH:grp * DH + DH]) for j in range(i + 1)]
                    add(q=q, k=k, d=d, coef=NSA_SLOPES[h], width=w, blocks=blocks, side=h % 2, branch=br,
                        gate=e.gate[:, i * 24 + br * H + h:i * 24 + br * H + h + 1],
                        group=pair * TT + TT - 1 - i, tile=i, group_end=h % 2 == 1 and br == 2, needs=(),
                        skip=grp if br == 0 else 0)
    for h in range(H):
        for i in reversed(range(TT)):
            L = (i + 1) * P
            add(q=[x[0:96, h % 2, i * P:i * P + P] for x in (e.mqh, e.mql)],
                k=[x[0:96, h % 2, 0:max(L, 2 * P)] for x in (e.mkh, e.mkl)],
                d=e.mask[:, SEQ - L:SEQ], coef=1.0, width=L,
                blocks=[(P, e.vm[:, j, h * DH:h * DH + DH]) for j in range(i + 1)], side=h % 2,
                branch=0, gate=None, group=(H // 2 + h // 2) * TT + TT - 1 - i, tile=i, group_end=h % 2 == 1,
                needs=((e.mla_split, h + 1),) if i == TT - 1 else ())
    return items


def even_scores(pe, e, it):
    bank = e.score[it.n % len(e.score)]
    if it.n >= len(e.score):
        pe.wait_ge(e.min_ready, it.n - len(e.score) + 1)
    for sem, value in it.needs:
        pe.wait_ge(sem, value)
    cols = it.k[0].shape[-1]
    product3(pe, bank[:, 0:cols], it.q[0], it.q[1], it.k[0], it.k[1], True, True
             ).then_inc(e.scores_ready, 1)


def even_attention_tensor(pe, t):
    e = t.even
    items = e.items

    def turn(it):
        pe.wait_ge(e.exp_done, it.n + 1)
        if it.n >= T_BANKS:
            pe.wait_ge(e.pt_ready, it.n - T_BANKS + 1)
        for j, (w, _) in enumerate(it.blocks):
            last = pe.transpose(e.turn[it.n % T_BANKS][0:w, j * P:j * P + P],
                                e.s[:, it.n % S_SLOTS, j * P:j * P + w], t.ident[:, :])
        last.then_inc(e.turned, 1)

    def values(it):
        pe.wait_ge(e.pt_ready, it.n + 1)
        if it.n >= 2:
            pe.wait_ge(e.summed, it.n - 1)
        for j, (w, v) in enumerate(it.blocks):
            last = pe.matmul(e.obank[it.n % 2][:, 0:DH], e.pt[0:w, it.n % PT_SLOTS, j * P:j * P + P], v,
                             start=j == 0, stop=j == len(it.blocks) - 1)
        last.then_inc(e.values_done, 1)

    def turn_sum(it):
        if it.group_end:
            pe.wait_ge(e.summed, it.n + 1)
            f, order = divmod(it.group, TT)
            i = it.tile
            if order == 0 and f:
                pe.wait_ge(e.o_ready, f)
            pe.transpose(e.outbank[:, i * P:i * P + P], e.acc[:, it.group % ACC_SLOTS, :],
                         t.ident[:, :]).then_inc(e.sum_turned, 1)

    for it in items[EARLY:S_LEAD]:
        even_scores(pe, e, it)
    for n in range(len(items) + TURN_LAG):
        if n + S_LEAD < len(items):
            even_scores(pe, e, items[n + S_LEAD])
        if n == 1:
            pe.wait_ge(e.evac, emptied(UQ + 5))
            pe.wait_ge(e.half_out, shared(UQ + 5))
        if n == V_LAG:
            pe.wait_ge(e.evac, emptied(UQ + H - 1))
            pe.wait_ge(e.half_out, shared(UQ + H - 1))
        if n == 0:
            pe.wait_ge(e.evac, emptied(UQ + 4))
            pe.wait_ge(e.half_out, shared(UQ + 4))
            keep_warm(pe, t, 6)
        if n == 1:
            keep_warm(pe, t, 6)
        if n < len(items):
            turn(items[n])
        if 0 <= n - V_LAG < len(items):
            values(items[n - V_LAG])
        if n >= TURN_LAG:
            turn_sum(items[n - TURN_LAG])


def even_minimum(dve, e, it):
    if it.n >= S_SLOTS:
        dve.wait_ge(e.turned, it.n - S_SLOTS + 1)
    if it.n >= COLS:
        dve.wait_ge(e.exp_done, it.n - COLS + 1)
    dve.wait_ge(e.scores_ready, it.n + 1)
    dve.tensor_tensor_reduce(e.s[:, it.n % S_SLOTS, 0:it.width],
                             e.score[it.n % len(e.score)][:, it.skip:it.skip + it.width], it.d, it.coef, 3e38,
                             ALU.add, ALU.min, e.nmax[:, it.slot]).then_inc(e.min_ready, 1)


def even_factor(dve, e, it):
    dve.wait_ge(e.exp_done, it.n + 1)
    one = dve.reciprocal(e.inv[:, it.slot], e.den[:, it.slot])
    if it.gate is None:
        one.then_inc(e.inv_ready, 2)
    else:
        one.then_inc(e.inv_ready, 1)
        dve.wait_ge(e.inv_ready, 2 * it.n + 1)
        dve.tensor_tensor(e.inv[:, it.slot], e.inv[:, it.slot], it.gate, ALU.mult).then_inc(e.inv_ready, 1)


def even_attention_vector(dve, t):
    e = t.even
    items = e.items

    def add(it):
        dve.wait_ge(e.values_done, it.n + 1)
        dve.wait_ge(e.inv_ready, 2 * it.n + 2)
        acc = e.acc[:, it.group % ACC_SLOTS, it.side * DH:it.side * DH + DH]
        out = e.obank[it.n % 2][:, 0:DH]
        if it.branch == 0:
            if it.group >= ACC_SLOTS:
                dve.wait_ge(e.sum_turned, it.group - ACC_SLOTS + 1)
            dve.tensor_scalar(acc, out, e.inv[:, it.slot], None, ALU.mult).then_inc(e.summed, 1)
        else:
            dve.wait_ge(e.summed, it.n)
            dve.scalar_tensor_tensor(acc, out, e.inv[:, it.slot], acc, ALU.mult, ALU.add
                                     ).then_inc(e.summed, 1)

    def lo(it):
        f, order = divmod(it.group, TT)
        if it.group_end and order == TT - 1:
            dve.wait_ge(e.o_hi, f + 1)
            dve.tensor_tensor(e.out_l[f], e.outbank[:, :], e.out_h[f].bitcast(F32), ALU.subtract
                              ).then_inc(e.o_ready, 1)

    for it in items[:EARLY - 1]:
        even_factor(dve, e, it)
    for n in range(EARLY, len(items) + LO_LAG):
        if n < len(items):
            even_minimum(dve, e, items[n])
        if n - 1 < len(items):
            even_factor(dve, e, items[n - 1])
        if 0 <= n - SUM_LAG < len(items):
            add(items[n - SUM_LAG])
        if n >= LO_LAG:
            lo(items[n - LO_LAG])


def even_exp(act, e, it):
    act.wait_ge(e.min_ready, it.n + 1)
    if it.n >= COLS:
        act.wait_ge(e.inv_ready, 2 * (it.n - COLS) + 1)
    s = e.s[:, it.n % S_SLOTS, 0:it.width]
    act.activation(s, s, ACT.Exp, bias=e.nmax[:, it.slot], scale=-1.0,
                   accum_out=e.den[:, it.slot]).then_inc(e.exp_done, 1)


def even_attention_scalar(act, t):
    e = t.even
    items = e.items

    def copy(it):
        w, cols = it.blocks[0][0], len(it.blocks) * P
        act.wait_ge(e.turned, it.n + 1)
        if it.n >= PT_SLOTS:
            act.wait_ge(e.values_done, it.n - PT_SLOTS + 1)
        act.activation(e.pt[0:w, it.n % PT_SLOTS, 0:cols], e.turn[it.n % T_BANKS][0:w, 0:cols],
                       ACT.Copy).then_inc(e.pt_ready, 1)

    def hi(it):
        f, order = divmod(it.group, TT)
        if it.group_end and order == TT - 1:
            act.wait_ge(e.sum_turned, it.group + 1)
            act.activation(e.out_h[f], e.outbank[:, :], ACT.Copy).then_inc(e.o_hi, 1)

    for n in range(EARLY, len(items) + HI_LAG):
        if n < len(items):
            even_exp(act, e, items[n])
        if 0 <= n - COPY_LAG < len(items):
            copy(items[n - COPY_LAG])
        if n >= HI_LAG:
            hi(items[n - HI_LAG])


def even_attention_gpsimd(g, t):
    e = t.even
    steps = 0

    def halves(full, hi, lo):
        nonlocal steps
        if steps:
            g.wait_ge(e.mla_step, steps)
        g.tensor_scalar(hi, full, 1.0, 1.0, ALU.mult, ALU.mult).then_inc(e.mla_step, 1)
        g.wait_ge(e.mla_step, steps + 1)
        g.tensor_tensor(lo, full, hi.bitcast(F32), ALU.subtract).then_inc(e.mla_step, 1)
        steps += 2

    g.wait_ge(t.units_used, SPLIT + U_EVEN + 33)
    g.wait_ge(e.evac, HCMP)
    for s in range(2):
        halves(e.krot[64:96, :], e.mkh[64:96, s, :], e.mkl[64:96, s, :])
    first = len(e.items) - H * TT
    for h in range(H):
        if h >= 2:
            g.wait_ge(e.scores_ready, first + TT * (h - 1))
        if h == 0:
            g.wait_ge(e.half_out, shared(UQ + H - 1))
        halves(e.kt[0:64, h, :], e.mkh[0:64, h % 2, :], e.mkl[0:64, h % 2, :])
        halves(e.qt[0:96, h, :], e.mqh[0:96, h % 2, :], e.mql[0:96, h % 2, :])
        g.wait_ge(e.mla_step, steps)
        g.sem_inc(e.mla_split, 1)


HEAD_UNITS = 2 * DG
V_UNITS = 4 * DG
BEFORE = 2
BETWEEN = (2, 1, 1) + (1, 2, 2, 1) * (DHEADS - 2)


def odd_units_between(n):
    first = HEAD_UNITS + BEFORE + sum(BETWEEN[:n])
    return range(first, first + (BETWEEN[n] if n < len(BETWEEN) else 0))


def odd_pairs_between(n):
    v = n - (DHEADS - 1) * TT
    return range(v, v + 1) if v >= 0 else range(0)


def odd_sync(sp, t):
    for u in range(ODD_UNITS):
        if u == 6:
            used(sp, t, U_ODD)
            for n in range(DG):
                sp.dma_start(t.odd.dist[n][:, :, :], t.dil_mask[n]).then_inc(t.masks_in[1], 16)
        if u < V_UNITS:
            src = t.od_v[u]
        else:
            src = t.od_qk[u - V_UNITS] if u < ODD_IN_UNITS else t.od_out[u - ODD_IN_UNITS] if u < ODD_UNITS - 1 else t.od_last
        load_unit(sp, t, U_ODD + u, src, ODD_W[u])


ODD_BANKS = (4, 3)
IN_EVACS = DG * TT + HEAD_UNITS * DHEADS


def odd_tensor(pe, t, x_ready):
    o = t.odd

    for u in range(V_UNITS):
        n, part = divmod(u, 4)
        split_ready(pe, t, U_ODD + u)
        s = (U_ODD + u) % SPLIT
        if n == 2 and part == 0:
            pe.wait_ge(o.evac, TT)
        for kk in range(2):
            k = 2 * part + kk
            if n == 0:
                pe.wait_ge(x_ready, k + 1)
            for i in range(TT):
                b, tok = slice(kk * 512, kk * 512 + 512), slice(i * P, i * P + P)
                last = product3(pe, t.bank[4 * (n % 2) + i][:, :], t.xh[:, k, tok], t.xl[:, k, tok],
                                t.whi[:, s, b], t.wlo[:, s, b], k == 0, k == KD - 1)
        last.then_inc(t.units_used, 1)

    def unit(u):
        split_ready(pe, t, U_ODD + V_UNITS + u)
        s = (U_ODD + V_UNITS + u) % SPLIT
        bank = t.bank[ODD_BANKS[u % 2]]
        pe.wait_ge(o.evac, 2 * TT if u == 0 else DG * TT + u - 1)
        for k in range(KD):
            b = slice(k * P, k * P + P)
            last = product3(pe, bank[:, :], t.whi[:, s, b], t.wlo[:, s, b], t.xh[:, k, :],
                            t.xl[:, k, :], k == 0, k == KD - 1)
        last.then_inc(t.units_used, 1)

    def pair(v):
        u = U_ODD + ODD_IN_UNITS + v
        split_ready(pe, t, u)
        pe.wait_ge(o.o_ready, DHEADS - 1)
        for half in range(2):
            m = 2 * v + half
            pe.wait_ge(o.evac, IN_EVACS + m - 1)
            for k in range(DHEADS - 1):
                at = (half * (DHEADS - 1) + k) * P
                b = slice(at, at + P)
                last = product3(pe, t.bank[ODD_BANKS[m % 2]][:, :], t.whi[:, u % SPLIT, b],
                                t.wlo[:, u % SPLIT, b], o.oh[:, k, :], o.ol[:, k, :], k == 0, k == DHEADS - 2)
            last.then_inc(t.units_used if half else o.tile_done, 1)

    for u in range(HEAD_UNITS):
        unit(u)
    pe.wait_ge(o.evac, DG * TT + HEAD_UNITS)
    scores_tensor(pe, o, o.items[0])
    unit(HEAD_UNITS)
    scores_tensor(pe, o, o.items[1])
    unit(HEAD_UNITS + 1)
    for it in o.items:
        last = len(it.chunks) - 1
        for c in range(last + 1):
            turn_tensor(pe, o, it, c)
            if c:
                values_tensor(pe, o, it, c - 1)
        for u in odd_units_between(it.n):
            unit(u)
        values_tensor(pe, o, it, last)
        if it.n + 2 < len(o.items):
            if (it.n + 2) % TT == 0:
                pe.wait_ge(o.evac, DG * TT + HEAD_UNITS * ((it.n + 2) // TT + 1))
            scores_tensor(pe, o, o.items[it.n + 2])
        for v in odd_pairs_between(it.n):
            pair(v)
    pe.sem_inc(t.z_done[4], 2)
    u = U_ODD + ODD_UNITS - 1
    split_ready(pe, t, u)
    pe.wait_ge(o.evac, IN_EVACS + KD)
    pe.wait_ge(o.o_ready, DHEADS)
    for m in range(KD):
        b = slice(m * P, m * P + P)
        pe.wait_ge(t.z_done[4], m + 1)
        product3(pe, t.bank[ODD_BANKS[m % 2]][:, :], t.whi[:, u % SPLIT, b], t.wlo[:, u % SPLIT, b],
                 o.oh[:, DHEADS - 1, :], o.ol[:, DHEADS - 1, :], True, True
                 ).then_inc(t.units_used if m == KD - 1 else o.tile_done, 1)
        if m >= KD - 2:
            direct_squares(pe, t, m - (KD - 2))
        elif m:
            keep_warm(pe, t, 2)
    for part in range(2, SQ_PARTS):
        direct_squares(pe, t, part)
    direct_means(pe, t)


def odd_vector(dve, t):
    o = t.odd
    for u in range(V_UNITS):
        if u % 4 < 3:
            split_lo(dve, t, U_ODD + u + LEAD)
        else:
            used(dve, t, U_ODD + u)
            for i in range(TT):
                dve.tensor_copy(o.v[:, i, u // 4, :], t.bank[4 * (u // 4 % 2) + i][:, :]).then_inc(o.evac, 1)
            split_lo(dve, t, U_ODD + u + LEAD)

    def unit(u):
        hp, r = divmod(u, HEAD_UNITS)
        kind, grp = divmod(r, DG)
        bank, side = t.bank[ODD_BANKS[u % 2]], hp % 2
        if hp >= 2 and r == 0:
            dve.wait_ge(o.scores_ready, o.items[TT * (hp - 1) - 1].fills[-1] + 1)
        used(dve, t, U_ODD + V_UNITS + u)
        if kind == 0:
            last = dve.tensor_scalar(o.q[:, side, grp, :], bank[:, :], DIL_SCALE, None, ALU.mult)
        else:
            last = dve.tensor_copy(o.k[:, side, grp, :], bank[:, :])
        last.then_inc(o.evac, 1)
        split_lo(dve, t, U_ODD + V_UNITS + u + LEAD)

    def pair(v):
        u = U_ODD + ODD_IN_UNITS + v
        for half in range(2):
            m = 2 * v + half
            if half:
                used(dve, t, u)
            else:
                dve.wait_ge(o.tile_done, v + 1)
            dve.scalar_tensor_tensor(t.xt[:, m, :], t.xt[:, m, :], ALPHA, t.bank[ODD_BANKS[m % 2]][:, :],
                                     ALU.mult, ALU.add).then_inc(o.evac, 1)
        split_lo(dve, t, u + LEAD)

    for u in range(HEAD_UNITS):
        unit(u)
    dve.wait_ge(t.dist_step, (4 + 2 * DG) * TT)
    softmax_max(dve, o, o.items[0])
    softmax_scale(dve, o, o.items[0])
    for u in range(HEAD_UNITS, HEAD_UNITS + BEFORE):
        unit(u)
    for it in o.items:
        if it.n + 1 < len(o.items):
            softmax_max(dve, o, o.items[it.n + 1])
            softmax_scale(dve, o, o.items[it.n + 1])
        for u in odd_units_between(it.n):
            unit(u)
        output_lo(dve, o, it)
        for v in odd_pairs_between(it.n):
            pair(v)
    u = U_ODD + ODD_UNITS - 1
    dve.wait_ge(o.evac, IN_EVACS + KD)
    for m in range(KD):
        if m == KD - 1:
            used(dve, t, u)
        else:
            dve.wait_ge(o.tile_done, KD // 2 + m + 1)
        dve.tensor_tensor(t.xt[:, m, :], t.xt[:, m, :], t.bank[ODD_BANKS[m % 2]][:, :],
                          ALU.add).then_inc(t.z_done[4], 1)
        if m >= 2:
            direct_add(dve, t, m - 1)
    direct_add(dve, t, KD - 1)
    split_lo(dve, t, u + LEAD)


def odd_scalar(act, t):
    o = t.odd
    for u in range(V_UNITS + HEAD_UNITS):
        split_hi(act, t, U_ODD + u + LEAD)
    exponent(act, o, o.items[0])
    for u in range(HEAD_UNITS, HEAD_UNITS + BEFORE):
        split_hi(act, t, U_ODD + V_UNITS + u + LEAD)
    for it in o.items:
        copy_out(act, o, it)
        if it.n + 1 < len(o.items):
            exponent(act, o, o.items[it.n + 1])
        for u in odd_units_between(it.n):
            split_hi(act, t, U_ODD + V_UNITS + u + LEAD)
        output_hi(act, o, it)
        for v in odd_pairs_between(it.n):
            split_hi(act, t, U_ODD + ODD_IN_UNITS + v + LEAD)
    for m in range(KD):
        act.wait_ge(t.z_done[DIRECT], m + 3)
        act.activation(t.direct_slots[m], t.xt[:, m, :], ACT.Square).then_inc(t.direct_sq, 1)
    split_hi(act, t, U_ODD + ODD_UNITS - 1 + LEAD)


def odd_keys(g, i):
    first = max(i * P - DIL[g][0], 0)
    return first, (i + 1) * P - first


def odd_gpsimd(g, t):
    o = t.odd
    for n in range(DG):
        distances_gpsimd(g, t, o.dist[n], (t.masks_in[1], 48), lambda i: odd_keys(n, i)[1],
                         lambda i: t.pos_k[:, odd_keys(n, i)[0]:(i + 1) * P])


def odd_items(t):
    o = t.odd
    raw = []
    for hp in range(DHEADS):
        for i in reversed(range(TT)):
            runs, blocks, side = [], [], hp % 2
            for n in range(DG):
                first, w = odd_keys(n, i)
                runs.append((o.q[:, side, n, i * P:i * P + P], o.k[:, side, n, first:first + w], o.dist[n][:, i, 0:w],
                             -DIL_SLOPES[n * DHEADS + hp], w))
                blocks += [(P, o.v[:, j, n, hp * P:hp * P + P]) for j in range(first // P, i + 1)]
            raw.append(dict(runs=runs,
                            blocks=blocks, place=(hp, i),
                            opens=i == TT - 1, fill_end=hp if i == 0 else None))
    return plan_items(raw)


def start_vector(dve, t):
    c, ang, turns = t.setup, t.lnbuf[0], t.lnbuf[1]
    dve.wait_ge(t.consts_in, t.n_consts)

    def step(n, ins):
        ins.then_inc(c, 1)
        dve.wait_ge(c, n)

    step(1, dve.tensor_scalar(t.neg_pos_q[:, :], t.pos_qi[:, :], -1.0, None, ALU.mult))
    step(2, dve.tensor_copy(t.pos_k[:, :], t.pos_ki[:, :]))
    step(3, dve.tensor_scalar(ang[:, :], t.pos_k[:, :], t.cst[:, C_FREQ:C_FREQ + 1], None, ALU.mult))
    step(4, dve.tensor_scalar(turns[:, :], ang[:, :], 1 / (2 * np.pi), t.cst[:, C_TURN:C_TURN + 1],
                              ALU.mult, ALU.add))
    step(5, dve.tensor_scalar(turns[:, :], turns[:, :], MAGIC, MAGIC, ALU.add, ALU.subtract))
    for n, part in enumerate((PI2_A, PI2_B, PI2_C)):
        step(6 + n, dve.scalar_tensor_tensor(ang[:, :], turns[:, :], -part, ang[:, :], ALU.mult, ALU.add))
    step(9, dve.tensor_scalar(ang[:, :], ang[:, :], t.cst[:, C_PHASE:C_PHASE + 1], PI_SAFE,
                              ALU.add, ALU.min))
    step(10, dve.tensor_scalar(ang[:, :], ang[:, :], -PI_SAFE, None, ALU.max))
    dve.wait_ge(t.sin_done, 1)
    step(11, dve.tensor_scalar(t.rope_q[:, :], t.rope_k[:, :], -MLA_SCALE, None, ALU.mult))


def start_scalar(act, t):
    act.wait_ge(t.setup, 10)
    act.activation(t.rope_k[:, :], t.lnbuf[0][:, :], ACT.Sin).then_inc(t.sin_done, 1)


def input_hi(act, t):
    for k in range(KD):
        act.wait_ge(t.x_in[k], 16)
        act.activation(t.xh[:, k, :], t.xt[:, k, :], ACT.Copy).then_inc(t.in_hi, 1)


def input_lo(g, t):
    for k in range(KD):
        g.wait_ge(t.in_hi, k + 1)
        g.tensor_tensor(t.xl[:, k, :], t.xt[:, k, :], t.xh[:, k, :].bitcast(F32),
                        ALU.subtract).then_inc(t.in_ready, 1)


def trunk(nc, d, out):
    t = Store()
    t.n_dist = 0
    t.x_t, t.w_gate, t.w_up, t.w_down = d["x_t"], d["w_gate"], d["w_up"], d["w_down"]
    t.ev_in, t.ev_vg, t.ev_w1, t.ev_uk, t.ev_uv = (d[n] for n in (
        "ev_in", "ev_vg", "ev_w1", "ev_uk", "ev_uv"))
    t.ev_uq, t.ev_out = d["ev_uq"], d["ev_out"]
    t.od_v, t.od_qk, t.od_out, t.od_last = (d["od_" + n] for n in ("v", "qk", "out", "last"))
    t.tri_mask, t.causal_mask, t.cmp_mask, t.dil_mask = (d[n] for n in (
        "tri_mask", "causal_mask", "cmp_mask", "dil_mask"))
    with ExitStack() as ctx:
        def sb(name, shape, dtype=F32, scope=ctx):
            return scope.enter_context(nc.sbuf_tensor(name, shape, dtype))

        def sem(name):
            return ctx.enter_context(nc.semaphore(name))

        def sems(name, n):
            return [sem(f"{name}_{i}") for i in range(n)]

        t.xt = sb("xt", [P, KD, SEQ])
        t.xh = sb("xh", [P, KD, SEQ], F32R)
        t.xl = sb("xl", [P, KD, SEQ], F32R)
        t.raw = sb("raw", [P, RAW, UNIT])
        t.whi = sb("whi", [P, SPLIT, UNIT], F32R)
        t.wlo = sb("wlo", [P, SPLIT, UNIT], F32R)
        t.rope_k = sb("rope_k", [P, SEQ])
        t.rope_q = sb("rope_q", [P, SEQ])
        t.pos_k = sb("pos_k", [P, SEQ])
        t.neg_pos_q = sb("neg_pos_q", [P, TT])
        t.dist = sb("dist", [P, SEQ])
        t.pos_ki = t.dist[:, :].bitcast(I32)
        t.pos_qi = sb("pos_qi", [P, TT], I32)
        t.zsum, t.qsum, t.sq = t.lnbuf = [sb(n, [P, SEQ]) for n in ("zsum", "qsum", "sq")]
        t.norm_tmp = (t.dist, t.qsum, t.zsum, t.sq)
        t.zsum3, t.qsum3, t.sq3 = (b[:, :].rearrange("p (a n) -> p a n", a=1) for b in t.lnbuf)
        t.ident = sb("ident", [P, P])
        t.ones = sb("ones", [P, P])
        t.ones_kv = sb("ones_kv", [P, P])
        t.ones_q = sb("ones_q", [P, P])
        t.gains = sb("gains", [P, 6, DEPTH, KD])
        t.rms_g = sb("rms_g", [P, KV + KQ])
        t.w2k = sb("w2k", [P, 2, P])
        t.w2v = sb("w2v", [P, 2, DH])
        t.cmp_pos = sb("cmp_pos", [P, CMP_K])
        t.cst = sb("cst", [P, N_CST])
        t.cmp_valid = sb("cmp_valid", [P, 1])
        t.stats = sb("stats", [P, 2 * TT])
        t.part_stats = sb("part_stats", [P, 2 * TT])
        t.mu2, t.var, t.std, t.rstd, t.nmr = (sb(n, [P, TT]) for n in ("mu2", "var", "std", "rstd", "nmr"))
        t.small = [(t.cst[:, :], d["c_cst"]), (t.pos_qi[:, :], d["c_pos_q"]), (t.pos_ki, d["c_pos_k"]),
                 (t.ident[:, :], d["c_ident"]), (t.gains[:, :, :, :], d["c_gains"]),
                 (t.ones[:, :], d["c_ones"]), (t.ones_kv[:, :], d["c_ones_kv"]), (t.ones_q[:, :], d["c_ones_q"]),
                 (t.rms_g[:, :], d["c_rms_g"]), (t.w2k[:, :, :], d["c_w2k"]),
                 (t.w2v[:, :, :], d["c_w2v"]), (t.cmp_pos[:, :], d["c_cmp_pos"]),
                 (t.cmp_valid[:, :], d["c_cmp_valid"])]
        t.n_consts = 16 * len(t.small)

        with ExitStack() as scope:
            t.hh = sb("hh", [P, KF, SEQ], F32R, scope)
            t.hl = sb("hl", [P, KF, SEQ], F32R, scope)
            t.sg = sb("sg", [P, 2, SEQ], F32, scope)
            t.hf = sb("hf", [P, 2, SEQ], F32, scope)
        e = t.even = Store()
        e.hid = t.lnbuf[0][:, :].rearrange("p (a n) -> p a n", a=2)
        with ExitStack() as scope:
            e.vm = sb("e_vm", [P, TT, H * DH], F32, scope)
            with ExitStack() as part:
                e.qn = sb("e_qn", [P, 4, SEQ], F32, part)
            e.out2 = sb("e_out2", [P, 4, SEQ], F32R, scope)
            e.kn = sb("e_kn", [P, 2, SEQ], F32, scope)
            e.vn = sb("e_vn", [P, 2, TT, P], F32, scope)
            e.dist = sb("e_dist", [P, TT, SEQ], F32, scope)
            e.distc = sb("e_distc", [P, TT, NC], F32, scope)
            e.mask = sb("e_mask", [P, SEQ], F32, scope)
            e.kch, e.kcl = (sb(n, [P, NB], F32R, scope) for n in ("e_kch", "e_kcl"))
            e.vc = sb("e_vc", [P, 2 * DH], F32, scope)
            e.gate = sb("e_gate", [P, TT * 24], F32, scope)
            e.gel = sb("e_gel", [P, 2, 2, NB], F32, scope)
            e.krot = sb("e_krot", [P, SEQ], F32, scope)
            e.ra = sb("e_ra", [P, SEQ], F32, scope)
            e.rb = sb("e_rb", [P, SEQ], F32, scope)
            e.nmax, e.den, e.inv = (sb(n, [P, COLS], F32, scope) for n in ("e_nmax", "e_den", "e_inv"))
            with ExitStack() as part:
                e.x = sb("e_x", [P, 2, 2, SEQ], F32, part)
                e.bf = sb("e_bf", [P, 2, CMP_K, NB], F32, part)
                e.bh = sb("e_bh", [P, 2, CMP_K, NB], F32R, part)
                e.bl = sb("e_bl", [P, 2, CMP_K, NB], F32R, part)
            e.qt = sb("e_qt", [P, H, SEQ], F32, scope)
            e.kt = sb("e_kt", [P, H, SEQ], F32, scope)
            with ExitStack() as part:
                e.craw = sb("e_craw", [P, KV + KQ, SEQ], F32, part)
                e.ch = sb("e_ch", [P, KV + KQ, SEQ], F32R, part)
                e.cl = sb("e_cl", [P, KV + KQ, SEQ], F32R, part)
                e.rs = sb("e_rs", [P, 2, SEQ], F32, part)
            e.s = sb("e_s", [P, S_SLOTS, SEQ], F32, scope)
            e.mqh, e.mql, e.mkh, e.mkl = (sb(n, [P, 2, SEQ], F32R, scope) for n in (
                "e_mqh", "e_mql", "e_mkh", "e_mkl"))
            e.pt = sb("e_pt", [P, PT_SLOTS, 4 * P], F32, scope)
        e.nqh, e.nql, e.nkh, e.nkl = t.xh[:, 0:4, :], t.xl[:, 0:4, :], t.xh[:, 4:6, :], t.xl[:, 4:6, :]
        e.out_h = [t.xh[:, 6, :], t.xh[:, 7, :], e.out2[:, 0, :], e.out2[:, 1, :]] + [t.xh[:, f, :] for f in range(4)]
        e.out_l = [t.xl[:, 6, :], t.xl[:, 7, :], e.out2[:, 2, :], e.out2[:, 3, :]] + [t.xl[:, f, :] for f in range(4)]
        e.acc = e.ra[:, :].rearrange("p (a n) -> p a n", a=ACC_SLOTS)
        o = t.odd = Store()
        o.ident, o.slots = t.ident, 3
        with ExitStack() as scope:
            o.q = sb("o_q", [P, 2, DG, SEQ], F32, scope)
            o.k = sb("o_k", [P, 2, DG, SEQ], F32, scope)
            o.v = sb("o_v", [P, TT, DG, DHEADS * P], F32, scope)
            o.dist = [sb(f"o_dist{n}", [P, TT, 2 * P if n == 0 else SEQ], F32, scope) for n in range(DG)]
            o.s = sb("o_s", [P, o.slots, 10 * P], F32, scope)
            o.pt = sb("o_pt", [P, PT_SLOTS, 4 * P], F32, scope)
            o.oh = sb("o_oh", [P, DHEADS, SEQ], F32R, scope)
            o.ol = sb("o_ol", [P, DHEADS, SEQ], F32R, scope)
            o.nmax, o.den, o.inv = (sb(n, [P, o.slots], F32, scope) for n in ("o_nmax", "o_den", "o_inv"))
        o.ktile = [0, 1, 2, 3]
        flat = o.s[:, :, :].rearrange("p a n -> p (a n)")
        t.direct_slots = [flat[:, m * SEQ:m * SEQ + SEQ] for m in range(KD - 1)] + [t.sq[:, :]]

        t.bank = [ctx.enter_context(nc.psum_tensor(f"bank{i}", [P, 512], F32)) for i in range(8)]
        e.score, e.turn, e.outbank, e.obank = t.bank[4:7], (t.bank[7], t.bank[3]), t.bank[2], t.bank[0:2]
        o.score, o.obank, o.turn = t.bank[0:3], t.bank[5:6], t.bank[6:8]

        t.consts_in, t.out_stored = sem("consts_in"), sem("out_stored")
        t.setup, t.sin_done, t.in_hi, t.in_ready = (sem(n) for n in ("setup", "sin_done", "in_hi", "in_ready"))
        t.units_hi, t.units_split, t.units_used = (sem(n) for n in ("units_hi", "units_split", "units_used"))
        t.dist_step = sem("dist_step")
        t.x_in, t.raw_landed, t.masks_in = sems("x_in", KD), sems("raw_landed", RAW), sems("masks_in", 2)
        t.h_mul, t.h_hi, t.h_ready, t.silu_done = (sems(n, 4) for n in ("h_mul", "h_hi", "h_ready", "silu_done"))
        t.z_done, t.acc = (sems(n, 6) for n in ("z_done", "acc"))
        t.x_hi, t.x_ready = (sems(n, 6) for n in ("x_hi", "x_ready"))
        t.col_sums, t.col, t.std_done, t.last_sq, t.diag, t.maps = (sem(n) for n in (
            "col_sums", "col", "std_done", "last_sq", "diag", "maps"))
        t.direct_sq, t.direct_pair, t.direct_z, t.direct_summed = (sem("direct_" + n) for n in (
            "sq", "pair", "z", "summed"))
        t.norm_a, t.norm_b, t.norm_c = (sem(n) for n in ("norm_a", "norm_b", "norm_c"))
        for a, name in ((e, "e"), (o, "o")):
            a.scores_ready, a.exp_done, a.inv_ready = (sem(f"{name}_{n}") for n in ("scores_ready", "exp_done", "inv_ready"))
            a.turned, a.pt_ready, a.values_done = (sem(f"{name}_{n}") for n in ("turned", "pt_ready", "values_done"))
            a.o_hi, a.o_ready, a.evac = (sem(f"{name}_{n}") for n in ("o_hi", "o_ready", "evac"))
        e.min_ready, e.summed, e.sum_turned = (sem("e_" + n) for n in ("min_ready", "summed", "sum_turned"))
        o.scores_read, o.max_ready, o.probs_ready = (sem("o_" + n) for n in ("scores_read", "max_ready", "probs_ready"))
        e.tile_done, e.squared, e.rms_sum, e.rms_std, e.rms_inv = (sem("e_" + n) for n in (
            "tile_done", "squared", "rms_sum", "rms_std", "rms_inv"))
        e.c_full, e.c_hi, e.c_lo, e.b_full, e.b_hi, e.b_lo = (sem("e_" + n) for n in (
            "c_full", "c_hi", "c_lo", "b_full", "b_hi", "b_lo"))
        e.gelu, e.gate_exp, e.gate_step, e.rope, e.q_rot, e.half_out = (sem("e_" + n) for n in (
            "gelu", "gate_exp", "gate_step", "rope", "q_rot", "half_out"))
        e.n_hi, e.n_lo, e.kc_hi, e.mla_step, e.mla_split = (sem("e_" + n) for n in (
            "n_hi", "n_lo", "kc_hi", "mla_step", "mla_split"))
        o.tile_done = sem("o_tile_done")
        e.items, o.items = even_items(t), odd_items(t)

        block = ctx.enter_context(nc.Block())

        @block.sync
        def _(sp):
            ffn_sync(sp, t, 0)
            even_sync(sp, t)
            ffn_sync(sp, t, 1)
            ffn_sync(sp, t, 2)
            odd_sync(sp, t)
            ffn_sync(sp, t, 3)
            for k in range(KD):
                sp.wait_ge(t.norm_c, KD * 5 + k + 1)
                sp.dma_start(out[k], t.xt[:, k, :]).then_inc(t.out_stored, 16)
            sp.wait_ge(t.out_stored, 16 * KD)

        @block.tensor
        def _(pe):
            pe.sem_inc(t.units_used, SPLIT)
            ffn_tensor(pe, t, 0, t.in_ready)
            norm_tensor(pe, t, 0)
            even_tensor(pe, t, t.x_ready[0])
            norm_tensor(pe, t, 1)
            ffn_tensor(pe, t, 1, t.x_ready[1])
            norm_tensor(pe, t, 2)
            ffn_tensor(pe, t, 2, t.x_ready[2])
            norm_tensor(pe, t, 3)
            odd_tensor(pe, t, t.x_ready[3])
            norm_tensor(pe, t, 4)
            ffn_tensor(pe, t, 3, t.x_ready[4])
            norm_tensor(pe, t, 5)

        @block.scalar
        def _(act):
            for u in range(LEAD):
                split_hi(act, t, u)
            input_hi(act, t)
            start_scalar(act, t)
            ffn_scalar(act, t, 0)
            norm_scalar(act, t, 0)
            even_scalar(act, t)
            norm_scalar(act, t, 1)
            ffn_scalar(act, t, 1)
            norm_scalar(act, t, 2)
            ffn_scalar(act, t, 2)
            norm_scalar(act, t, 3)
            odd_scalar(act, t)
            norm_scalar(act, t, 4)
            ffn_scalar(act, t, 3)
            norm_scalar(act, t, 5)

        @block.vector
        def _(dve):
            dve.sem_inc(t.units_split, RAW)
            for u in range(LEAD):
                split_lo(dve, t, u)
            start_vector(dve, t)
            ffn_vector(dve, t, 0)
            norm_vector(dve, t, 0)
            even_vector(dve, t)
            norm_vector(dve, t, 1)
            ffn_vector(dve, t, 1)
            norm_vector(dve, t, 2)
            ffn_vector(dve, t, 2)
            norm_vector(dve, t, 3)
            odd_vector(dve, t)
            norm_vector(dve, t, 4)
            ffn_vector(dve, t, 3)
            norm_vector(dve, t, 5)

        @block.gpsimd
        def _(g):
            for k in range(KD):
                g.dma_start(t.xt[:, k, :], t.x_t[k]).then_inc(t.x_in[k], 16)
            input_lo(g, t)
            g.wait_ge(t.setup, 11)
            sums_gpsimd(g, t, 0)
            norm_gpsimd(g, t, 0)
            even_gpsimd(g, t)
            sums_gpsimd(g, t, 1)
            norm_gpsimd(g, t, 1)
            sums_gpsimd(g, t, 2)
            norm_gpsimd(g, t, 2)
            sums_gpsimd(g, t, 3)
            norm_gpsimd(g, t, 3)
            odd_gpsimd(g, t)
            direct_pairs(g, t)
            norm_gpsimd(g, t, 4)
            sums_gpsimd(g, t, 5)


def constants():
    q, k = np.arange(SEQ)[:, None], np.arange(SEQ)[None, :]
    by_tile = lambda m: np.ascontiguousarray(
        np.where(m, 0.0, BIG).astype(np.float32).reshape(TT, P, -1).transpose(1, 0, 2))
    tri = np.zeros((P, SEQ), np.float32)
    tri[:, SEQ - P:] = np.where(np.arange(P)[:, None] >= np.arange(P)[None, :], 0.0, BIG)
    win = np.zeros((P, TT, 2 * P), np.float32)
    full = by_tile((q >= k) & (q - k <= DIL[0][0]))
    for i in range(TT):
        first, w = odd_keys(0, i)
        win[:, i, :w] = full[:, i, first:first + w]
    half = ROPE // 2
    freq = (10000.0 ** (-np.arange(half, dtype=np.float32) / half)).astype(np.float32)
    cst = np.zeros((P, N_CST), np.float32)
    for m in range(H // 2):
        cst[:64, C_QN + m], cst[64:, C_QN + m] = (-NSA_SCALE / NSA_SLOPES[h] for h in (m, 4 + m))
    cst[:, C_INVD] = 1 / D_MODEL
    cst[:, C_RMS_EPS] = RMS_EPS
    cst[:, C_FREQ] = np.tile(freq, P // half)
    turn = np.zeros(P)
    turn[64:96], turn[96:112] = 0.25, 0.5
    cst[:, C_TURN] = turn
    cst[:, C_PHASE] = 2 * np.pi * turn
    return {
        "c_cst": cst, "c_ident": np.eye(P, dtype=np.float32),
        "c_ones": np.ones((P, P), np.float32),
        "c_ones_kv": np.full((P, P), 1 / KV_RANK, np.float32),
        "c_ones_q": np.full((P, P), 1 / Q_RANK, np.float32),
        "c_cmp_valid": (np.arange(P) >= 31).astype(np.float32)[:, None],
        "tri_mask": tri, "causal_mask": by_tile(q >= k),
        "cmp_mask": by_tile(16 * np.arange(NC)[None, :] + 31 <= q),
        "dil_mask0": win, "dil_mask1": by_tile((q >= k) & ((q - k) % DIL[1][1] == 0)),
        "dil_mask2": by_tile((q >= k) & ((q - k) % DIL[2][1] == 0)),
    }


def blocks(w):
    k, m = w.shape
    return np.ascontiguousarray(w.reshape(k // P, P, m // P, P).transpose(2, 1, 0, 3)).reshape(m // P, P, -1)


def rows(w):
    k, m = w.shape
    return np.ascontiguousarray(w.reshape(k // P, P, m).transpose(1, 0, 2)).reshape(P, -1)


def layouts(inp):
    a = {}
    a["x_t"] = np.ascontiguousarray(inp["x"][0].T).reshape(KD, P, SEQ)
    pos = inp["positions"][0]
    a["c_pos_k"] = np.ascontiguousarray(np.broadcast_to(pos, (P, SEQ)))
    a["c_pos_q"] = np.ascontiguousarray(pos.reshape(TT, P).T)
    norms = [inp[f"ln{n}_{c}"] for n in (1, 2, 3) for c in "gb"]
    a["c_gains"] = np.ascontiguousarray(np.stack(norms).reshape(6, DEPTH, KD, P).transpose(3, 0, 1, 2))
    for f in range(4):
        n, layer = 1 + f % 2, f // 2
        a[f"w_gate{f}"] = blocks(inp[f"ffn{n}_w_gate"][layer])
        a[f"w_up{f}"] = blocks(inp[f"ffn{n}_w_up"][layer])
        a[f"w_down{f}"] = blocks(inp[f"ffn{n}_w_down"][layer])
    w = inp["mix_in_even"][0]
    cut = np.split(w, np.cumsum([Q_RANK, KV_RANK, ROPE, H * DH] + [2 * DH] * 6), axis=1)
    c_q, c_kv, k_pe, q, k_c, v_c, k_s, v_s, k_w, v_w, gate = cut
    half = ROPE // 2
    swap = lambda m: np.concatenate([m[:, half:], m[:, :half]], axis=1)
    tiles = [c_kv, c_q, np.concatenate([k_pe, swap(k_pe)] * 2, axis=1)]
    tiles += [np.concatenate([m[:, s:s + DH]] * 2, axis=1) for m in (k_c, v_c) for s in (0, DH)]
    tiles += [k_s, k_w]
    tiles += [np.concatenate([q[:, m * DH:m * DH + DH], q[:, (4 + m) * DH:(5 + m) * DH]], axis=1)
              for m in range(4)]
    a["ev_in"] = blocks(np.concatenate(tiles, axis=1))
    a["ev_vg"] = rows(np.concatenate([v_s, v_w, gate], axis=1))
    a["ev_w1"] = np.ascontiguousarray(np.stack([inp[f"nsa_cmp_{kind}_w1"][0] for kind in "kv"])
                                      .reshape(8, 4, P, HID).transpose(0, 2, 1, 3)).reshape(8, P, UNIT)
    w2k, w2v = inp["nsa_cmp_k_w2"][0], inp["nsa_cmp_v_w2"][0]
    a["c_w2k"] = rows(np.concatenate([w2k, w2k], axis=1)).reshape(P, 2, P)
    a["c_w2v"] = rows(w2v).reshape(P, 2, DH)
    a["c_cmp_pos"] = np.ascontiguousarray(inp["nsa_cmp_pos"][0].reshape(CMP_K, P).T)
    a["ev_uk"], a["ev_uv"] = rows(inp["mla_w_uk"][0]), rows(inp["mla_w_uv"][0])
    uq = inp["mla_w_uq"][0].reshape(Q_RANK, H, NOPE + ROPE)
    uq = np.concatenate([uq, uq[..., NOPE + half:], uq[..., NOPE:NOPE + half]], axis=2)
    a["ev_uq"] = np.ascontiguousarray(blocks(uq.reshape(Q_RANK, H * P)).reshape(UQ_UNITS, 2, P, -1)
                                      .transpose(0, 2, 1, 3)).reshape(UQ_UNITS, P, -1)
    a["c_rms_g"] = np.ascontiguousarray(np.concatenate([inp["mla_kv_norm"][0], inp["mla_q_norm"][0]])
                                        .reshape(KV + KQ, P).T)
    a["ev_out"] = blocks(inp["mix_out_even"][0])
    od = inp["mix_in_odd"][0].reshape(D_MODEL, 3, DG, DHEADS, P)
    a["od_qk"] = blocks(od[:, :2].transpose(0, 3, 1, 2, 4).reshape(D_MODEL, -1))
    a["od_v"] = np.ascontiguousarray(od[:, 2].reshape(4, 2, P, DG, DHEADS * P).transpose(3, 0, 2, 1, 4)
                                     ).reshape(V_UNITS, P, 2 * DHEADS * P)
    rest = (DHEADS - 1) * P
    a["od_out"] = np.ascontiguousarray(blocks(inp["mix_out_odd"][0][:rest]).reshape(KD // 2, 2, P, -1)
                                       .transpose(0, 2, 1, 3)).reshape(KD // 2, P, -1)
    a["od_last"] = rows(inp["mix_out_odd"][0][rest:])
    return a


def build(nc, arrays):
    d = {n: nc.dram_tensor(n, a.shape, mybir.dt.from_np(a.dtype), kind="ExternalInput").ap()
         for n, a in arrays.items()}
    for n in ("w_gate", "w_up", "w_down"):
        d[n] = [d[f"{n}{f}"] for f in range(4)]
    d["dil_mask"] = [d[f"dil_mask{n}"] for n in range(DG)]
    out = nc.dram_tensor("out_t", (KD, P, SEQ), F32, kind="ExternalOutput").ap()
    trunk(nc, d, out)


def kernel(**inputs):
    import concourse.bacc as bacc
    from concourse.bass_utils import run_bass_kernel_spmd

    arrays = {**layouts({n: np.asarray(v) for n, v in inputs.items()}), **constants()}
    nc = bacc.Bacc("TRN2", target_bir_lowering=False, num_devices=1)
    build(nc, arrays)
    r = run_bass_kernel_spmd(nc, [arrays], core_ids=[0])
    out = np.asarray(r.results[0]["out_t"]).reshape(D_MODEL, SEQ)
    return np.ascontiguousarray(out.T)[None]
```
